# Optimizing a Trainium2 kernel written in Bass

```python
import math
import jax, jax.numpy as jnp
from jax import lax
import numpy as np

D_MODEL = 1024
BATCH = 1
SEQ = 256
DEPTH = 1

HEAD_DIM = 64
N_HEADS_MOBA = 8
N_HEADS_SB = 8
D_MOBA = N_HEADS_MOBA * HEAD_DIM
D_SB = N_HEADS_SB * HEAD_DIM
D_MIX = D_MOBA + D_SB
MOBA_BLOCK = 256
MOBA_TOPK = 3
MOBA_Q_CHUNK = 128
SB_Q_BLOCK = 128
REL_BUCKETS = 32
REL_MAX_DIST = 128
PEER_HEADS = 8
PEER_N_KEYS = 128
PEER_N_EXPERTS = PEER_N_KEYS * PEER_N_KEYS
PEER_D_KEY = 256
PEER_TOPK = 16
PEER_TOKEN_CHUNK = 128
PLE_DIM = 256
EPS = 1e-6

kernel_name = "hybrid_moba_stickbreak_peer_layer"

def rms_norm(x, g):
    xf = x.astype(jnp.float32)
    y = xf * lax.rsqrt(jnp.mean(xf * xf, axis=-1, keepdims=True) + EPS)
    return (y * g.astype(jnp.float32)).astype(x.dtype)

def rel_bucket(dist):
    n = jnp.maximum(dist, 0)
    max_exact = REL_BUCKETS // 2
    nf = jnp.maximum(n, 1).astype(jnp.float32)
    large = max_exact + (jnp.log(nf / max_exact) / math.log(REL_MAX_DIST / max_exact)
                         * (REL_BUCKETS - max_exact)).astype(jnp.int32)
    large = jnp.minimum(large, REL_BUCKETS - 1)
    return jnp.where(n < max_exact, n, large)

def moba_attention(q, k, v, rel_bias):
    B, S, H, Dh = q.shape
    L, C = MOBA_BLOCK, MOBA_Q_CHUNK
    n_blk = -(-S // L)
    K = min(MOBA_TOPK, n_blk)
    pad = n_blk * L - S
    kp = jnp.pad(k, ((0, 0), (0, pad), (0, 0), (0, 0)))
    vp = jnp.pad(v, ((0, 0), (0, pad), (0, 0), (0, 0)))
    k_bh = kp.reshape(B, n_blk, L, H, Dh).transpose(0, 3, 1, 2, 4)
    v_bh = vp.reshape(B, n_blk, L, H, Dh).transpose(0, 3, 1, 2, 4)
    k_mean = jnp.mean(k_bh.astype(jnp.float32), axis=3)
    n_chunks = S // C
    q_r = q.reshape(B, n_chunks, C, H, Dh)
    scale = Dh ** -0.5
    bias_t = rel_bias.T.astype(jnp.float32)
    h_idx = jnp.arange(H)

    def one_chunk(args):
        bi, c = args
        q_c = q_r[bi, c].astype(jnp.float32)
        k_b, v_b = k_bh[bi], v_bh[bi]
        t = c * C + jnp.arange(C)
        blk = (c * C) // L
        gate = jnp.einsum('chd,hnd->hcn', q_c, k_mean[bi])
        gate = jnp.where(jnp.arange(n_blk) < blk, gate, -jnp.inf)
        _, sel = lax.top_k(gate, K)
        valid = jnp.arange(K) < blk
        k_sel = k_b[h_idx[:, None, None], sel].astype(jnp.float32)
        v_sel = v_b[h_idx[:, None, None], sel].astype(jnp.float32)
        pos_sel = sel[..., None] * L + jnp.arange(L)
        b_sel = bias_t[h_idx[:, None, None, None], rel_bucket(t[None, :, None, None] - pos_sel)]
        lg_sel = jnp.einsum('chd,hckld->hckl', q_c, k_sel) * scale + b_sel
        lg_sel = jnp.where(valid[None, None, :, None], lg_sel, -jnp.inf).reshape(H, C, K * L)
        k_own = k_b[:, blk].astype(jnp.float32)
        v_own = v_b[:, blk].astype(jnp.float32)
        dist_own = t[:, None] - (blk * L + jnp.arange(L))[None, :]
        lg_own = jnp.einsum('chd,hld->hcl', q_c, k_own) * scale + bias_t[:, rel_bucket(dist_own)]
        lg_own = jnp.where(dist_own[None] >= 0, lg_own, -jnp.inf)
        probs = jax.nn.softmax(jnp.concatenate([lg_sel, lg_own], axis=-1), axis=-1)
        p_sel, p_own = probs[..., :K * L], probs[..., K * L:]
        out = (jnp.einsum('hcm,hcmd->chd', p_sel, v_sel.reshape(H, C, K * L, Dh))
               + jnp.einsum('hcl,hld->chd', p_own, v_own))
        return out.astype(v.dtype)

    b_ids = jnp.repeat(jnp.arange(B), n_chunks)
    c_ids = jnp.tile(jnp.arange(n_chunks), B)
    out = lax.map(one_chunk, (b_ids, c_ids))
    return out.reshape(B, S, H, Dh)

def stick_breaking_attention(q, k, v):
    B, S, H, Dh = q.shape
    scale = Dh ** -0.5
    outs = []
    for qb in range(S // SB_Q_BLOCK):
        q0 = qb * SB_Q_BLOCK
        kv_len = q0 + SB_Q_BLOCK
        q_b = q[:, q0:kv_len].astype(jnp.float32)
        k_b = k[:, :kv_len].astype(jnp.float32)
        v_b = v[:, :kv_len].astype(jnp.float32)
        z = jnp.einsum('bthd,bshd->bhts', q_b, k_b) * scale
        t = q0 + jnp.arange(SB_Q_BLOCK)
        strict = jnp.arange(kv_len)[None, :] < t[:, None]
        log_1m = jnp.where(strict, jax.nn.log_sigmoid(-z), 0.0)
        acc = lax.cumsum(log_1m, axis=3, reverse=True) - log_1m
        w = jnp.where(strict, jnp.exp(jax.nn.log_sigmoid(z) + acc), 0.0)
        outs.append(jnp.einsum('bhts,bshd->bthd', w, v_b).astype(q.dtype))
    return jnp.concatenate(outs, axis=1)

def peer_ffn(x, w_query, sub_keys, u_table, v_table):
    B, S, D = x.shape
    T = B * S
    xf = x.reshape(T, D)
    qk = jnp.einsum('td,dhk->thk', xf, w_query).astype(jnp.float32)
    half = PEER_D_KEY // 2
    s1 = jnp.einsum('thk,nk->thn', qk[..., :half], sub_keys[0].astype(jnp.float32))
    s2 = jnp.einsum('thk,nk->thn', qk[..., half:], sub_keys[1].astype(jnp.float32))
    v1, i1 = lax.top_k(s1, PEER_TOPK)
    v2, i2 = lax.top_k(s2, PEER_TOPK)
    cand = (v1[..., :, None] + v2[..., None, :]).reshape(T, PEER_HEADS, PEER_TOPK * PEER_TOPK)
    cand_idx = (i1[..., :, None] * PEER_N_KEYS + i2[..., None, :]).reshape(T, PEER_HEADS, -1)
    top_s, top_pos = lax.top_k(cand, PEER_TOPK)
    e_idx = jnp.take_along_axis(cand_idx, top_pos, axis=-1)
    gates = jax.nn.softmax(top_s, axis=-1)
    E = PEER_HEADS * PEER_TOPK
    n_ch = T // PEER_TOKEN_CHUNK
    xs = (xf.reshape(n_ch, PEER_TOKEN_CHUNK, D),
          e_idx.reshape(n_ch, PEER_TOKEN_CHUNK, E),
          gates.reshape(n_ch, PEER_TOKEN_CHUNK, E).astype(x.dtype))

    def one_chunk(args):
        x_c, idx_c, g_c = args
        u = u_table[idx_c]
        hid = jax.nn.gelu(jnp.einsum('cd,ced->ce', x_c, u), approximate=False)
        return jnp.einsum('ce,ced->cd', g_c * hid, v_table[idx_c])

    return lax.map(one_chunk, xs).reshape(B, S, D)

def setup_inputs(seed: int = 0) -> dict:
    key = jax.random.key(seed)
    ks = jax.random.split(key, 20)
    f = jnp.float32
    nrm = lambda k, shape, s: jax.random.normal(k, shape, f) * s
    gain = lambda k, shape: 1.0 + 0.05 * jax.random.normal(k, shape, f)
    return {
        "x": nrm(ks[0], (BATCH, SEQ, D_MODEL), 1.0),
        "p": nrm(ks[1], (DEPTH, BATCH, SEQ, PLE_DIM), 1.0),
        "rel_bias": nrm(ks[2], (REL_BUCKETS, N_HEADS_MOBA), 0.5),
        "attn_norm": gain(ks[3], (DEPTH, D_MODEL)),
        "w_in": nrm(ks[4], (DEPTH, D_MODEL, 3 * D_MIX), D_MODEL ** -0.5),
        "q_norm": gain(ks[5], (DEPTH, HEAD_DIM)),
        "k_norm": gain(ks[6], (DEPTH, HEAD_DIM)),
        "out_norm_moba": gain(ks[7], (DEPTH, D_MOBA)),
        "out_norm_sb": gain(ks[8], (DEPTH, D_SB)),
        "w_out": nrm(ks[9], (DEPTH, D_MIX, D_MODEL), D_MIX ** -0.5),
        "ffn_norm": gain(ks[10], (DEPTH, D_MODEL)),
        "peer_query": nrm(ks[11], (DEPTH, D_MODEL, PEER_HEADS, PEER_D_KEY), D_MODEL ** -0.5),
        "peer_sub_keys": nrm(ks[12], (DEPTH, 2, PEER_N_KEYS, PEER_D_KEY // 2), (PEER_D_KEY // 2) ** -0.5),
        "peer_u": nrm(ks[13], (DEPTH, PEER_N_EXPERTS, D_MODEL), D_MODEL ** -0.5),
        "peer_v": nrm(ks[14], (DEPTH, PEER_N_EXPERTS, D_MODEL), PEER_HEADS ** -0.5),
        "ple_norm": gain(ks[15], (DEPTH, D_MODEL)),
        "w_ple_gate": nrm(ks[16], (DEPTH, D_MODEL, D_MODEL), D_MODEL ** -0.5),
        "w_ple": nrm(ks[17], (DEPTH, PLE_DIM, D_MODEL), PLE_DIM ** -0.5),
    }

def reference(x, p, rel_bias, attn_norm, w_in, q_norm, k_norm, out_norm_moba, out_norm_sb,
              w_out, ffn_norm, peer_query, peer_sub_keys, peer_u, peer_v, ple_norm,
              w_ple_gate, w_ple):
    B, S, _ = x.shape
    h = x
    for i in range(DEPTH):
        xn = rms_norm(h, attn_norm[i])
        proj = xn @ w_in[i]
        qm, km, vm, qs, ks_, vs = jnp.split(proj, 6, axis=-1)
        heads = lambda t, nh: t.reshape(B, S, nh, HEAD_DIM)
        qm = rms_norm(heads(qm, N_HEADS_MOBA), q_norm[i])
        km = rms_norm(heads(km, N_HEADS_MOBA), k_norm[i])
        o_m = moba_attention(qm, km, heads(vm, N_HEADS_MOBA), rel_bias)
        o_s = stick_breaking_attention(heads(qs, N_HEADS_SB), heads(ks_, N_HEADS_SB),
                                       heads(vs, N_HEADS_SB))
        o_m = rms_norm(o_m.reshape(B, S, D_MOBA), out_norm_moba[i])
        o_s = rms_norm(o_s.reshape(B, S, D_SB), out_norm_sb[i])
        h = h + jnp.concatenate([o_m, o_s], axis=-1) @ w_out[i]
        h = h + peer_ffn(rms_norm(h, ffn_norm[i]), peer_query[i], peer_sub_keys[i],
                         peer_u[i], peer_v[i])
        gate = jax.nn.sigmoid(rms_norm(h, ple_norm[i]) @ w_ple_gate[i])
        h = h + gate * (p[i] @ w_ple[i])
    return h


_drawn_inputs = setup_inputs


def setup_inputs(seed=0):
    import zlib

    import numpy as np

    out = dict(_drawn_inputs(seed))
    spreads = {}
    factors = {'ple_norm': 8.0}
    for name, (base, spread) in spreads.items():
        noise = np.random.default_rng([zlib.crc32(name.encode()), seed]).standard_normal(out[name].shape)
        drawn = base * np.exp(spread * noise) if base else spread * noise
        out[name] = __import__('jax').numpy.asarray(drawn.astype(out[name].dtype))
    for name, factor in factors.items():
        out[name] = (out[name] * factor).astype(out[name].dtype)
    return out
```

```python
from contextlib import ExitStack

import numpy as np
import concourse.bass as bass
from concourse import mybir

P = 128
SEQ = 256
D = 1024
DC = D // P
TT = SEQ // P
HD = 64
NH = 8
REL = 32
N_KEYS = 128
TOPK = 16
PH = 8
PG = 2 * PH
PLE = 256
EPS = 1e-6
SCALE = HD ** -0.5
GW = 512
GATHER_SPLIT = 80
TAB = 384

Q_M, K_M, Q_S, K_S, V_M, V_S = range(6)
OUT0, QUERY0, N_GROUPS = 6, 8, 12


def layer_program(nc, x, p_t, rel_bias, bucket_onehot, consts, gains, qk_gain, w_in, w_out, w_query,
                  subkeys_t, u_chunks, v_chunks, w_gate, w_ple, out):
    f32, f32r, u32 = mybir.dt.float32, mybir.dt.float32r, mybir.dt.uint32
    ALU, ACT, AX = mybir.AluOpType, mybir.ActivationFunctionType, mybir.AxisListType

    ctx = ExitStack()
    with ctx:
        base = (nc.sbuf_base + 63) // 64 * 64
        sizes = dict(h=2 * D, xt_hi=DC * SEQ, xt_lo=DC * SEQ, cst=5 * P, gains=4 * DC, qkg=32, stats=192)
        at, where = base, {}
        for name, n in sizes.items():
            where[name] = at
            at += 4 * n
        ZONE = at
        BIG = ZONE + 4 * 13312
        assert BIG + 4 * P * SEQ <= nc.sbuf_usable_end

        def tile(name, shape, offset, dt=f32):
            return nc.alloc_sbuf_tensor_at(name, shape, dt, offset=offset)

        h = tile("h", [P, TT, D], where["h"])
        xt_hi = tile("xt_hi", [P, DC, SEQ], where["xt_hi"], f32r)
        xt_lo = tile("xt_lo", [P, DC, SEQ], where["xt_lo"], f32r)
        cst = tile("cst", [P, 5, P], where["cst"])
        gain = tile("gain", [P, 4, DC], where["gains"])
        qkg = tile("qkg", [P, 2], where["qkg"])
        stats = tile("stats", [P, 192], where["stats"])
        ident, neg_tri, neg_ones, iota = cst[:, 0, :], cst[:, 1, :], cst[:, 2, :], cst[:, 3, :]
        flip = cst[:, 4, :]

        w_raw = tile("w_raw", [P, 2, DC, GW], BIG)
        w_hi = tile("w_hi", [P, 2, DC, GW], BIG + 4 * 8192, f32r)
        w_lo = tile("w_lo", [P, 2, DC, GW], BIG + 4 * 16384, f32r)
        UP = BIG + 4 * 24576
        bias = tile("bias", [P, NH, SEQ], UP)
        skew = tile("skew", [P, NH, SEQ], UP + 4 * 6144)
        v_all = tile("v_all", [P, TT, 2 * NH * HD], UP + 4 * 2048)
        qk_nat = tile("qk_nat", [P, TT, 2 * NH, HD], UP + 4 * 4096)
        o_nat = tile("o_nat", [P, TT, D], UP + 4 * 4096)
        qkt_s = tile("qkt_s", [P, 8, SEQ], UP + 4 * 6144)
        query_hi = tile("query_hi", [P, PG, SEQ], UP, f32r)
        query_lo = tile("query_lo", [P, PG, SEQ], UP + 4 * 4096, f32r)
        slots = tile("slots", [P, N_KEYS, SEQ], BIG)
        o = UP
        top_v = tile("top_v", [P, TT, PG, TOPK], o); o += 4 * 512
        top_i = tile("top_i", [P, TT, PG, TOPK], o, u32); o += 4 * 512
        top_f = tile("top_f", [P, TT, PG, TOPK], o); o += 4 * 512
        rest = tile("rest", [P, 2, 256], o); o += 4 * 512
        cand = tile("cand", [P, PH, TOPK, TOPK], o); o += 4 * 2048
        best_v = tile("best_v", [P, TT, PH, TOPK], o); o += 4 * 256
        best_p = tile("best_p", [P, TT, PH * TOPK], o, u32); o += 4 * 256
        pos_u = tile("pos_u", [P, 2, PH * TOPK], o, u32); o += 4 * 256
        pos_f = tile("pos_f", [P, 2, PH * TOPK], o); o += 4 * 256
        hit = tile("hit", [P, PH, TOPK, TOPK], o); o += 4 * 2048
        pick = tile("pick", [P, TT, 2, P], o); o += 4 * 512
        gate = tile("gate", [P, TT, PH, TOPK], o); o += 4 * 256
        assert o <= BIG + 4 * P * SEQ
        wg_raw = tile("wg_raw", [P, DC, D], BIG)
        wg_hi = tile("wg_hi", [P, DC, D], BIG + 4 * 8192, f32r)
        wg_lo = tile("wg_lo", [P, DC, D], BIG + 4 * 16384, f32r)
        wp_hi = tile("wp_hi", [P, 2, D], BIG + 4 * 24576, f32r)
        wp_lo = tile("wp_lo", [P, 2, D], BIG + 4 * 26624, f32r)
        pt_hi = tile("pt_hi", [P, 2, SEQ], BIG + 4 * 28672, f32r)
        pt_lo = tile("pt_lo", [P, 2, SEQ], BIG + 4 * 29184, f32r)
        sig = tile("sig", [P, 4, 512], BIG + 4 * 29696)

        s0 = tile("s0", [P, NH, P], ZONE)
        s1 = tile("s1", [P, NH, SEQ], ZONE + 4 * 1024)
        square = tile("square", [P, 2 * NH, HD], ZONE)
        probs_t = tile("probs_t", [P, 4, 512], ZONE + 4 * 3072)
        sb_sp = tile("sb_sp", [P, 2, 1536], ZONE + 4 * 5120)
        sb_w = tile("sb_w", [P, 2, 1536], ZONE + 4 * 8192)
        qkt_m = tile("qkt_m", [P, 8, SEQ], ZONE + 4 * 11264)
        xs = tile("xs", [P, TT, D], ZONE + 4 * 5120)
        tab_in = tile("tab_in", [REL + 1, TAB + NH], ZONE + 4 * 8192)
        tab_out = tile("tab_out", [NH, TAB], ZONE + 4 * 9216)
        t_raw = tile("t_raw", [P, 2, D], ZONE)
        t_hi = tile("t_hi", [P, 2, D], ZONE + 4 * 2048, f32r)
        scores = tile("scores", [P, TT, PG, N_KEYS], ZONE + 4 * 4096)
        t_lo = tile("t_lo", [P, 2, D], ZONE + 4 * 8192, f32r)
        o = ZONE + 4 * 10240
        g_hi = tile("g_hi", [P, 2, SEQ], o, f32r); o += 4 * 512
        g_lo = tile("g_lo", [P, 2, SEQ], o, f32r); o += 4 * 512
        pick_t = tile("pick_t", [P, 3, SEQ], o); o += 4 * 768
        sk_raw = tile("sk_raw", [P, 2, N_KEYS], o); o += 4 * 256
        sk_hi = tile("sk_hi", [P, 2, N_KEYS], o, f32r); o += 4 * 256
        sk_lo = tile("sk_lo", [P, 2, N_KEYS], o, f32r); o += 4 * 256
        pt_raw = tile("pt_raw", [P, 2, SEQ], o); o += 4 * 512
        assert o <= BIG
        hot_i = tile("hot_i", [P, 2, 4, P], ZONE + 4 * 4096)
        hot_j = tile("hot_j", [P, 2, 4, P], ZONE + 4 * 5120)
        xs_end = tile("xs_end", [P, TT, D], ZONE + 4 * 4096)
        wp_raw = tile("wp_raw", [P, 2, D], ZONE + 4 * 6144)

        bank = [ctx.enter_context(nc.psum_tensor(f"bank{b}", [P, 512], f32)) for b in range(8)]
        table = nc.dram_tensor("bias_table", (NH, TAB), f32, kind="Internal")

        def half(b, j):
            return bank[b][:, 256 * j:256 * (j + 1)]

        def sem(name):
            return ctx.enter_context(nc.semaphore(name))

        x_loaded, small_loaded, tab_loaded = sem("x_loaded"), sem("small_loaded"), sem("tab_loaded")
        tab_made, tab_copied = sem("tab_made"), sem("tab_copied")
        tab_stored, bias_loaded = sem("tab_stored"), sem("bias_loaded")
        flip_done, bias_ready = sem("flip_done"), sem("bias_ready")
        w_loaded = [sem("w_loaded0"), sem("w_loaded1")]
        w_hi_ready, w_lo_ready, w_used = sem("w_hi_ready"), sem("w_lo_ready"), sem("w_used")
        squares_done, mean_ready, root_ready = sem("squares_done"), sem("mean_ready"), sem("root_ready")
        xs_ready, xt_done, xt_hi_ready, xt_lo_ready = (sem("xs_ready"), sem("xt_done"), sem("xt_hi_ready"),
                                                       sem("xt_lo_ready"))
        group_out = sem("group_out")
        qk_mean, qk_root, qk_normed = sem("qk_mean"), sem("qk_root"), sem("qk_normed")
        qkt_done, qkt_out = sem("qkt_done"), sem("qkt_out")
        z_done, z_softplus, sp_added, sp_masked = sem("z_done"), sem("z_softplus"), sem("sp_added"), sem("sp_masked")
        z_read, cum_done, w_exp, w_masked = sem("z_read"), sem("cum_done"), sem("w_exp"), sem("w_masked")
        qk_done, qk_biased, s_shifted, s_exp = sem("qk_done"), sem("qk_biased"), sem("s_shifted"), sem("s_exp")
        pt_done, pt_out, pv_done, pv_out = sem("pt_done"), sem("pt_out"), sem("pv_done"), sem("pv_out")
        spv_done, spv_out = sem("spv_done"), sem("spv_out")
        h1_ready, query_hi_ready, query_lo_ready = sem("h1_ready"), sem("query_hi_ready"), sem("query_lo_ready")
        sk_loaded, sk_hi_ready, sk_lo_ready = sem("sk_loaded"), sem("sk_hi_ready"), sem("sk_lo_ready")
        s_done, s_out = sem("s_done"), sem("s_out")
        t_loaded = [sem("t_loaded0"), sem("t_loaded1")]
        t_hi_ready, t_lo_ready = sem("t_hi_ready"), sem("t_lo_ready")
        hid_done, gelu_done = sem("hid_done"), sem("gelu_done")
        hit_ready, hit_used = sem("hit_ready"), sem("hit_used")
        hit_eq = sem("hit_eq")
        gate_shifted, gate_exp, picks_ready = sem("gate_shifted"), sem("gate_exp"), sem("picks_ready")
        pick_t_done, pick_t_out = sem("pick_t_done"), sem("pick_t_out")
        hot_i_diff, hot_i_square = sem("hot_i_diff"), sem("hot_i_square")
        hot_i_ready, hot_j_ready, gates_done, gated = (sem("hot_i_ready"), sem("hot_j_ready"), sem("gates_done"),
                                                       sem("gated"))
        g_hi_ready, g_lo_ready, v_used = sem("g_hi_ready"), sem("g_lo_ready"), sem("v_used")
        wg_loaded, wp_loaded, wg_hi_ready, wg_lo_ready = (sem("wg_loaded"), sem("wp_loaded"), sem("wg_hi_ready"),
                                                          sem("wg_lo_ready"))
        ple_hi, ple_lo, ple_done = sem("ple_hi"), sem("ple_lo"), sem("ple_done")
        h2_ready, gate_done, sig_ready, sig_used, y_ready, stored = (
            sem("h2_ready"), sem("gate_done"), sem("sig_ready"), sem("sig_used"), sem("y_ready"), sem("stored"))
        act_step, dve_step, pool_step = sem("act_step"), sem("dve_step"), sem("pool_step")

        block = ctx.enter_context(nc.Block())

        def w_source(n):
            if n < OUT0:
                return w_in[n]
            return w_out[n - OUT0] if n < QUERY0 else w_query[n - QUERY0]

        SS, RSTD = stats[:, 0:4], stats[:, 4:8]
        QSS, QRSTD = stats[:, 8:40], stats[:, 40:72]
        MX0, MX1, SUM = stats[:, 72:80], stats[:, 80:88], stats[:, 88:104]
        GSUM = stats[:, 104:120]
        MS = stats[:, 120:124]

        @block.sync
        def _(sp):
            for tt in range(TT):
                sp.dma_start(h[:, tt, :], x[tt * P:(tt + 1) * P, :]).then_inc(x_loaded, 16)
            sp.dma_start(cst[:, :, :], consts).then_inc(small_loaded, 16)
            sp.dma_start(gain[:, :, :], gains).then_inc(small_loaded, 16)
            sp.dma_start(qkg[:, :], qk_gain).then_inc(small_loaded, 16)

            def load_group(n):
                if n >= 2:
                    sp.wait_ge(w_lo_ready, n - 1)
                sp.dma_start(w_raw[:, n % 2, :, :], w_source(n)).then_inc(w_loaded[n % 2], 16)

            load_group(0)
            sp.dma_start(tab_in[:, 0:TAB], bucket_onehot).then_inc(tab_loaded, 16)
            sp.dma_start(tab_in[0:REL, TAB:TAB + NH], rel_bias).then_inc(tab_loaded, 16)
            load_group(1)
            sp.wait_ge(tab_copied, 1)
            sp.dma_start(table.ap(), tab_out[:, :]).then_inc(tab_stored, 16)
            sp.wait_ge(tab_stored, 16)
            sp.dma_start(skew[:, :, :], bass.AP(table, 0, [[1, P], [TAB, NH], [1, SEQ]])).then_inc(bias_loaded, 16)
            for n in range(2, N_GROUPS):
                load_group(n)
                if n == 9:
                    sp.wait_ge(spv_out, 2)
                    sp.wait_ge(pv_out, 2)
                    sp.dma_start(sk_raw[:, :, :], subkeys_t).then_inc(sk_loaded, 16)
                    for j in range(2):
                        sp.dma_start(t_raw[:, j, :], u_chunks[j]).then_inc(t_loaded[j], 16)
            with sp.Fori(1, N_KEYS // 2) as i:
                for j in range(2):
                    sp.wait_ge(t_lo_ready, 2 * i + j - 1)
                    sp.dma_start(t_raw[:, j, :], u_chunks[bass.ds(2 * i + j, 1)].rearrange("o p f -> (o p) f")
                                 ).then_inc(t_loaded[j], 16)

            def v_pairs(first, last):
                with sp.Fori(first, last) as i:
                    for j in range(2):
                        sp.wait_ge(t_lo_ready, N_KEYS + 2 * i + j - 1)
                        sp.dma_start(t_raw[:, j, :], v_chunks[bass.ds(2 * i + j, 1)].rearrange("o p f -> (o p) f")
                                     ).then_inc(t_loaded[j], 16)

            v_pairs(0, 34)
            sp.wait_ge(g_lo_ready, 32)
            sp.dma_start(wg_raw[:, :, :], w_gate).then_inc(wg_loaded, 16)
            sp.dma_start(wp_raw[:, :, :], w_ple).then_inc(wp_loaded, 16)
            sp.dma_start(pt_raw[:, :, :], p_t).then_inc(wp_loaded, 16)
            v_pairs(34, N_KEYS // 2)
            for tt in range(TT):
                sp.wait_ge(y_ready, 2 * (tt + 1))
                sp.dma_start(out[tt * P:(tt + 1) * P, :], h[:, tt, :]).then_inc(stored, 16)
            sp.wait_ge(stored, 16 * TT)

        @block.scalar
        def _(act):
            steps = [0]

            def link(ins):
                steps[0] += 1
                ins.then_inc(act_step, 1)
                act.wait_ge(act_step, steps[0])

            def split_group(n):
                act.wait_ge(w_loaded[n % 2], 16 * (n // 2 + 1))
                if n >= 2:
                    act.wait_ge(w_used, n - 1)
                nc.scalar.activation(w_hi[:, n % 2, :, :], w_raw[:, n % 2, :, :], ACT.Copy).then_inc(w_hi_ready, 1)

            def norm(k, src, halves, xs=xs):
                n = D // halves
                for tt in range(TT):
                    for q in range(halves):
                        c = tt * halves + q
                        nc.scalar.activation(xs[:, tt, q * n:(q + 1) * n], src[:, tt, q * n:(q + 1) * n], ACT.Square,
                                             accum_out=SS[:, c:c + 1]).then_inc(squares_done, 1)
                act.wait_ge(mean_ready, k + 1)
                nc.scalar.activation(RSTD[:, 0:TT * halves], MS[:, 0:TT * halves], ACT.Sqrt).then_inc(root_ready, 1)

            def transposed_hi(k):
                for b in range(4):
                    act.wait_ge(xt_done, 4 * k + b + 1)
                    for c in (2 * b, 2 * b + 1):
                        ins = nc.scalar.activation(xt_hi[:, c, :], half(b, c % 2), ACT.Copy, scale=gain[:, k, c:c + 1])
                    ins.then_inc(xt_hi_ready, 1)

            def out_of_psum(n):
                act.wait_ge(w_used, n + 1)
                b = 4 if n in (Q_M, Q_S) else 6
                for q in range(2):
                    if n in (Q_M, K_M):
                        dst = qk_nat[:, q, NH * n:NH * (n + 1), :].rearrange("p a b -> p (a b)")
                    elif n in (Q_S, K_S):
                        g = 4 * (n - Q_S) + 2 * q
                        dst = qkt_s[:, g:g + 2, :].rearrange("p a b -> p (a b)")
                    else:
                        dst = v_all[:, q, 512 * (n - V_M):512 * (n - V_M + 1)]
                    nc.scalar.copy(dst, bank[b + q][:, :]).then_inc(group_out, 1)

            act.wait_ge(x_loaded, 16 * TT)
            norm(0, h, 1)
            split_group(0)
            act.wait_ge(small_loaded, 48)
            transposed_hi(0)
            act.wait_ge(tab_made, 1)
            nc.scalar.copy(tab_out[:, :], bank[7][0:NH, 0:TAB]).then_inc(tab_copied, 1)
            split_group(1)
            out_of_psum(Q_M)
            split_group(2)
            for b in range(4):
                act.wait_ge(flip_done, b + 1)
                nc.scalar.copy(bias[:, 2 * b:2 * b + 2, :].rearrange("p a b -> p (a b)"), bank[b][:, :]).then_inc(
                    bias_ready, 1)
            out_of_psum(K_M)
            act.wait_ge(qk_mean, 1)
            nc.scalar.activation(QRSTD, QSS, ACT.Sqrt).then_inc(qk_root, 1)
            split_group(3)
            out_of_psum(Q_S)
            for b in range(4):
                act.wait_ge(qkt_done, b + 1)
                nc.scalar.activation(qkt_m[:, 2 * b:2 * b + 2, :].rearrange("p a b -> p (a b)"), bank[b][:, :],
                                     ACT.Copy, scale=qkg[:, b // 2:b // 2 + 1]).then_inc(qkt_out, 1)
            split_group(4)
            out_of_psum(K_S)
            split_group(5)
            for e in range(2):
                act.wait_ge(z_done, e + 1)
                for b in range(3):
                    src = bank[3 * e + b][:, :]
                    nc.scalar.activation(sb_w[:, e, 512 * b:512 * (b + 1)], src, ACT.Relu, scale=SCALE)
                    ins = nc.scalar.activation(sb_sp[:, e, 512 * b:512 * (b + 1)], src, ACT.Abs, scale=SCALE)
                link(ins)
            for e in range(2):
                link(nc.scalar.activation(sb_sp[:, e, :], sb_sp[:, e, :], ACT.Exp, scale=-1.0))
                nc.scalar.activation(sb_sp[:, e, :], sb_sp[:, e, :], ACT.Ln, bias=1.0).then_inc(z_softplus, 1)
            out_of_psum(V_M)
            split_group(6)
            out_of_psum(V_S)
            split_group(7)
            act.wait_ge(s_shifted, 1)
            nc.scalar.activation(s0[:, :, :], s0[:, :, :], ACT.Exp).then_inc(s_exp, 1)
            for e in range(2):
                act.wait_ge(cum_done, e + 1)
                for b in range(3):
                    nc.scalar.activation(sb_w[:, e, 512 * b:512 * (b + 1)], bank[3 * e + b][:, :], ACT.Exp,
                                         scale=SCALE).then_inc(w_exp, 1)
            act.wait_ge(s_shifted, 2)
            nc.scalar.activation(s1[:, :, :], s1[:, :, :], ACT.Exp).then_inc(s_exp, 1)
            for b in range(6):
                act.wait_ge(pt_done, b + 1)
                if b >= 4:
                    act.wait_ge(pv_done, 1)
                nc.scalar.copy(probs_t[:, b % 4, :], bank[b][:, :]).then_inc(pt_out, 1)
            for tt in range(TT):
                act.wait_ge(spv_done, tt + 1)
                nc.scalar.copy(o_nat[:, tt, 512:1024], bank[tt][:, :]).then_inc(spv_out, 1)
            act.wait_ge(spv_out, 2)
            act.wait_ge(pv_out, 2)
            norm(1, o_nat, 2)
            transposed_hi(1)
            act.wait_ge(h1_ready, 4)
            norm(2, h, 1)
            split_group(8)
            transposed_hi(2)
            split_group(9)

            def query_part(n):
                act.wait_ge(w_used, QUERY0 + n + 1)
                for q in range(2):
                    g = 4 * n + 2 * q
                    nc.scalar.copy(query_hi[:, g:g + 2, :].rearrange("p a b -> p (a b)"),
                                   bank[4 + 2 * (n % 2) + q][:, :]).then_inc(query_hi_ready, 1)

            query_part(0)
            split_group(10)
            query_part(1)
            split_group(11)
            act.wait_ge(sk_loaded, 16)
            nc.scalar.copy(sk_hi[:, :, :], sk_raw[:, :, :]).then_inc(sk_hi_ready, 1)
            query_part(2)

            def table_hi(j, count):
                act.wait_ge(t_loaded[j], count)
                nc.scalar.activation(t_hi[:, j, :], t_raw[:, j, :], ACT.Copy).then_inc(t_hi_ready, 1)

            query_part(3)
            act.wait_ge(pt_out, 6)
            table_hi(0, 16)
            table_hi(1, 16)
            for u in range(8):
                act.wait_ge(s_done, u + 1)
                b = [0, 1, 2, 3, 6, 7, 0, 1][u]
                nc.scalar.copy(scores[:, u // 4, 4 * (u % 4):4 * (u % 4) + 4, :].rearrange("p a b -> p (a b)"),
                               bank[b][:, :]).then_inc(s_out, 1)
            act.wait_ge(hid_done, 1)
            nc.scalar.activation(slots[:, 0, :], bank[4][:, 0:SEQ], ACT.Gelu).then_inc(gelu_done, 1)

            def u_pairs(first, last):
                with act.Fori(first, last) as i:
                    for j in range(2):
                        act.wait_ge(hid_done, 2 * i + j - 1)
                        table_hi(j, 16 * i + 16)
                        act.wait_ge(hid_done, 2 * i + j)
                        nc.scalar.activation(slots[:, bass.ds(2 * i + j - 1, 1), :].rearrange("p o t -> p (o t)"),
                                             bank[5 - j][:, 0:SEQ], ACT.Gelu).then_inc(gelu_done, 1)

            u_pairs(1, GATHER_SPLIT // 2)
            act.wait_ge(gate_shifted, TT)
            nc.scalar.activation(gate[:, :, :, :], gate[:, :, :, :], ACT.Exp).then_inc(gate_exp, 1)
            act.wait_ge(picks_ready, 1)
            act.wait_ge(pick_t_out, 3)
            nc.scalar.preload_act_table(ACT.Gelu)
            u_pairs(GATHER_SPLIT // 2, N_KEYS // 2)
            act.wait_ge(hid_done, N_KEYS)
            nc.scalar.activation(slots[:, N_KEYS - 1, :], bank[5][:, 0:SEQ], ACT.Gelu).then_inc(gelu_done, 1)

            table_hi(0, 16 * (N_KEYS // 2 + 1))
            table_hi(1, 16 * (N_KEYS // 2 + 1))

            def one_hots(k, count):
                act.wait_ge(hot_i_diff, count)
                nc.scalar.activation(hot_i[:, k, :, :], hot_i[:, k, :, :], ACT.Square).then_inc(hot_i_square, 1)
                act.wait_ge(hot_i_square, count)
                nc.scalar.activation(hot_i[:, k, :, :], hot_i[:, k, :, :], ACT.Relu, scale=-1.0,
                                     bias=1.0).then_inc(hot_i_ready, 1)

            one_hots(0, 1)
            one_hots(1, 2)
            with act.Fori(1, SEQ // 8) as i:
                for k in range(2):
                    one_hots(k, 2 * i + k + 1)

            def gated_hi(j, n):
                src = slots[:, bass.ds(n, 1), :].rearrange("p o t -> p (o t)")
                nc.scalar.activation(g_hi[:, j, :], src, ACT.Copy).then_inc(g_hi_ready, 1)

            act.wait_ge(gated, SEQ // 4)
            gated_hi(0, 0)
            gated_hi(1, 1)

            def v_pairs(first, last, extra):
                with act.Fori(first, last) as i:
                    for j in range(2):
                        act.wait_ge(v_used, 2 * i + j - 1)
                        table_hi(j, 16 * i + 16 * (N_KEYS // 2 + 1))
                        gated_hi(j, 2 * i + j)
                    if extra:
                        part = wg_hi[:, :, :].rearrange("p c n -> p (c n)")
                        src = wg_raw[:, :, :].rearrange("p c n -> p (c n)")
                        nc.scalar.activation(part[:, bass.ds((i - 48) * 512, 512)], src[:, bass.ds((i - 48) * 512, 512)],
                                             ACT.Copy).then_inc(wg_hi_ready, 1)

            v_pairs(1, 48, False)
            act.wait_ge(wg_loaded, 16)
            act.wait_ge(g_lo_ready, 96)
            v_pairs(48, N_KEYS // 2, True)
            act.wait_ge(wp_loaded, 32)
            act.wait_ge(g_lo_ready, N_KEYS)
            nc.scalar.activation(wp_hi[:, :, :], wp_raw[:, :, :], ACT.Copy).then_inc(ple_hi, 1)
            nc.scalar.activation(pt_hi[:, :, :], pt_raw[:, :, :], ACT.Copy).then_inc(ple_hi, 1)
            act.wait_ge(h2_ready, 4)
            norm(3, h, 1, xs_end)
            transposed_hi(3)
            for u in range(4):
                act.wait_ge(gate_done, u + 1)
                nc.scalar.activation(sig[:, u, :], bank[u][:, :], ACT.Sigmoid).then_inc(sig_ready, 1)

        @block.vector
        def _(dve):
            steps = [0]

            def link(ins):
                steps[0] += 1
                ins.then_inc(dve_step, 1)
                dve.wait_ge(dve_step, steps[0])

            def split_group(n):
                dve.wait_ge(w_hi_ready, n + 1)
                nc.vector.tensor_tensor(w_lo[:, n % 2, :, :], w_raw[:, n % 2, :, :],
                                        w_hi[:, n % 2, :, :].bitcast(f32), ALU.subtract).then_inc(w_lo_ready, 1)

            squares = [0]

            def norm(k, src, halves, xs=xs):
                n = D // halves
                squares[0] += TT * halves
                dve.wait_ge(squares_done, squares[0])
                nc.vector.tensor_scalar(MS[:, 0:TT * halves], SS[:, 0:TT * halves], 1.0 / n, EPS, ALU.mult,
                                        ALU.add).then_inc(mean_ready, 1)
                dve.wait_ge(root_ready, k + 1)
                link(nc.vector.reciprocal(RSTD[:, 0:TT * halves], RSTD[:, 0:TT * halves]))
                for tt in range(TT):
                    for q in range(halves):
                        c = tt * halves + q
                        ins = nc.vector.tensor_scalar(xs[:, tt, q * n:(q + 1) * n], src[:, tt, q * n:(q + 1) * n],
                                                      RSTD[:, c:c + 1], None, ALU.mult)
                    ins.then_inc(xs_ready, 1)

            def transposed_lo(k):
                for b in range(4):
                    dve.wait_ge(xt_hi_ready, 4 * k + b + 1)
                    for c in (2 * b, 2 * b + 1):
                        ins = nc.vector.scalar_tensor_tensor(out=xt_lo[:, c, :], in0=half(b, c % 2),
                                                             scalar=gain[:, k, c:c + 1],
                                                             in1=xt_hi[:, c, :].bitcast(f32), op0=ALU.mult,
                                                             op1=ALU.subtract)
                    ins.then_inc(xt_lo_ready, 1)

            dve.wait_ge(tab_loaded, 32)
            nc.vector.memset(tab_in[REL:REL + 1, TAB:TAB + NH], -1e30).then_inc(tab_loaded, 1)
            norm(0, h, 1)
            split_group(0)
            transposed_lo(0)
            split_group(1)
            split_group(2)
            dve.wait_ge(group_out, 4)
            for tt in range(TT):
                link(nc.vector.tensor_tensor(square[:, :, :], qk_nat[:, tt, :, :], qk_nat[:, tt, :, :], ALU.mult))
                link(nc.vector.tensor_reduce(QSS[:, 16 * tt:16 * tt + 16], square[:, :, :], AX.X, ALU.add))
            nc.vector.tensor_scalar(QSS, QSS, 1.0 / HD, EPS, ALU.mult, ALU.add).then_inc(qk_mean, 1)
            dve.wait_ge(qk_root, 1)
            link(nc.vector.reciprocal(QRSTD, QRSTD))
            for tt in range(TT):
                r = QRSTD[:, 16 * tt:16 * tt + 16].unsqueeze(2).to_broadcast([P, 2 * NH, HD])
                nc.vector.tensor_tensor(qk_nat[:, tt, :, :], qk_nat[:, tt, :, :], r, ALU.mult).then_inc(qk_normed, 1)
            split_group(3)
            split_group(4)
            split_group(5)
            for e in range(2):
                dve.wait_ge(z_softplus, e + 1)
                nc.vector.tensor_tensor(sb_sp[:, e, :], sb_sp[:, e, :], sb_w[:, e, :], ALU.add).then_inc(sp_added, 1)
            split_group(6)
            dve.wait_ge(bias_ready, 4)

            def biased(r, dst, first, n, s_from):
                dve.wait_ge(qk_done, r + 1)
                for e in range(2):
                    a, b = first + e, first + e + 2 * n - 1
                    ins = nc.vector.scalar_tensor_tensor(
                        out=dst[:, a:b:2, :], in0=bank[6 + e][:, :].rearrange("p (a b) -> p a b", a=n), scalar=SCALE,
                        in1=bias[:, a:b:2, s_from:SEQ], op0=ALU.mult, op1=ALU.add)
                ins.then_inc(qk_biased, 1)

            def shifted(tt, s, mx):
                dve.wait_ge(qk_biased, [1, 3][tt])
                link(nc.vector.tensor_reduce(mx, s[:, :, :], AX.X, ALU.max))
                n = [P, SEQ][tt]
                nc.vector.tensor_tensor(s[:, :, :], s[:, :, :], mx.unsqueeze(2).to_broadcast([P, NH, n]),
                                        ALU.subtract).then_inc(s_shifted, 1)

            biased(0, s0, 0, 4, P)
            biased(1, s1, 0, 2, 0)
            shifted(0, s0, MX0)
            biased(2, s1, 4, 2, 0)
            shifted(1, s1, MX1)
            for tt, s in ((0, s0), (1, s1)):
                dve.wait_ge(s_exp, tt + 1)
                link(nc.vector.tensor_reduce(SUM[:, 8 * tt:8 * tt + 8], s[:, :, :], AX.X, ALU.add))
                link(nc.vector.reciprocal(SUM[:, 8 * tt:8 * tt + 8], SUM[:, 8 * tt:8 * tt + 8]))
            split_group(7)
            for tt in range(TT):
                dve.wait_ge(pv_done, tt + 1)
                r = SUM[:, 8 * tt:8 * tt + 8].unsqueeze(2).to_broadcast([P, NH, HD])
                nc.vector.tensor_tensor(o_nat[:, tt, 0:512].rearrange("p (a b) -> p a b", a=NH),
                                        bank[6 + tt][:, :].rearrange("p (a b) -> p a b", a=NH), r,
                                        ALU.mult).then_inc(pv_out, 1)
            norm(1, o_nat, 2)
            transposed_lo(1)
            for g in range(2):
                dve.wait_ge(w_used, OUT0 + g + 1)
                for tt in range(TT):
                    nc.vector.tensor_tensor(h[:, tt, 512 * g:512 * g + 512], h[:, tt, 512 * g:512 * g + 512],
                                            bank[4 + 2 * g + tt][:, :], ALU.add).then_inc(h1_ready, 1)
            norm(2, h, 1)
            split_group(8)
            transposed_lo(2)
            split_group(9)

            def query_part(n):
                for q in range(2):
                    dve.wait_ge(query_hi_ready, 2 * n + q + 1)
                    g = 4 * n + 2 * q
                    nc.vector.tensor_tensor(query_lo[:, g:g + 2, :].rearrange("p a b -> p (a b)"),
                                            bank[4 + 2 * (n % 2) + q][:, :],
                                            query_hi[:, g:g + 2, :].rearrange("p a b -> p (a b)").bitcast(f32),
                                            ALU.subtract).then_inc(query_lo_ready, 1)

            query_part(0)
            split_group(10)
            query_part(1)
            split_group(11)
            dve.wait_ge(sk_hi_ready, 1)
            nc.vector.tensor_tensor(sk_lo[:, :, :], sk_raw[:, :, :], sk_hi[:, :, :].bitcast(f32),
                                    ALU.subtract).then_inc(sk_lo_ready, 1)
            query_part(2)
            query_part(3)

            def table_lo(j, count):
                dve.wait_ge(t_hi_ready, count)
                nc.vector.tensor_tensor(t_lo[:, j, :], t_raw[:, j, :], t_hi[:, j, :].bitcast(f32),
                                        ALU.subtract).then_inc(t_lo_ready, 1)

            table_lo(0, 1)
            table_lo(1, 2)
            dve.wait_ge(s_out, 8)

            def top16(src, values, places, scratch):
                link(nc.vector.max(values[:, 0:8], src))
                link(nc.vector.match_replace(scratch, values[:, 0:8], src, -3e38))
                nc.vector.max_index(places[:, 0:8], values[:, 0:8], src)
                link(nc.vector.max(values[:, 8:16], scratch))
                link(nc.vector.max_index(places[:, 8:16], values[:, 8:16], scratch))

            def halves(tt, g):
                top16(scores[:, tt, g, :], top_v[:, tt, g, :], top_i[:, tt, g, :], rest[:, g % 2, 0:P])

            def pairs_of(tt):
                v = top_v[:, tt, :, :].rearrange("p (h two) k -> p h two k", two=2)
                link(nc.vector.tensor_copy(top_f[:, tt, :, :], top_i[:, tt, :, :]))
                link(nc.vector.tensor_tensor(cand[:, :, :, :],
                                             v[:, :, 0, :].unsqueeze(3).to_broadcast([P, PH, TOPK, TOPK]),
                                             v[:, :, 1, :].unsqueeze(2).to_broadcast([P, PH, TOPK, TOPK]), ALU.add))

            def best_of(tt, hh):
                top16(cand[:, hh, :, :].rearrange("p a b -> p (a b)"), best_v[:, tt, hh, :],
                      best_p[:, tt, TOPK * hh:TOPK * (hh + 1)], rest[:, hh % 2, :])

            def positions(tt):
                nc.vector.tensor_scalar(pos_u[:, 0, :], best_p[:, tt, :], 4, None, ALU.logical_shift_right)
                link(nc.vector.tensor_scalar(pos_u[:, 1, :], best_p[:, tt, :], 15, None, ALU.bitwise_and))
                link(nc.vector.tensor_copy(pos_f[:, :, :], pos_u[:, :, :]))
                top = best_v[:, tt, :, 0:1].to_broadcast([P, PH, TOPK])
                nc.vector.tensor_tensor(gate[:, tt, :, :], best_v[:, tt, :, :], top,
                                        ALU.subtract).then_inc(gate_shifted, 1)

            def compared(tt, q):
                if 2 * tt + q:
                    dve.wait_ge(hit_used, 2 * tt + q)
                lanes = iota[:, 0:TOPK].unsqueeze(1).unsqueeze(1).to_broadcast([P, PH, TOPK, TOPK])
                place = pos_f[:, q, :].rearrange("p (a b) -> p a b", a=PH).unsqueeze(3).to_broadcast(
                    [P, PH, TOPK, TOPK])
                nc.vector.tensor_tensor(hit[:, :, :, :], lanes, place, ALU.is_equal).then_inc(hit_eq, 1)

            def picked(tt, q):
                dve.wait_ge(hit_ready, 2 * tt + q + 1)
                nc.vector.tensor_reduce(pick[:, tt, q, :].rearrange("p (a b) -> p a b", a=PH), hit[:, :, :, :], AX.X,
                                        ALU.add).then_inc(hit_used, 1)

            units = [lambda g=g: halves(0, g) for g in range(PG)] + [lambda: pairs_of(0)]
            units += [lambda hh=hh: best_of(0, hh) for hh in range(PH)] + [lambda: positions(0), lambda: compared(0, 0)]
            second = [lambda g=g: halves(1, g) for g in range(PG)]
            second[4:4] = [lambda: picked(0, 0), lambda: compared(0, 1)]
            second[10:10] = [lambda: picked(0, 1)]
            units += second + [lambda: pairs_of(1)]
            units += [lambda hh=hh: best_of(1, hh) for hh in range(PH)] + [lambda: positions(1)]
            wait = lambda: None
            units += [lambda: compared(1, 0), wait, wait, lambda: picked(1, 0), lambda: compared(1, 1), wait, wait,
                      lambda: picked(1, 1)]
            assert len(units) < GATHER_SPLIT - 2
            for n in range(2, GATHER_SPLIT):
                if units:
                    units.pop(0)()
                table_lo(n % 2, n + 1)
            dve.wait_ge(gate_exp, 1)
            link(nc.vector.tensor_reduce(GSUM.rearrange("p (a b) -> p a b", a=TT), gate[:, :, :, :], AX.X, ALU.add))
            link(nc.vector.reciprocal(GSUM, GSUM))
            nc.vector.tensor_tensor(gate[:, :, :, :], gate[:, :, :, :],
                                    GSUM.rearrange("p (a b) -> p a b", a=TT).unsqueeze(3).to_broadcast(
                                        [P, TT, PH, TOPK]), ALU.mult).then_inc(picks_ready, 1)
            for q in range(3):
                dve.wait_ge(pick_t_done, q + 1)
                nc.vector.tensor_copy(pick_t[:, q, :], half(q, 0)).then_inc(pick_t_out, 1)
            with dve.Fori(GATHER_SPLIT // 2, N_KEYS // 2) as i:
                for j in range(2):
                    table_lo(j, 2 * i + j + 1)
            table_lo(0, N_KEYS + 1)
            table_lo(1, N_KEYS + 2)

            def one_hots(k, s):
                for q in range(4):
                    t = 4 * s + q
                    ins = nc.vector.tensor_scalar(hot_j[:, k, q, :], iota, pick_t[:, 1, bass.ds(t, 1)],
                                                  pick_t[:, 2, bass.ds(t, 1)], ALU.is_equal, ALU.mult)
                ins.then_inc(hot_j_ready, 1)

            def gated_set(k, s):
                dst = slots[:, :, bass.ds(4 * s, 4)]
                nc.vector.tensor_tensor(dst, dst, bank[2 + k][:, :].rearrange("p (t j) -> p j t", t=4),
                                        ALU.mult).then_inc(gated, 1)

            dve.wait_ge(pick_t_out, 3)
            one_hots(0, 0)
            one_hots(1, 1)
            dve.wait_ge(gelu_done, N_KEYS)
            with dve.Fori(1, SEQ // 8) as i:
                for k in range(2):
                    dve.wait_ge(gates_done, 2 * i + k - 1)
                    gated_set(k, 2 * i + k - 2)
                    one_hots(k, 2 * i + k)
            for k in range(2):
                dve.wait_ge(gates_done, SEQ // 4 - 1 + k)
                gated_set(k, SEQ // 4 - 2 + k)

            def gated_lo(j, n, count):
                dve.wait_ge(g_hi_ready, count)
                src = slots[:, bass.ds(n, 1), :].rearrange("p o t -> p (o t)")
                nc.vector.tensor_tensor(g_lo[:, j, :], src, g_hi[:, j, :].bitcast(f32),
                                        ALU.subtract).then_inc(g_lo_ready, 1)

            gated_lo(0, 0, 1)
            gated_lo(1, 1, 2)

            def v_pairs(first, last, extra):
                with dve.Fori(first, last) as i:
                    for j in range(2):
                        table_lo(j, N_KEYS + 2 * i + j + 1)
                        gated_lo(j, 2 * i + j, 2 * i + j + 1)
                    if extra:
                        dve.wait_ge(wg_hi_ready, i - 47)
                        at = bass.ds((i - 48) * 512, 512)
                        flat = lambda t: t[:, :, :].rearrange("p c n -> p (c n)")
                        nc.vector.tensor_tensor(flat(wg_lo)[:, at], flat(wg_raw)[:, at],
                                                flat(wg_hi)[:, at].bitcast(f32), ALU.subtract).then_inc(wg_lo_ready, 1)

            v_pairs(1, 48, False)
            v_pairs(48, N_KEYS // 2, True)
            dve.wait_ge(v_used, N_KEYS)
            for tt in range(TT):
                for q in range(2):
                    nc.vector.tensor_tensor(h[:, tt, 512 * q:512 * q + 512], h[:, tt, 512 * q:512 * q + 512],
                                            bank[2 * tt + q][:, :], ALU.add).then_inc(h2_ready, 1)
            norm(3, h, 1, xs_end)
            transposed_lo(3)
            for u in range(4):
                tt, q = u // 2, u % 2
                dve.wait_ge(sig_ready, u + 1)
                nc.vector.tensor_tensor(sig[:, u, :], sig[:, u, :], bank[4 + u][:, :],
                                        ALU.mult).then_inc(sig_used, 1)
                dve.wait_ge(sig_used, u + 1)
                nc.vector.tensor_tensor(h[:, tt, 512 * q:512 * q + 512], h[:, tt, 512 * q:512 * q + 512],
                                        sig[:, u, :], ALU.add).then_inc(y_ready, 1)

        @block.gpsimd
        def _(pool):
            def strict(t, e, half_s):
                if half_s == 0:
                    v = t[:, e, 0:1024].rearrange("p (i t) -> p i t", i=4)[:, :, 0:P]
                else:
                    v = t[:, e, 1024:1536].rearrange("p (i t) -> p i t", i=4)
                return nc.gpsimd.affine_select(out=v, in_=v, compare_op=ALU.is_gt, fill=0.0, base=0,
                                               pattern=[[0, 4], [1, P]], channel_multiplier=-1)

            for e in range(2):
                pool.wait_ge(sp_added, e + 1)
                strict(sb_sp, e, 0)
                strict(sb_sp, e, 1).then_inc(sp_masked, 1)
            for e in range(2):
                pool.wait_ge(w_exp, 3 * (e + 1))
                strict(sb_w, e, 0)
                strict(sb_w, e, 1).then_inc(w_masked, 1)
            for tt in range(TT):
                for q in range(2):
                    number = top_f[:, tt, :, :].rearrange("p (h two) k -> p h two k", two=2)[:, :, q, :].unsqueeze(
                        2).to_broadcast([P, PH, TOPK, TOPK])
                    pool.wait_ge(hit_eq, 2 * tt + q + 1)
                    nc.gpsimd.tensor_tensor(hit[:, :, :, :], hit[:, :, :, :], number, ALU.mult).then_inc(hit_ready, 1)

            def one_hots(k, s):
                chosen = pick_t[:, 0, bass.ds(4 * s, 4)].unsqueeze(2).to_broadcast([P, 4, P])
                nc.gpsimd.tensor_tensor(hot_i[:, k, :, :], iota.unsqueeze(1).to_broadcast([P, 4, P]), chosen,
                                        ALU.subtract).then_inc(hot_i_diff, 1)

            pool.wait_ge(pick_t_out, 3)
            one_hots(0, 0)
            one_hots(1, 1)
            with pool.Fori(1, SEQ // 8) as i:
                for k in range(2):
                    pool.wait_ge(gates_done, 2 * i + k - 1)
                    one_hots(k, 2 * i + k)
            pool.wait_ge(ple_hi, 2)
            nc.gpsimd.tensor_tensor(wp_lo[:, :, :], wp_raw[:, :, :], wp_hi[:, :, :].bitcast(f32),
                                    ALU.subtract).then_inc(ple_lo, 1)
            nc.gpsimd.tensor_tensor(pt_lo[:, :, :], pt_raw[:, :, :], pt_hi[:, :, :].bitcast(f32),
                                    ALU.subtract).then_inc(ple_lo, 1)

        @block.tensor
        def _(pe):
            mm = nc.tensor.matmul

            def transposes(k, xs=xs):
                for c in range(DC):
                    for tt in range(TT):
                        if c == 0:
                            pe.wait_ge(xs_ready, TT * k + tt + 1)
                        ins = nc.tensor.transpose(bank[c // 2][:, 256 * (c % 2) + P * tt:256 * (c % 2) + P * (tt + 1)],
                                                  xs[:, tt, P * c:P * (c + 1)], ident)
                    if c % 2:
                        ins.then_inc(xt_done, 1)

            def three(dst, pairs, last=None):
                n = len(pairs)
                for c, ((ah, al), (bh, bl)) in enumerate(pairs):
                    mm(dst, ah, bh, start=(c == 0), stop=False)
                    mm(dst, ah, bl, start=False, stop=False)
                    ins = mm(dst, al, bh, start=False, stop=(c == n - 1))
                return ins

            def rows_group(n, b):
                pe.wait_ge(w_lo_ready, n + 1)
                for tt in range(TT):
                    t = slice(P * tt, P * (tt + 1))
                    ins = three(bank[b + tt][:, :], [((xt_hi[:, c, t], xt_lo[:, c, t]),
                                                      (w_hi[:, n % 2, c, :], w_lo[:, n % 2, c, :])) for c in range(DC)])
                ins.then_inc(w_used, 1)

            def columns_group(n, b):
                pe.wait_ge(w_lo_ready, n + 1)
                for q in range(4):
                    m = slice(P * q, P * (q + 1))
                    ins = three(half(b + q // 2, q % 2), [((w_hi[:, n % 2, c, m], w_lo[:, n % 2, c, m]),
                                                          (xt_hi[:, c, :], xt_lo[:, c, :])) for c in range(DC)])
                ins.then_inc(w_used, 1)

            pe.wait_ge(small_loaded, 48)
            transposes(0)
            pe.wait_ge(tab_loaded, 33)
            mm(bank[7][0:NH, 0:TAB], tab_in[:, TAB:TAB + NH], tab_in[:, 0:TAB], start=True, stop=True).then_inc(
                tab_made, 1)
            pe.wait_ge(xt_lo_ready, 4)
            rows_group(Q_M, 4)
            pe.wait_ge(tab_copied, 1)
            rows_group(K_M, 6)
            pe.wait_ge(bias_loaded, 16)
            for b in range(4):
                mm(bank[b][:, :], flip, skew[:, 2 * b:2 * b + 2, :].rearrange("p a b -> p (a b)"), start=True,
                   stop=True).then_inc(flip_done, 1)
            pe.wait_ge(group_out, 2)
            columns_group(Q_S, 4)
            pe.wait_ge(qk_normed, TT)
            pe.wait_ge(bias_ready, 4)
            for g in range(8):
                for tt in range(TT):
                    ins = nc.tensor.transpose(bank[g // 2][:, 256 * (g % 2) + P * tt:256 * (g % 2) + P * (tt + 1)],
                                              qk_nat[:, tt, 2 * g:2 * g + 2, :].rearrange("p a b -> p (a b)"), ident)
                if g % 2:
                    ins.then_inc(qkt_done, 1)
            pe.wait_ge(group_out, 4)
            columns_group(K_S, 6)

            pe.wait_ge(qkt_out, 4)
            pe.wait_ge(group_out, 8)
            for e in range(2):
                r = slice(HD * e, HD * (e + 1))
                for i in range(4):
                    mm(bank[3 * e + i // 2][:, 256 * (i % 2):256 * (i % 2) + 256], qkt_s[r, 4 + i, 0:P], qkt_s[r, i, :],
                       start=(i % 2 == 0), stop=True, skip_group_check=True)
                for i in range(4):
                    ins = mm(bank[3 * e + 2][:, P * i:P * (i + 1)], qkt_s[r, 4 + i, P:SEQ], qkt_s[r, i, P:SEQ],
                             start=(i == 0), stop=True, skip_group_check=True)
                ins.then_inc(z_done, 1)
            rows_group(V_M, 6)
            pe.wait_ge(group_out, 10)
            rows_group(V_S, 6)

            pe.wait_ge(group_out, 12)
            for r, (tt, first, n) in enumerate(((0, 0, 4), (1, 0, 2), (1, 4, 2))):
                if r:
                    pe.wait_ge(qk_biased, r)
                width = P * (tt + 1)
                for i in range(n):
                    for e in range(2):
                        hh = first + 2 * i + e
                        rows = slice(HD * e, HD * (e + 1))
                        ins = mm(bank[6 + e][:, width * i:width * (i + 1)], qkt_m[rows, hh // 2, P * tt:P * (tt + 1)],
                                 qkt_m[rows, 4 + hh // 2, 0:width], start=True, stop=True)
                ins.then_inc(qk_done, 1)
            for e in range(2):
                pe.wait_ge(sp_masked, e + 1)
                lower, upper = sb_sp[:, e, 0:1024], sb_sp[:, e, 1024:1536]
                for b in range(2):
                    mm(bank[3 * e + b][:, :], neg_tri, lower[:, 512 * b:512 * (b + 1)], start=False, stop=False,
                       skip_group_check=True)
                    mm(bank[3 * e + b][:, :].rearrange("p (i t) -> p i t", i=2)[:, :, P:SEQ], neg_ones,
                       upper[:, 256 * b:256 * (b + 1)].rearrange("p (i t) -> p i t", i=2), start=False, stop=True,
                       skip_group_check=True)
                mm(bank[3 * e + 2][:, :], neg_tri, upper, start=False, stop=True,
                   skip_group_check=True).then_inc(cum_done, 1)

            pe.wait_ge(w_exp, 6)
            pe.wait_ge(s_exp, 1)
            for hh in range(NH):
                ins = nc.tensor.transpose(bank[hh // 4][:, P * (hh % 4):P * (hh % 4 + 1)], s0[:, hh, :], ident)
                if hh % 4 == 3:
                    ins.then_inc(pt_done, 1)
            pe.wait_ge(s_exp, 2)
            for hh in range(NH):
                for ss in range(2):
                    c = 256 * (hh % 2) + P * ss
                    ins = nc.tensor.transpose(bank[2 + hh // 2][:, c:c + P], s1[:, hh, P * ss:P * (ss + 1)], ident)
                if hh % 2:
                    ins.then_inc(pt_done, 1)
            pe.wait_ge(qk_biased, 3)
            pe.wait_ge(pt_out, 2)
            for hh in range(NH):
                ins = mm(bank[6][:, HD * hh:HD * (hh + 1)], probs_t[:, hh // 4, P * (hh % 4):P * (hh % 4 + 1)],
                         v_all[:, 0, HD * hh:HD * (hh + 1)], start=True, stop=True)
            ins.then_inc(pv_done, 1)
            for hh in range(NH):
                if hh % 2 == 0:
                    pe.wait_ge(pt_out, 3 + hh // 2)
                place = (2 + hh // 2) % 4
                for ss in range(2):
                    c = 256 * (hh % 2) + P * ss
                    ins = mm(bank[7][:, HD * hh:HD * (hh + 1)], probs_t[:, place, c:c + P],
                             v_all[:, ss, HD * hh:HD * (hh + 1)], start=(ss == 0), stop=(ss == 1))
            ins.then_inc(pv_done, 1)
            pe.wait_ge(w_masked, 2)
            for tt in range(TT):
                for hh in range(NH):
                    e, i = hh % 2, hh // 2
                    cols = slice(512 + HD * hh, 512 + HD * (hh + 1))
                    dst = bank[tt][:, HD * hh:HD * (hh + 1)]
                    c = 256 * i + P * tt
                    ins = mm(dst, sb_w[:, e, c:c + P], v_all[:, 0, cols], start=True, stop=(tt == 0))
                    if tt:
                        ins = mm(dst, sb_w[:, e, 1024 + P * i:1024 + P * (i + 1)], v_all[:, 1, cols], start=False,
                                 stop=True)
                ins.then_inc(spv_done, 1)

            transposes(1)
            pe.wait_ge(pv_out, 2)
            pe.wait_ge(xt_lo_ready, 8)
            rows_group(OUT0, 4)
            rows_group(OUT0 + 1, 6)

            transposes(2)
            pe.wait_ge(xt_lo_ready, 12)
            for n in range(4):
                if n == 0:
                    pe.wait_ge(h1_ready, 4)
                if n >= 2:
                    pe.wait_ge(query_lo_ready, 2 * (n - 1))
                columns_group(QUERY0 + n, 4 + 2 * (n % 2))
            pe.wait_ge(sk_lo_ready, 1)
            pe.wait_ge(query_lo_ready, 8)
            for u in range(8):
                tt, g0 = u // 4, 4 * (u % 4)
                b = [0, 1, 2, 3, 6, 7, 0, 1][u]
                if u >= 6:
                    pe.wait_ge(s_out, u - 5)
                t = slice(P * tt, P * (tt + 1))
                for q in range(4):
                    g = g0 + q
                    ins = three(bank[b][:, P * q:P * (q + 1)], [((query_hi[:, g, t], query_lo[:, g, t]),
                                                                (sk_hi[:, g % 2, :], sk_lo[:, g % 2, :]))])
                ins.then_inc(s_done, 1)

            def hidden(j, count):
                pe.wait_ge(t_lo_ready, count)
                three(bank[4 + j][:, 0:SEQ], [((t_hi[:, j, P * c:P * (c + 1)], t_lo[:, j, P * c:P * (c + 1)]),
                                               (xt_hi[:, c, :], xt_lo[:, c, :])) for c in range(DC)]
                      ).then_inc(hid_done, 1)

            hidden(0, 1)
            hidden(1, 2)

            def u_pairs(first, last):
                with pe.Fori(first, last) as i:
                    for j in range(2):
                        pe.wait_ge(gelu_done, 2 * i + j - 1)
                        hidden(j, 2 * i + j + 1)

            u_pairs(1, GATHER_SPLIT // 2)
            for q in range(2):
                if q == 0:
                    pe.wait_ge(hit_used, 2 * TT)
                for tt in range(TT):
                    ins = nc.tensor.transpose(bank[q][:, P * tt:P * (tt + 1)], pick[:, tt, q, :],
                                              ident)
                ins.then_inc(pick_t_done, 1)
            pe.wait_ge(picks_ready, 1)
            for tt in range(TT):
                ins = nc.tensor.transpose(bank[2][:, P * tt:P * (tt + 1)],
                                          gate[:, tt, :, :].rearrange("p a b -> p (a b)"), ident)
            ins.then_inc(pick_t_done, 1)
            u_pairs(GATHER_SPLIT // 2, N_KEYS // 2)

            def gates(k, count):
                pe.wait_ge(hot_i_ready, count)
                pe.wait_ge(hot_j_ready, count)
                for q in range(4):
                    ins = mm(bank[2 + k][:, P * q:P * (q + 1)], hot_i[:, k, q, :], hot_j[:, k, q, :], start=True,
                             stop=True)
                ins.then_inc(gates_done, 1)

            gates(0, 1)
            gates(1, 2)
            with pe.Fori(1, SEQ // 8) as i:
                for k in range(2):
                    pe.wait_ge(gated, 2 * i + k - 1)
                    gates(k, 2 * i + k + 1)

            def expert_sum(j, count, first):
                pe.wait_ge(t_lo_ready, count + N_KEYS)
                pe.wait_ge(g_lo_ready, count)
                for tt in range(TT):
                    t = slice(P * tt, P * (tt + 1))
                    for q in range(2):
                        d = slice(512 * q, 512 * (q + 1))
                        dst = bank[2 * tt + q][:, :]
                        mm(dst, g_hi[:, j, t], t_hi[:, j, d], start=first, stop=False, skip_group_check=True)
                        mm(dst, g_hi[:, j, t], t_lo[:, j, d], start=False, stop=False, skip_group_check=True)
                        ins = mm(dst, g_lo[:, j, t], t_hi[:, j, d], start=False, stop=True, skip_group_check=True)
                ins.then_inc(v_used, 1)

            expert_sum(0, 1, True)
            expert_sum(1, 2, False)
            with pe.Fori(1, N_KEYS // 2) as i:
                for j in range(2):
                    expert_sum(j, 2 * i + j + 1, False)

            pe.wait_ge(ple_lo, 2)
            for u in range(4):
                tt, q = u // 2, u % 2
                t, d = slice(P * tt, P * (tt + 1)), slice(512 * q, 512 * (q + 1))
                three(bank[4 + u][:, :], [((pt_hi[:, c, t], pt_lo[:, c, t]), (wp_hi[:, c, d], wp_lo[:, c, d]))
                                          for c in range(PLE // P)]).then_inc(ple_done, 1)
            pe.wait_ge(h2_ready, 4)
            transposes(3, xs_end)
            pe.wait_ge(xt_lo_ready, 16)
            pe.wait_ge(wg_lo_ready, 16)
            for u in range(4):
                tt, q = u // 2, u % 2
                t, d = slice(P * tt, P * (tt + 1)), slice(512 * q, 512 * (q + 1))
                three(bank[u][:, :], [((xt_hi[:, c, t], xt_lo[:, c, t]), (wg_hi[:, c, d], wg_lo[:, c, d]))
                                      for c in range(DC)]).then_inc(gate_done, 1)


def bucket_table():
    dist = 255 - np.arange(TAB)
    n = np.maximum(dist, 0)
    exact = REL // 2
    large = exact + (np.log(np.maximum(n, 1) / exact) / np.log(128 / exact) * (REL - exact)).astype(np.int64)
    bucket = np.where(n < exact, n, np.minimum(large, REL - 1))
    bucket = np.where(dist < 0, REL, bucket)
    return (np.arange(REL + 1)[:, None] == bucket[None, :]).astype(np.float32)


def constants():
    i = np.arange(P)
    tri = np.where(i[:, None] >= i[None, :], -1.0 / SCALE, 0.0)
    return np.ascontiguousarray(np.stack(
        [np.eye(P), tri, np.full((P, P), -1.0 / SCALE), np.broadcast_to(i, (P, P)),
         np.eye(P)[::-1]], axis=1).astype(np.float32))


def by_group(w, width=GW):
    k, n = w.shape
    return np.ascontiguousarray(w.reshape(k // P, P, n // width, width).transpose(2, 1, 0, 3))


def kernel(**inputs):
    import concourse.bacc as bacc
    from concourse.bass_utils import run_bass_kernel_spmd

    a = {k: np.asarray(v) for k, v in inputs.items()}
    w_in = by_group(a["w_in"][0])[[0, 1, 3, 4, 2, 5]]
    column = lambda g: g.reshape(DC, P).T
    arrays = {
        "x": a["x"].reshape(SEQ, D),
        "p_t": a["p"].reshape(SEQ, PLE // P, P).transpose(2, 1, 0),
        "rel_bias": a["rel_bias"],
        "bucket_onehot": bucket_table(),
        "consts": constants(),
        "gains": np.stack([column(a["attn_norm"][0]),
                           column(np.concatenate([a["out_norm_moba"][0], a["out_norm_sb"][0]])),
                           column(a["ffn_norm"][0]), column(a["ple_norm"][0])], axis=1),
        "qk_gain": np.stack([np.tile(a["q_norm"][0], 2), np.tile(a["k_norm"][0], 2)], axis=1),
        "w_in": w_in,
        "w_out": by_group(a["w_out"][0]),
        "w_query": by_group(a["peer_query"][0].reshape(D, PG * P)),
        "subkeys_t": a["peer_sub_keys"][0].transpose(2, 0, 1),
        "u_chunks": a["peer_u"][0].reshape(N_KEYS, N_KEYS, DC, P).transpose(1, 3, 2, 0).reshape(N_KEYS, P, D),
        "v_chunks": a["peer_v"][0].reshape(N_KEYS, N_KEYS, D).transpose(1, 0, 2),
        "w_gate": a["w_ple_gate"][0].reshape(DC, P, D).transpose(1, 0, 2),
        "w_ple": a["w_ple"][0].reshape(PLE // P, P, D).transpose(1, 0, 2),
    }
    arrays = {k: np.ascontiguousarray(v) for k, v in arrays.items()}
    nc = bacc.Bacc("TRN2", target_bir_lowering=False, num_devices=1)
    args = [nc.dram_tensor(k, v.shape, mybir.dt.from_np(v.dtype), kind="ExternalInput").ap() for k, v in arrays.items()]
    out = nc.dram_tensor("out", (SEQ, D), mybir.dt.float32, kind="ExternalOutput").ap()
    layer_program(nc, *args, out)
    r = run_bass_kernel_spmd(nc, [arrays], core_ids=[0])
    return r.results[0]["out"].reshape(1, SEQ, D)
```

```python
from contextlib import ExitStack

import numpy as np
import concourse.bass as bass
from concourse import mybir

P = 128
SEQ = 256
D = 1024
DC = D // P
TT = SEQ // P
HD = 64
NH = 8
REL = 32
N_KEYS = 128
TOPK = 16
PH = 8
PG = 2 * PH
PLE = 256
EPS = 1e-6
SCALE = HD ** -0.5
GW = 512
RING = 4
LEAD = 2
FIRST = 64
ONES_AT = 44
ONES = 4
TOPK_END = 52
EXP_AT = 52
PICKS_AT = 56
BLOCKS = ((0, 1, 16), (1, 3, 8), (4, 4, 4), (8, 8, 1))
PAIRS = sum(n * m for _, n, m in BLOCKS)
assert all(b < m for a0, n, m in BLOCKS for a in range(a0, a0 + n) for b in range(16 // (a + 1)))
SETS = SEQ // 4
assert SETS == N_KEYS - FIRST
TAB = 384

Q_M, K_M, Q_S, K_S, V_M, V_S = range(6)
OUT0, QUERY0, N_GROUPS = 6, 8, 12


def layer_program(nc, x, p_t, rel_bias, bucket_onehot, consts, gains, qk_gain, w_in, w_out, w_query,
                  subkeys_t, u_chunks, v_chunks, w_gate, w_ple, out):
    f32, f32r, u32 = mybir.dt.float32, mybir.dt.float32r, mybir.dt.uint32
    ALU, ACT, AX = mybir.AluOpType, mybir.ActivationFunctionType, mybir.AxisListType

    ctx = ExitStack()
    with ctx:
        base = (nc.sbuf_base + 63) // 64 * 64
        sizes = dict(h=2 * D, xt_hi=DC * SEQ, xt_lo=DC * SEQ, cst=5 * P, gains=4 * DC, qkg=32, stats=192)
        at, where = base, {}
        for name, n in sizes.items():
            where[name] = at
            at += 4 * n
        ZONE = at
        BIG = ZONE + 4 * 13312
        assert BIG + 4 * P * SEQ <= nc.sbuf_usable_end

        def tile(name, shape, offset, dt=f32):
            return nc.alloc_sbuf_tensor_at(name, shape, dt, offset=offset)

        h = tile("h", [P, TT, D], where["h"])
        xt_hi = tile("xt_hi", [P, DC, SEQ], where["xt_hi"], f32r)
        xt_lo = tile("xt_lo", [P, DC, SEQ], where["xt_lo"], f32r)
        cst = tile("cst", [P, 5, P], where["cst"])
        gain = tile("gain", [P, 4, DC], where["gains"])
        qkg = tile("qkg", [P, 2], where["qkg"])
        stats = tile("stats", [P, 192], where["stats"])
        ident, neg_tri, neg_ones, iota = cst[:, 0, :], cst[:, 1, :], cst[:, 2, :], cst[:, 3, :]
        flip = cst[:, 4, :]

        w_raw = tile("w_raw", [P, 2, DC, GW], BIG)
        w_hi = tile("w_hi", [P, 2, DC, GW], BIG + 4 * 8192, f32r)
        w_lo = tile("w_lo", [P, 2, DC, GW], BIG + 4 * 16384, f32r)
        UP = BIG + 4 * 24576
        bias = tile("bias", [P, NH, SEQ], UP)
        skew = tile("skew", [P, NH, SEQ], UP + 4 * 6144)
        v_all = tile("v_all", [P, TT, 2 * NH * HD], UP + 4 * 2048)
        qk_nat = tile("qk_nat", [P, TT, 2 * NH, HD], UP + 4 * 4096)
        o_nat = tile("o_nat", [P, TT, D], UP + 4 * 4096)
        qkt_s = tile("qkt_s", [P, 8, SEQ], UP + 4 * 6144)
        query = tile("query", [P, PG, SEQ], UP)
        slots = tile("slots", [P, N_KEYS, SEQ], BIG)
        scores = tile("scores", [P, TT, PG, N_KEYS], BIG + 4 * 20480)
        o = UP
        top_v = tile("top_v", [P, TT, PG, TOPK], o); o += 4 * 512
        top_i = tile("top_i", [P, TT, PG, TOPK], o, u32); o += 4 * 512
        top_f = tile("top_f", [P, TT, PG, TOPK], o); o += 4 * 512
        rest = tile("rest", [P, 2, 256], o); o += 4 * 512
        cand = tile("cand", [P, PH, PAIRS], o); o += 4 * PH * PAIRS
        best_v = tile("best_v", [P, TT, PH, TOPK], o); o += 4 * 256
        pos_u = tile("pos_u", [P, 3, PH * TOPK], o, u32); o += 4 * 384
        pos_f = tile("pos_f", [P, 3, PH * TOPK], o); o += 4 * 384
        pos_m = tile("pos_m", [P, 4, PH * TOPK], o); o += 4 * 512
        pos_ab = tile("pos_ab", [P, 2, PH * TOPK], o); o += 4 * 256
        assert o <= BIG + 4 * P * SEQ
        wg_raw = tile("wg_raw", [P, DC, D], BIG)
        wg_lo = tile("wg_lo", [P, DC, D], BIG, f32r)
        wg_hi = tile("wg_hi", [P, DC, D], BIG + 4 * 8192, f32r)
        wp_raw = tile("wp_raw", [P, 2, D], BIG + 4 * 16384)
        wp_lo = tile("wp_lo", [P, 2, D], BIG + 4 * 16384, f32r)
        wp_hi = tile("wp_hi", [P, 2, D], BIG + 4 * 18432, f32r)
        pt_raw = tile("pt_raw", [P, 2, SEQ], BIG + 4 * 20480)
        pt_lo = tile("pt_lo", [P, 2, SEQ], BIG + 4 * 20480, f32r)
        pt_hi = tile("pt_hi", [P, 2, SEQ], BIG + 4 * 20992, f32r)
        xs_end = tile("xs_end", [P, TT, D], BIG + 4 * 21504)
        sig = tile("sig", [P, 4, 512], BIG + 4 * 24576)

        s0 = tile("s0", [P, NH, P], ZONE)
        s1 = tile("s1", [P, NH, SEQ], ZONE + 4 * 1024)
        square = tile("square", [P, 2 * NH, HD], ZONE)
        probs_t = tile("probs_t", [P, 4, 512], ZONE + 4 * 3072)
        sb_sp = tile("sb_sp", [P, 2, 1536], ZONE + 4 * 5120)
        sb_w = tile("sb_w", [P, 2, 1536], ZONE + 4 * 8192)
        qkt_m = tile("qkt_m", [P, 8, SEQ], ZONE + 4 * 11264)
        xs = tile("xs", [P, TT, D], ZONE + 4 * 5120)
        tab_in = tile("tab_in", [REL + 1, TAB + NH], ZONE + 4 * 8192)
        tab_out = tile("tab_out", [NH, TAB], ZONE + 4 * 9216)
        t_raw = tile("t_raw", [P, RING, D], ZONE)
        t_lo = tile("t_lo", [P, RING, D], ZONE, f32r)
        hit = tile("hit", [P, PH, TOPK, TOPK], ZONE + 4 * 4096)
        hot_i = tile("hot_i", [P, 2, 4, P], ZONE + 4 * 4096)
        hot_j = tile("hot_j", [P, 2, 4, P], ZONE + 4 * 5120)
        late = tile("late", [P, RING, SEQ], ZONE + 4 * 6144)
        g_hi = tile("g_hi", [P, 2, SEQ], ZONE + 4 * 6144, f32r)
        g_lo = tile("g_lo", [P, 2, SEQ], ZONE + 4 * 6656, f32r)
        t_hi = tile("t_hi", [P, RING, D], ZONE + 4 * 7168, f32r)
        o = ZONE + 4 * 11264
        pick_t = tile("pick_t", [P, 3, SEQ], o); o += 4 * 768
        sk = tile("sk", [P, 2, N_KEYS], o); o += 4 * 256
        pick = tile("pick", [P, TT, 2, P], o); o += 4 * 512
        gate = tile("gate", [P, TT, PH, TOPK], o); o += 4 * 256
        assert o <= BIG

        bank = [ctx.enter_context(nc.psum_tensor(f"bank{b}", [P, 512], f32)) for b in range(8)]
        table = nc.dram_tensor("bias_table", (NH, TAB), f32, kind="Internal")

        def half(b, j):
            return bank[b][:, 256 * j:256 * (j + 1)]

        def sem(name):
            return ctx.enter_context(nc.semaphore(name))

        x_loaded, small_loaded, tab_loaded = sem("x_loaded"), sem("small_loaded"), sem("tab_loaded")
        tab_made, tab_copied = sem("tab_made"), sem("tab_copied")
        tab_stored, bias_loaded = sem("tab_stored"), sem("bias_loaded")
        flip_done, bias_ready = sem("flip_done"), sem("bias_ready")
        w_loaded = [sem("w_loaded0"), sem("w_loaded1")]
        w_hi_ready, w_lo_ready, w_used = sem("w_hi_ready"), sem("w_lo_ready"), sem("w_used")
        squares_done, mean_ready, root_ready = sem("squares_done"), sem("mean_ready"), sem("root_ready")
        xs_ready, xt_done, xt_hi_ready, xt_lo_ready = (sem("xs_ready"), sem("xt_done"), sem("xt_hi_ready"),
                                                       sem("xt_lo_ready"))
        group_out = sem("group_out")
        qk_mean, qk_root, qk_normed = sem("qk_mean"), sem("qk_root"), sem("qk_normed")
        qkt_done, qkt_out = sem("qkt_done"), sem("qkt_out")
        z_done, z_softplus, sp_added, sp_masked = sem("z_done"), sem("z_softplus"), sem("sp_added"), sem("sp_masked")
        z_read, cum_done, w_exp, w_masked = sem("z_read"), sem("cum_done"), sem("w_exp"), sem("w_masked")
        qk_done, qk_biased, s_shifted, s_exp = sem("qk_done"), sem("qk_biased"), sem("s_shifted"), sem("s_exp")
        pt_done, pt_out, pv_done, pv_out = sem("pt_done"), sem("pt_out"), sem("pv_done"), sem("pv_out")
        spv_done, spv_out = sem("spv_done"), sem("spv_out")
        h1_ready, query_ready, sk_loaded = sem("h1_ready"), sem("query_ready"), sem("sk_loaded")
        s_done, s_out = sem("s_done"), sem("s_out")
        t_loaded = [sem(f"t_loaded{q}") for q in range(RING)]
        t_hi_ready, t_lo_ready, t_lo_pool = sem("t_hi_ready"), sem("t_lo_ready"), sem("t_lo_pool")
        halves_done, ones_ready, late_used = sem("halves_done"), sem("ones_ready"), sem("late_used")
        table_row = sem("table_row")
        hid_done, gelu_done = sem("hid_done"), sem("gelu_done")
        hit_ready, hit_used = sem("hit_ready"), sem("hit_used")
        hit_eq = sem("hit_eq")
        gate_shifted, gate_exp, picks_ready = sem("gate_shifted"), sem("gate_exp"), sem("picks_ready")
        pick_t_done, pick_t_out = sem("pick_t_done"), sem("pick_t_out")
        hot_i_diff, hot_i_square = sem("hot_i_diff"), sem("hot_i_square")
        hot_i_ready, hot_j_ready, gates_done, gated = (sem("hot_i_ready"), sem("hot_j_ready"), sem("gates_done"),
                                                       sem("gated"))
        g_hi_ready, g_lo_ready, v_used = sem("g_hi_ready"), sem("g_lo_ready"), sem("v_used")
        wg_loaded, wp_loaded, wg_hi_ready, wg_lo_ready = sem("wg_loaded"), sem("wp_loaded"), sem("wg_hi_ready"), sem("wg_lo_ready")
        ple_hi, ple_lo, ple_done = sem("ple_hi"), sem("ple_lo"), sem("ple_done")
        h2_ready, gate_done, sig_ready, sig_used, y_ready, stored = (
            sem("h2_ready"), sem("gate_done"), sem("sig_ready"), sem("sig_used"), sem("y_ready"), sem("stored"))
        act_step, dve_step, pool_step = sem("act_step"), sem("dve_step"), sem("pool_step")

        block = ctx.enter_context(nc.Block())

        def u_lo(q, i):
            return (t_lo_pool, (RING - 1) * i + q) if q else (t_lo_ready, i + 1)

        v_lo = N_KEYS // RING + 1 - LEAD

        def w_source(n):
            if n < OUT0:
                return w_in[n]
            return w_out[n - OUT0] if n < QUERY0 else w_query[n - QUERY0]

        SS, RSTD = stats[:, 0:4], stats[:, 4:8]
        QSS, QRSTD = stats[:, 8:40], stats[:, 40:72]
        MX0, MX1, SUM = stats[:, 72:80], stats[:, 80:88], stats[:, 88:104]
        GSUM = stats[:, 104:120]
        MS = stats[:, 120:124]

        @block.sync
        def _(sp):
            for tt in range(TT):
                sp.dma_start(h[:, tt, :], x[tt * P:(tt + 1) * P, :]).then_inc(x_loaded, 16)
            sp.dma_start(cst[:, :, :], consts).then_inc(small_loaded, 16)
            sp.dma_start(gain[:, :, :], gains).then_inc(small_loaded, 16)
            sp.dma_start(qkg[:, :], qk_gain).then_inc(small_loaded, 16)
            sp.dma_start(tab_in[:, 0:TAB], bucket_onehot).then_inc(tab_loaded, 16)
            sp.dma_start(tab_in[0:REL, TAB:TAB + NH], rel_bias).then_inc(tab_loaded, 16)

            def load_group(n):
                if n >= 2:
                    sp.wait_ge(w_lo_ready, n - 1)
                sp.dma_start(w_raw[:, n % 2, :, :], w_source(n)).then_inc(w_loaded[n % 2], 16)

            load_group(0)
            load_group(1)
            sp.wait_ge(tab_copied, 1)
            sp.dma_start(table.ap(), tab_out[:, :]).then_inc(tab_stored, 16)
            sp.wait_ge(tab_stored, 16)
            sp.dma_start(skew[:, :, :], bass.AP(table, 0, [[1, P], [TAB, NH], [1, SEQ]])).then_inc(bias_loaded, 16)
            for n in range(2, N_GROUPS):
                load_group(n)
                if n == 9:
                    sp.wait_ge(spv_out, 2)
                    sp.wait_ge(pv_out, 2)
                    sp.dma_start(sk[:, :, :], subkeys_t).then_inc(sk_loaded, 16)
                    for q in range(RING):
                        sp.dma_start(t_raw[:, q, :], u_chunks[q]).then_inc(t_loaded[q], 16)

            def load_chunk(table, q, n):
                sp.dma_start(t_raw[:, q, :], table[bass.ds(n, 1)].rearrange("o p f -> (o p) f")
                             ).then_inc(t_loaded[q], 16)

            with sp.Fori(1, N_KEYS // RING) as i:
                for q in range(RING):
                    sp.wait_ge(hid_done, RING * i + q - RING + 1)
                    load_chunk(u_chunks, q, RING * i + q)
            for q in range(RING):
                sp.wait_ge(hid_done, N_KEYS - RING + q + 1)
                load_chunk(v_chunks, q, q)

            def v_loads(first, last, gate_weights):
                with sp.Fori(first, last) as i:
                    if gate_weights:
                        sp.dma_start(wg_raw[:, bass.ds(i - first, 1), :].rearrange("p o n -> p (o n)"),
                                     w_gate[:, bass.ds(i - first, 1), :].rearrange("p o n -> p (o n)")
                                     ).then_inc(wg_loaded, 16)
                    for q in range(RING):
                        sp.wait_ge(v_used, RING * i + q - RING + 1)
                        load_chunk(v_chunks, q, RING * i + q)

            v_loads(1, 12, False)
            sp.wait_ge(g_lo_ready, 32)
            v_loads(12, 20, True)
            v_loads(20, 23, False)
            sp.wait_ge(g_lo_ready, 82)
            sp.dma_start(wp_raw[:, :, :], w_ple).then_inc(wp_loaded, 16)
            sp.dma_start(pt_raw[:, :, :], p_t).then_inc(wp_loaded, 16)
            v_loads(23, N_KEYS // RING, False)
            for tt in range(TT):
                sp.wait_ge(y_ready, 2 * (tt + 1))
                sp.dma_start(out[tt * P:(tt + 1) * P, :], h[:, tt, :]).then_inc(stored, 16)
            sp.wait_ge(stored, 16 * TT)

        @block.scalar
        def _(act):
            steps = [0]

            def link(ins):
                steps[0] += 1
                ins.then_inc(act_step, 1)
                act.wait_ge(act_step, steps[0])

            def split_group(n):
                act.wait_ge(w_loaded[n % 2], 16 * (n // 2 + 1))
                if n >= 2:
                    act.wait_ge(w_used, n - 1)
                nc.scalar.activation(w_hi[:, n % 2, :, :], w_raw[:, n % 2, :, :], ACT.Copy).then_inc(w_hi_ready, 1)

            def norm(k, src, halves, xs=xs):
                n = D // halves
                for tt in range(TT):
                    for q in range(halves):
                        c = tt * halves + q
                        nc.scalar.activation(xs[:, tt, q * n:(q + 1) * n], src[:, tt, q * n:(q + 1) * n], ACT.Square,
                                             accum_out=SS[:, c:c + 1]).then_inc(squares_done, 1)
                act.wait_ge(mean_ready, k + 1)
                nc.scalar.activation(RSTD[:, 0:TT * halves], MS[:, 0:TT * halves], ACT.Sqrt).then_inc(root_ready, 1)

            def transposed_hi(k):
                for b in range(4):
                    act.wait_ge(xt_done, 4 * k + b + 1)
                    for c in (2 * b, 2 * b + 1):
                        ins = nc.scalar.activation(xt_hi[:, c, :], half(b, c % 2), ACT.Copy, scale=gain[:, k, c:c + 1])
                    ins.then_inc(xt_hi_ready, 1)

            def out_of_psum(n):
                act.wait_ge(w_used, n + 1)
                b = 4 if n in (Q_M, Q_S) else 6
                for q in range(2):
                    if n in (Q_M, K_M):
                        dst = qk_nat[:, q, NH * n:NH * (n + 1), :].rearrange("p a b -> p (a b)")
                    elif n in (Q_S, K_S):
                        g = 4 * (n - Q_S) + 2 * q
                        dst = qkt_s[:, g:g + 2, :].rearrange("p a b -> p (a b)")
                    else:
                        dst = v_all[:, q, 512 * (n - V_M):512 * (n - V_M + 1)]
                    nc.scalar.copy(dst, bank[b + q][:, :]).then_inc(group_out, 1)

            act.wait_ge(x_loaded, 16 * TT)
            norm(0, h, 1)
            split_group(0)
            act.wait_ge(small_loaded, 48)
            transposed_hi(0)
            act.wait_ge(tab_made, 1)
            nc.scalar.copy(tab_out[:, :], bank[7][0:NH, 0:TAB]).then_inc(tab_copied, 1)
            split_group(1)
            out_of_psum(Q_M)
            split_group(2)
            for b in range(4):
                act.wait_ge(flip_done, b + 1)
                nc.scalar.copy(bias[:, 2 * b:2 * b + 2, :].rearrange("p a b -> p (a b)"), bank[b][:, :]).then_inc(
                    bias_ready, 1)
            out_of_psum(K_M)
            act.wait_ge(qk_mean, 1)
            nc.scalar.activation(QRSTD, QSS, ACT.Sqrt).then_inc(qk_root, 1)
            split_group(3)
            out_of_psum(Q_S)
            for b in range(4):
                act.wait_ge(qkt_done, b + 1)
                nc.scalar.activation(qkt_m[:, 2 * b:2 * b + 2, :].rearrange("p a b -> p (a b)"), bank[b][:, :],
                                     ACT.Copy, scale=qkg[:, b // 2:b // 2 + 1]).then_inc(qkt_out, 1)
            split_group(4)
            out_of_psum(K_S)
            split_group(5)
            for e in range(2):
                act.wait_ge(z_done, e + 1)
                for b in range(3):
                    src = bank[3 * e + b][:, :]
                    nc.scalar.activation(sb_w[:, e, 512 * b:512 * (b + 1)], src, ACT.Relu, scale=SCALE)
                    ins = nc.scalar.activation(sb_sp[:, e, 512 * b:512 * (b + 1)], src, ACT.Abs, scale=SCALE)
                link(ins)
            for e in range(2):
                link(nc.scalar.activation(sb_sp[:, e, :], sb_sp[:, e, :], ACT.Exp, scale=-1.0))
                nc.scalar.activation(sb_sp[:, e, :], sb_sp[:, e, :], ACT.Ln, bias=1.0).then_inc(z_softplus, 1)
            out_of_psum(V_M)
            split_group(6)
            out_of_psum(V_S)
            split_group(7)
            act.wait_ge(s_shifted, 1)
            nc.scalar.activation(s0[:, :, :], s0[:, :, :], ACT.Exp).then_inc(s_exp, 1)
            for e in range(2):
                act.wait_ge(cum_done, e + 1)
                for b in range(3):
                    nc.scalar.activation(sb_w[:, e, 512 * b:512 * (b + 1)], bank[3 * e + b][:, :], ACT.Exp,
                                         scale=SCALE).then_inc(w_exp, 1)
            act.wait_ge(s_shifted, 2)
            nc.scalar.activation(s1[:, :, :], s1[:, :, :], ACT.Exp).then_inc(s_exp, 1)
            for b in range(6):
                act.wait_ge(pt_done, b + 1)
                if b >= 4:
                    act.wait_ge(pv_done, 1)
                nc.scalar.copy(probs_t[:, b % 4, :], bank[b][:, :]).then_inc(pt_out, 1)
            for tt in range(TT):
                act.wait_ge(spv_done, tt + 1)
                nc.scalar.copy(o_nat[:, tt, 512:1024], bank[tt][:, :]).then_inc(spv_out, 1)
            act.wait_ge(spv_out, 2)
            act.wait_ge(pv_out, 2)
            norm(1, o_nat, 2)
            transposed_hi(1)
            act.wait_ge(h1_ready, 4)
            norm(2, h, 1)
            split_group(8)
            transposed_hi(2)
            split_group(9)

            def query_part(n):
                act.wait_ge(w_used, QUERY0 + n + 1)
                for q in range(2):
                    g = 4 * n + 2 * q
                    nc.scalar.copy(query[:, g:g + 2, :].rearrange("p a b -> p (a b)"),
                                   bank[4 + 2 * (n % 2) + q][:, :]).then_inc(query_ready, 1)

            query_part(0)
            split_group(10)
            query_part(1)
            split_group(11)
            query_part(2)

            def table_hi(q, count):
                act.wait_ge(t_loaded[q % RING], 16 * count)
                nc.scalar.activation(t_hi[:, q % RING, :], t_raw[:, q % RING, :], ACT.Copy).then_inc(t_hi_ready, 1)

            query_part(3)
            for n in range(LEAD):
                table_hi(n, 1)
            for u in range(8):
                act.wait_ge(s_done, u + 1)
                b = [0, 1, 2, 3, 6, 7, 0, 1][u]
                nc.scalar.copy(scores[:, u // 4, 4 * (u % 4):4 * (u % 4) + 4, :].rearrange("p a b -> p (a b)"),
                               bank[b][:, :]).then_inc(s_out, 1)

            def u_steps(first, last):
                with act.Fori(first // RING, last // RING) as i:
                    for q in range(RING):
                        table_hi(q + LEAD, i + 1 + (q + LEAD) // RING)
                        act.wait_ge(hid_done, RING * i + q + 1)
                        nc.scalar.activation(slots[:, bass.ds(RING * i + q, 1), :].rearrange("p o t -> p (o t)"),
                                             bank[4 + q][:, 0:SEQ], ACT.Gelu).then_inc(gelu_done, 1)

            nc.scalar.preload_act_table(ACT.Gelu)
            u_steps(0, EXP_AT)
            act.wait_ge(gate_shifted, TT)
            nc.scalar.activation(gate[:, :, :, :], gate[:, :, :, :], ACT.Exp).then_inc(gate_exp, 1)
            nc.scalar.preload_act_table(ACT.Gelu)
            u_steps(EXP_AT, FIRST)

            def one_hots(k, count):
                act.wait_ge(hot_i_diff, count)
                nc.scalar.activation(hot_i[:, k, :, :], hot_i[:, k, :, :], ACT.Square).then_inc(hot_i_square, 1)
                act.wait_ge(hot_i_square, count)
                nc.scalar.activation(hot_i[:, k, :, :], hot_i[:, k, :, :], ACT.Relu, scale=-1.0,
                                     bias=1.0).then_inc(hot_i_ready, 1)

            def late_step(q, i, first=False):
                table_hi(q + LEAD, i + 1 + (q + LEAD) // RING)
                one_hots(q % 2, RING * i + q - FIRST + 1)
                if not first:
                    act.wait_ge(late_used, RING * i + q - FIRST - RING + 1)
                act.wait_ge(hid_done, RING * i + q + 1)
                nc.scalar.activation(late[:, q, :], bank[4 + q][:, 0:SEQ], ACT.Gelu).then_inc(gelu_done, 1)

            for q in range(RING):
                late_step(q, FIRST // RING, True)
            with act.Fori(FIRST // RING + 1, N_KEYS // RING) as i:
                for q in range(RING):
                    late_step(q, i)

            def gated_hi(k, n):
                src = slots[:, bass.ds(n, 1), :].rearrange("p o t -> p (o t)")
                nc.scalar.activation(g_hi[:, k, :], src, ACT.Copy).then_inc(g_hi_ready, 1)

            act.wait_ge(gated, SETS)
            act.wait_ge(late_used, N_KEYS - FIRST)
            gated_hi(0, 0)

            def v_step(q, i, skip=(), first=False):
                if q + 1 not in skip:
                    if not first:
                        act.wait_ge(v_used, RING * i + q)
                    gated_hi((q + 1) % 2, RING * i + q + 1)
                if q + LEAD not in skip:
                    table_hi(q + LEAD, i + 1 + (q + LEAD) // RING + N_KEYS // RING)

            def gate_weights_hi(c):
                act.wait_ge(wg_loaded, 16 * DC)
                at = bass.ds(c, 1)
                nc.scalar.activation(wg_hi[:, at, :], wg_raw[:, at, :], ACT.Copy).then_inc(wg_hi_ready, 1)

            for q in range(RING):
                v_step(q, 0, first=(q == 0))
            with act.Fori(1, 24) as i:
                for q in range(RING):
                    v_step(q, i)
            act.wait_ge(wp_loaded, 32)
            act.wait_ge(g_lo_ready, 84)
            nc.scalar.activation(wp_hi[:, :, :], wp_raw[:, :, :], ACT.Copy).then_inc(ple_hi, 1)
            nc.scalar.activation(pt_hi[:, :, :], pt_raw[:, :, :], ACT.Copy).then_inc(ple_hi, 1)
            with act.Fori(24, N_KEYS // RING - 1) as i:
                for q in range(RING):
                    v_step(q, i)
                gate_weights_hi(i - 24)
            for q in range(RING):
                v_step(q, N_KEYS // RING - 1, skip=(RING, RING + 1))
            gate_weights_hi(DC - 1)
            act.wait_ge(h2_ready, 4)
            norm(3, h, 1, xs_end)
            transposed_hi(3)
            for u in range(4):
                act.wait_ge(gate_done, u + 1)
                nc.scalar.activation(sig[:, u, :], bank[u][:, :], ACT.Sigmoid).then_inc(sig_ready, 1)

        @block.vector
        def _(dve):
            steps = [0]

            def link(ins):
                steps[0] += 1
                ins.then_inc(dve_step, 1)
                dve.wait_ge(dve_step, steps[0])

            def split_group(n):
                dve.wait_ge(w_hi_ready, n + 1)
                nc.vector.tensor_tensor(w_lo[:, n % 2, :, :], w_raw[:, n % 2, :, :],
                                        w_hi[:, n % 2, :, :].bitcast(f32), ALU.subtract).then_inc(w_lo_ready, 1)

            squares = [0]

            def norm(k, src, halves, xs=xs):
                n = D // halves
                squares[0] += TT * halves
                dve.wait_ge(squares_done, squares[0])
                nc.vector.tensor_scalar(MS[:, 0:TT * halves], SS[:, 0:TT * halves], 1.0 / n, EPS, ALU.mult,
                                        ALU.add).then_inc(mean_ready, 1)
                dve.wait_ge(root_ready, k + 1)
                link(nc.vector.reciprocal(RSTD[:, 0:TT * halves], RSTD[:, 0:TT * halves]))
                for tt in range(TT):
                    for q in range(halves):
                        c = tt * halves + q
                        ins = nc.vector.tensor_scalar(xs[:, tt, q * n:(q + 1) * n], src[:, tt, q * n:(q + 1) * n],
                                                      RSTD[:, c:c + 1], None, ALU.mult)
                    ins.then_inc(xs_ready, 1)

            def transposed_lo(k):
                for b in range(4):
                    dve.wait_ge(xt_hi_ready, 4 * k + b + 1)
                    for c in (2 * b, 2 * b + 1):
                        ins = nc.vector.scalar_tensor_tensor(out=xt_lo[:, c, :], in0=half(b, c % 2),
                                                             scalar=gain[:, k, c:c + 1],
                                                             in1=xt_hi[:, c, :].bitcast(f32), op0=ALU.mult,
                                                             op1=ALU.subtract)
                    ins.then_inc(xt_lo_ready, 1)

            nc.vector.memset(tab_in[REL:REL + 1, TAB:TAB + NH], -1e30).then_inc(table_row, 1)
            norm(0, h, 1)
            split_group(0)
            transposed_lo(0)
            split_group(1)
            split_group(2)
            dve.wait_ge(group_out, 4)
            for tt in range(TT):
                link(nc.vector.tensor_tensor(square[:, :, :], qk_nat[:, tt, :, :], qk_nat[:, tt, :, :], ALU.mult))
                link(nc.vector.tensor_reduce(QSS[:, 16 * tt:16 * tt + 16], square[:, :, :], AX.X, ALU.add))
            nc.vector.tensor_scalar(QSS, QSS, 1.0 / HD, EPS, ALU.mult, ALU.add).then_inc(qk_mean, 1)
            dve.wait_ge(qk_root, 1)
            link(nc.vector.reciprocal(QRSTD, QRSTD))
            for tt in range(TT):
                r = QRSTD[:, 16 * tt:16 * tt + 16].unsqueeze(2).to_broadcast([P, 2 * NH, HD])
                nc.vector.tensor_tensor(qk_nat[:, tt, :, :], qk_nat[:, tt, :, :], r, ALU.mult).then_inc(qk_normed, 1)
            split_group(3)
            split_group(4)
            split_group(5)
            for e in range(2):
                dve.wait_ge(z_softplus, e + 1)
                nc.vector.tensor_tensor(sb_sp[:, e, :], sb_sp[:, e, :], sb_w[:, e, :], ALU.add).then_inc(sp_added, 1)
            split_group(6)
            dve.wait_ge(bias_ready, 4)

            def biased(r, dst, first, n, s_from):
                dve.wait_ge(qk_done, r + 1)
                for e in range(2):
                    a, b = first + e, first + e + 2 * n - 1
                    ins = nc.vector.scalar_tensor_tensor(
                        out=dst[:, a:b:2, :], in0=bank[6 + e][:, :].rearrange("p (a b) -> p a b", a=n), scalar=SCALE,
                        in1=bias[:, a:b:2, s_from:SEQ], op0=ALU.mult, op1=ALU.add)
                ins.then_inc(qk_biased, 1)

            def shifted(tt, s, mx):
                dve.wait_ge(qk_biased, [1, 3][tt])
                link(nc.vector.tensor_reduce(mx, s[:, :, :], AX.X, ALU.max))
                n = [P, SEQ][tt]
                nc.vector.tensor_tensor(s[:, :, :], s[:, :, :], mx.unsqueeze(2).to_broadcast([P, NH, n]),
                                        ALU.subtract).then_inc(s_shifted, 1)

            biased(0, s0, 0, 4, P)
            biased(1, s1, 0, 2, 0)
            shifted(0, s0, MX0)
            biased(2, s1, 4, 2, 0)
            shifted(1, s1, MX1)
            for tt, s in ((0, s0), (1, s1)):
                dve.wait_ge(s_exp, tt + 1)
                link(nc.vector.tensor_reduce(SUM[:, 8 * tt:8 * tt + 8], s[:, :, :], AX.X, ALU.add))
                link(nc.vector.reciprocal(SUM[:, 8 * tt:8 * tt + 8], SUM[:, 8 * tt:8 * tt + 8]))
            split_group(7)
            for tt in range(TT):
                dve.wait_ge(pv_done, tt + 1)
                r = SUM[:, 8 * tt:8 * tt + 8].unsqueeze(2).to_broadcast([P, NH, HD])
                nc.vector.tensor_tensor(o_nat[:, tt, 0:512].rearrange("p (a b) -> p a b", a=NH),
                                        bank[6 + tt][:, :].rearrange("p (a b) -> p a b", a=NH), r,
                                        ALU.mult).then_inc(pv_out, 1)
            norm(1, o_nat, 2)
            transposed_lo(1)
            for g in range(2):
                dve.wait_ge(w_used, OUT0 + g + 1)
                for tt in range(TT):
                    nc.vector.tensor_tensor(h[:, tt, 512 * g:512 * g + 512], h[:, tt, 512 * g:512 * g + 512],
                                            bank[4 + 2 * g + tt][:, :], ALU.add).then_inc(h1_ready, 1)
            norm(2, h, 1)
            split_group(8)
            transposed_lo(2)
            split_group(9)

            split_group(10)
            split_group(11)

            def table_lo(q, count):
                dve.wait_ge(t_hi_ready, count)
                nc.vector.tensor_tensor(t_lo[:, q % RING, :], t_raw[:, q % RING, :],
                                        t_hi[:, q % RING, :].bitcast(f32), ALU.subtract).then_inc(t_lo_ready, 1)

            table_lo(0, 1)
            dve.wait_ge(s_out, 8)

            def top16(jobs):
                def each(op):
                    done = []
                    for job in jobs:
                        steps[0] += 1
                        op(*job).then_inc(dve_step, 1)
                        done.append(steps[0])
                    return done

                def after(done, op):
                    waits = iter(done)

                    def waited(*job):
                        dve.wait_ge(dve_step, next(waits))
                        return op(*job)
                    return each(waited)

                first = each(lambda src, v, i, rest: nc.vector.max(v[:, 0:8], src))
                replaced = after(first, lambda src, v, i, rest: nc.vector.match_replace(rest, v[:, 0:8], src, -3e38))
                each(lambda src, v, i, rest: nc.vector.max_index(i[:, 0:8], v[:, 0:8], src))
                second = after(replaced, lambda src, v, i, rest: nc.vector.max(v[:, 8:16], rest))
                last = after(second, lambda src, v, i, rest: nc.vector.max_index(i[:, 8:16], v[:, 8:16], rest))
                dve.wait_ge(dve_step, last[-1])

            def halves(tt, g):
                top16([(scores[:, tt, g + k, :], top_v[:, tt, g + k, :], top_i[:, tt, g + k, :], rest[:, k, 0:P])
                       for k in range(2)])

            def pairs_of(tt):
                v = top_v[:, tt, :, :].rearrange("p (h two) k -> p h two k", two=2)
                link(nc.vector.tensor_copy(top_f[:, tt, :, :], top_i[:, tt, :, :]))
                place = 0
                for a, n, m in BLOCKS:
                    ins = nc.vector.tensor_tensor(
                        cand[:, :, place:place + n * m].rearrange("p h (a b) -> p h a b", a=n),
                        v[:, :, 0, a:a + n].unsqueeze(3).to_broadcast([P, PH, n, m]),
                        v[:, :, 1, 0:m].unsqueeze(2).to_broadcast([P, PH, n, m]), ALU.add)
                    place += n * m
                link(ins)

            def best_of(tt, h):
                top16([(cand[:, hh, :], best_v[:, tt, hh, :], pos_u[:, 0, TOPK * hh:TOPK * (hh + 1)],
                        rest[:, hh % 2, 0:PAIRS]) for hh in (h, h + 1)])

            def positions(tt):
                nc.vector.tensor_scalar(pos_u[:, 1, :], pos_u[:, 0, :], 3, None, ALU.logical_shift_right)
                link(nc.vector.tensor_scalar(pos_u[:, 2, :], pos_u[:, 0, :], 2, None, ALU.logical_shift_right))
                link(nc.vector.tensor_copy(pos_f[:, :, :], pos_u[:, :, :]))
                c, c8, c4 = (pos_f[:, k, :] for k in range(3))
                m0, m1, m2, m3 = (pos_m[:, k, :] for k in range(4))
                a, b = pos_ab[:, 0, :], pos_ab[:, 1, :]
                link(nc.vector.tensor_scalar(m0, c8, -1.0, 0.0, ALU.add, ALU.max))
                link(nc.vector.scalar_tensor_tensor(out=m1, in0=c4, scalar=-6.0, in1=m0, op0=ALU.add, op1=ALU.max))
                link(nc.vector.scalar_tensor_tensor(out=a, in0=c, scalar=-48.0, in1=m1, op0=ALU.add, op1=ALU.max))
                nc.vector.tensor_scalar(m2, a, 8.0, 8.0, ALU.mult, ALU.add)
                link(nc.vector.tensor_scalar(m3, a, 4.0, 24.0, ALU.mult, ALU.add))
                nc.vector.scalar_tensor_tensor(out=m0, in0=a, scalar=16.0, in1=m2, op0=ALU.mult, op1=ALU.min)
                link(nc.vector.scalar_tensor_tensor(out=m1, in0=a, scalar=48.0, in1=m3, op0=ALU.add, op1=ALU.min))
                link(nc.vector.tensor_tensor(m2, m0, m1, ALU.min))
                link(nc.vector.tensor_tensor(b, c, m2, ALU.subtract))
                top = best_v[:, tt, :, 0:1].to_broadcast([P, PH, TOPK])
                nc.vector.tensor_tensor(gate[:, tt, :, :], best_v[:, tt, :, :], top,
                                        ALU.subtract).then_inc(gate_shifted, 1)

            def picked(tt, q):
                lanes = iota[:, 0:TOPK].unsqueeze(1).unsqueeze(1).to_broadcast([P, PH, TOPK, TOPK])
                place = pos_ab[:, q, :].rearrange("p (a b) -> p a b", a=PH).unsqueeze(3).to_broadcast(
                    [P, PH, TOPK, TOPK])
                number = top_f[:, tt, :, :].rearrange("p (h two) k -> p h two k", two=2)[:, :, q, :].unsqueeze(
                    2).to_broadcast([P, PH, TOPK, TOPK])

                def summed():
                    ins = nc.vector.tensor_reduce(pick[:, tt, q, :].rearrange("p (a b) -> p a b", a=PH),
                                                  hit[:, :, :, :], AX.X, ALU.add)
                    ins.then_inc(hit_used, 1)
                    dve.wait_ge(hit_used, 2 * tt + q + 1)

                return [lambda: link(nc.vector.tensor_tensor(hit[:, :, :, :], lanes, place, ALU.is_equal)),
                        lambda: link(nc.vector.tensor_tensor(hit[:, :, :, :], hit[:, :, :, :], number, ALU.mult)),
                        summed]

            def gates_of_picks():
                dve.wait_ge(gate_exp, 1)
                link(nc.vector.tensor_reduce(GSUM.rearrange("p (a b) -> p a b", a=TT), gate[:, :, :, :], AX.X,
                                             ALU.add))
                link(nc.vector.reciprocal(GSUM, GSUM))
                nc.vector.tensor_tensor(gate[:, :, :, :], gate[:, :, :, :],
                                        GSUM.rearrange("p (a b) -> p a b", a=TT).unsqueeze(3).to_broadcast(
                                            [P, TT, PH, TOPK]), ALU.mult).then_inc(picks_ready, 1)

            pieces = []
            for tt in range(TT):
                pieces += [(1, lambda tt=tt, g=g: halves(tt, g)) for g in range(0, PG, 2)]
                if tt:
                    pieces += [(0, lambda: dve.sem_inc(halves_done, 1))]
                pieces += [(1, lambda tt=tt: pairs_of(tt))]
                pieces += [(1, lambda tt=tt, hh=hh: best_of(tt, hh)) for hh in range(0, PH, 2)]
                pieces += [(2, lambda tt=tt: positions(tt))]
                pieces += [(2, lambda step=step: step()) for q in range(2) for step in picked(tt, q)]
            splits = TOPK_END // RING
            total, spent, pieces = sum(w for w, _ in pieces), 0, iter(pieces)
            for k in range(splits):
                while spent * splits < total * (k + 1):
                    weight, piece = next(pieces)
                    piece()
                    spent += weight
                table_lo(0, RING * (k + 1) + 1)
            gates_of_picks()

            for n in range(TOPK_END + RING, FIRST, RING):
                table_lo(0, n + 1)
            for q in range(3):
                dve.wait_ge(pick_t_done, q + 1)
                nc.vector.tensor_copy(pick_t[:, q, :], half(q, 0)).then_inc(pick_t_out, 1)
            table_lo(0, FIRST + 1)

            def one_hots(k, s):
                for q in range(4):
                    t = 4 * s + q
                    ins = nc.vector.tensor_scalar(hot_j[:, k, q, :], iota, pick_t[:, 1, bass.ds(t, 1)],
                                                  pick_t[:, 2, bass.ds(t, 1)], ALU.is_equal, ALU.mult)
                ins.then_inc(hot_j_ready, 1)

            def gated_set(b, s):
                dve.wait_ge(gates_done, s + 1)
                dst = slots[:, :, bass.ds(4 * s, 4)]
                nc.vector.tensor_tensor(dst, dst, bank[b][:, :].rearrange("p (t j) -> p j t", t=4),
                                        ALU.mult).then_inc(gated, 1)

            def late_gelu(q, n, count):
                dve.wait_ge(gelu_done, n + 1)
                dve.wait_ge(gated, count)
                dst = slots[:, bass.ds(n, 1), :].rearrange("p o t -> p (o t)")
                nc.vector.tensor_tensor(dst, dst, late[:, q, :], ALU.mult).then_inc(late_used, 1)

            def late_step(q, i, nth=2):
                n = RING * i + q
                s = n - FIRST
                one_hots(q % 2, s)
                if nth == 1:
                    dve.wait_ge(ones_ready, (N_KEYS - FIRST) // ONES)
                    dve.wait_ge(gelu_done, FIRST)
                if nth:
                    if nth > 1:
                        dve.wait_ge(late_used, s - 1)
                    gated_set((q - 1) % RING, s - 1)
                    late_gelu((q - 1) % RING, n - 1, s)
                if (q + LEAD) % RING == 0:
                    table_lo(0, n + LEAD + 1)

            dve.wait_ge(pick_t_out, 3)
            for q in range(RING):
                late_step(q, FIRST // RING, q)
            with dve.Fori(FIRST // RING + 1, N_KEYS // RING) as i:
                for q in range(RING):
                    late_step(q, i)
            dve.wait_ge(late_used, N_KEYS - FIRST - 1)
            gated_set(RING - 1, SETS - 1)
            late_gelu(RING - 1, N_KEYS - 1, SETS)

            def gated_lo(k, n):
                dve.wait_ge(g_hi_ready, n + 1)
                src = slots[:, bass.ds(n, 1), :].rearrange("p o t -> p (o t)")
                nc.vector.tensor_tensor(g_lo[:, k, :], src, g_hi[:, k, :].bitcast(f32),
                                        ALU.subtract).then_inc(g_lo_ready, 1)

            gated_lo(0, 0)

            def v_step(q, i, skip=()):
                if q + 1 not in skip:
                    gated_lo((q + 1) % 2, RING * i + q + 1)
                if q + LEAD not in skip:
                    table_lo(q + LEAD, N_KEYS + RING * i + q + LEAD + 1)

            def gate_weights_lo(c):
                dve.wait_ge(wg_hi_ready, c + 1)
                at = bass.ds(c, 1)
                nc.vector.tensor_tensor(wg_lo[:, at, :], wg_raw[:, at, :], wg_hi[:, at, :].bitcast(f32),
                                        ALU.subtract).then_inc(wg_lo_ready, 1)

            with dve.Fori(0, 24) as i:
                for q in range(RING):
                    v_step(q, i)
            with dve.Fori(24, N_KEYS // RING - 1) as i:
                for q in range(RING):
                    v_step(q, i)
                gate_weights_lo(i - 24)
            for q in range(RING):
                v_step(q, N_KEYS // RING - 1, skip=(RING, RING + 1))
            gate_weights_lo(DC - 1)
            dve.wait_ge(v_used, N_KEYS)
            for tt in range(TT):
                for q in range(2):
                    nc.vector.tensor_tensor(h[:, tt, 512 * q:512 * q + 512], h[:, tt, 512 * q:512 * q + 512],
                                            bank[2 * tt + q][:, :], ALU.add).then_inc(h2_ready, 1)
            norm(3, h, 1, xs_end)
            transposed_lo(3)
            for u in range(4):
                tt, q = u // 2, u % 2
                dve.wait_ge(sig_ready, u + 1)
                nc.vector.tensor_tensor(sig[:, u, :], sig[:, u, :], bank[4 + u][:, :],
                                        ALU.mult).then_inc(sig_used, 1)
                dve.wait_ge(sig_used, u + 1)
                nc.vector.tensor_tensor(h[:, tt, 512 * q:512 * q + 512], h[:, tt, 512 * q:512 * q + 512],
                                        sig[:, u, :], ALU.add).then_inc(y_ready, 1)

        @block.gpsimd
        def _(pool):
            def strict(t, e, half_s):
                if half_s == 0:
                    v = t[:, e, 0:1024].rearrange("p (i t) -> p i t", i=4)[:, :, 0:P]
                else:
                    v = t[:, e, 1024:1536].rearrange("p (i t) -> p i t", i=4)
                return nc.gpsimd.affine_select(out=v, in_=v, compare_op=ALU.is_gt, fill=0.0, base=0,
                                               pattern=[[0, 4], [1, P]], channel_multiplier=-1)

            for e in range(2):
                pool.wait_ge(sp_added, e + 1)
                strict(sb_sp, e, 0)
                strict(sb_sp, e, 1).then_inc(sp_masked, 1)
            for e in range(2):
                pool.wait_ge(w_exp, 3 * (e + 1))
                strict(sb_w, e, 0)
                strict(sb_w, e, 1).then_inc(w_masked, 1)

            def table_lo(q, n):
                pool.wait_ge(t_hi_ready, n + 1)
                nc.gpsimd.tensor_tensor(t_lo[:, q, :], t_raw[:, q, :], t_hi[:, q, :].bitcast(f32),
                                        ALU.subtract).then_inc(t_lo_pool, 1)

            def u_steps(first, last):
                with pool.Fori(first // RING, last // RING) as i:
                    for q in range(RING):
                        if (q + LEAD) % RING:
                            table_lo((q + LEAD) % RING, RING * i + q + LEAD)

            def ones_steps(first, last):
                for n in range(first, last):
                    if (n + LEAD) % RING:
                        table_lo((n + LEAD) % RING, n + LEAD)
                    at = FIRST + ONES * (n - ONES_AT)
                    nc.gpsimd.memset(slots[:, at:at + ONES, :], 1.0).then_inc(ones_ready, 1)

            for n in range(1, LEAD):
                table_lo(n, n)
            u_steps(0, ONES_AT)
            pool.wait_ge(halves_done, 1)
            ones_steps(ONES_AT, TOPK_END)
            pool.wait_ge(hit_used, 4)
            pool.wait_ge(gate_shifted, TT)
            ones_end = ONES_AT + (N_KEYS - FIRST) // ONES
            ones_steps(TOPK_END, ones_end)
            u_steps(ones_end, FIRST)

            def one_hots(k, s):
                chosen = pick_t[:, 0, bass.ds(4 * s, 4)].unsqueeze(2).to_broadcast([P, 4, P])
                nc.gpsimd.tensor_tensor(hot_i[:, k, :, :], iota.unsqueeze(1).to_broadcast([P, 4, P]), chosen,
                                        ALU.subtract).then_inc(hot_i_diff, 1)

            def late_step(q, i, first=False):
                n = RING * i + q
                s = n - FIRST
                if not (first and q < 2):
                    pool.wait_ge(gates_done, s - 1)
                one_hots(q % 2, s)
                if (q + LEAD) % RING:
                    table_lo((q + LEAD) % RING, n + LEAD)

            pool.wait_ge(pick_t_out, 3)
            for q in range(RING):
                late_step(q, FIRST // RING, True)
            with pool.Fori(FIRST // RING + 1, N_KEYS // RING) as i:
                for q in range(RING):
                    late_step(q, i)
            pool.wait_ge(ple_hi, 2)
            nc.gpsimd.tensor_tensor(wp_lo[:, :, :], wp_raw[:, :, :], wp_hi[:, :, :].bitcast(f32),
                                    ALU.subtract).then_inc(ple_lo, 1)
            nc.gpsimd.tensor_tensor(pt_lo[:, :, :], pt_raw[:, :, :], pt_hi[:, :, :].bitcast(f32),
                                    ALU.subtract).then_inc(ple_lo, 1)

        @block.tensor
        def _(pe):
            mm = nc.tensor.matmul

            def transposes(k, xs=xs):
                for c in range(DC):
                    for tt in range(TT):
                        if c == 0:
                            pe.wait_ge(xs_ready, TT * k + tt + 1)
                        ins = nc.tensor.transpose(bank[c // 2][:, 256 * (c % 2) + P * tt:256 * (c % 2) + P * (tt + 1)],
                                                  xs[:, tt, P * c:P * (c + 1)], ident)
                    if c % 2:
                        ins.then_inc(xt_done, 1)

            def three(dst, pairs, last=None):
                n = len(pairs)
                for c, ((ah, al), (bh, bl)) in enumerate(pairs):
                    mm(dst, ah, bh, start=(c == 0), stop=False)
                    mm(dst, ah, bl, start=False, stop=False)
                    ins = mm(dst, al, bh, start=False, stop=(c == n - 1))
                return ins

            def rows_group(n, b):
                pe.wait_ge(w_lo_ready, n + 1)
                for tt in range(TT):
                    t = slice(P * tt, P * (tt + 1))
                    ins = three(bank[b + tt][:, :], [((xt_hi[:, c, t], xt_lo[:, c, t]),
                                                      (w_hi[:, n % 2, c, :], w_lo[:, n % 2, c, :])) for c in range(DC)])
                ins.then_inc(w_used, 1)

            def columns_group(n, b):
                pe.wait_ge(w_lo_ready, n + 1)
                for q in range(4):
                    m = slice(P * q, P * (q + 1))
                    ins = three(half(b + q // 2, q % 2), [((w_hi[:, n % 2, c, m], w_lo[:, n % 2, c, m]),
                                                          (xt_hi[:, c, :], xt_lo[:, c, :])) for c in range(DC)])
                ins.then_inc(w_used, 1)

            pe.wait_ge(small_loaded, 48)
            transposes(0)
            pe.wait_ge(tab_loaded, 32)
            pe.wait_ge(table_row, 1)
            mm(bank[7][0:NH, 0:TAB], tab_in[:, TAB:TAB + NH], tab_in[:, 0:TAB], start=True, stop=True).then_inc(
                tab_made, 1)
            pe.wait_ge(xt_lo_ready, 4)
            rows_group(Q_M, 4)
            pe.wait_ge(tab_copied, 1)
            rows_group(K_M, 6)
            pe.wait_ge(bias_loaded, 16)
            for b in range(4):
                mm(bank[b][:, :], flip, skew[:, 2 * b:2 * b + 2, :].rearrange("p a b -> p (a b)"), start=True,
                   stop=True).then_inc(flip_done, 1)
            pe.wait_ge(group_out, 2)
            columns_group(Q_S, 4)
            pe.wait_ge(qk_normed, TT)
            pe.wait_ge(bias_ready, 4)
            for g in range(8):
                for tt in range(TT):
                    ins = nc.tensor.transpose(bank[g // 2][:, 256 * (g % 2) + P * tt:256 * (g % 2) + P * (tt + 1)],
                                              qk_nat[:, tt, 2 * g:2 * g + 2, :].rearrange("p a b -> p (a b)"), ident)
                if g % 2:
                    ins.then_inc(qkt_done, 1)
            pe.wait_ge(group_out, 4)
            columns_group(K_S, 6)

            pe.wait_ge(qkt_out, 4)
            pe.wait_ge(group_out, 8)
            for e in range(2):
                r = slice(HD * e, HD * (e + 1))
                for i in range(4):
                    mm(bank[3 * e + i // 2][:, 256 * (i % 2):256 * (i % 2) + 256], qkt_s[r, 4 + i, 0:P], qkt_s[r, i, :],
                       start=(i % 2 == 0), stop=True, skip_group_check=True)
                for i in range(4):
                    ins = mm(bank[3 * e + 2][:, P * i:P * (i + 1)], qkt_s[r, 4 + i, P:SEQ], qkt_s[r, i, P:SEQ],
                             start=(i == 0), stop=True, skip_group_check=True)
                ins.then_inc(z_done, 1)
            rows_group(V_M, 6)
            pe.wait_ge(group_out, 10)
            rows_group(V_S, 6)

            pe.wait_ge(group_out, 12)
            for r, (tt, first, n) in enumerate(((0, 0, 4), (1, 0, 2), (1, 4, 2))):
                if r:
                    pe.wait_ge(qk_biased, r)
                width = P * (tt + 1)
                for i in range(n):
                    for e in range(2):
                        hh = first + 2 * i + e
                        rows = slice(HD * e, HD * (e + 1))
                        ins = mm(bank[6 + e][:, width * i:width * (i + 1)], qkt_m[rows, hh // 2, P * tt:P * (tt + 1)],
                                 qkt_m[rows, 4 + hh // 2, 0:width], start=True, stop=True)
                ins.then_inc(qk_done, 1)
            for e in range(2):
                pe.wait_ge(sp_masked, e + 1)
                lower, upper = sb_sp[:, e, 0:1024], sb_sp[:, e, 1024:1536]
                for b in range(2):
                    mm(bank[3 * e + b][:, :], neg_tri, lower[:, 512 * b:512 * (b + 1)], start=False, stop=False,
                       skip_group_check=True)
                    mm(bank[3 * e + b][:, :].rearrange("p (i t) -> p i t", i=2)[:, :, P:SEQ], neg_ones,
                       upper[:, 256 * b:256 * (b + 1)].rearrange("p (i t) -> p i t", i=2), start=False, stop=True,
                       skip_group_check=True)
                mm(bank[3 * e + 2][:, :], neg_tri, upper, start=False, stop=True,
                   skip_group_check=True).then_inc(cum_done, 1)

            pe.wait_ge(w_exp, 6)
            pe.wait_ge(s_exp, 1)
            for hh in range(NH):
                ins = nc.tensor.transpose(bank[hh // 4][:, P * (hh % 4):P * (hh % 4 + 1)], s0[:, hh, :], ident)
                if hh % 4 == 3:
                    ins.then_inc(pt_done, 1)
            pe.wait_ge(s_exp, 2)
            for hh in range(NH):
                for ss in range(2):
                    c = 256 * (hh % 2) + P * ss
                    ins = nc.tensor.transpose(bank[2 + hh // 2][:, c:c + P], s1[:, hh, P * ss:P * (ss + 1)], ident)
                if hh % 2:
                    ins.then_inc(pt_done, 1)
            pe.wait_ge(qk_biased, 3)
            pe.wait_ge(pt_out, 2)
            for hh in range(NH):
                ins = mm(bank[6][:, HD * hh:HD * (hh + 1)], probs_t[:, hh // 4, P * (hh % 4):P * (hh % 4 + 1)],
                         v_all[:, 0, HD * hh:HD * (hh + 1)], start=True, stop=True)
            ins.then_inc(pv_done, 1)
            for hh in range(NH):
                if hh % 2 == 0:
                    pe.wait_ge(pt_out, 3 + hh // 2)
                place = (2 + hh // 2) % 4
                for ss in range(2):
                    c = 256 * (hh % 2) + P * ss
                    ins = mm(bank[7][:, HD * hh:HD * (hh + 1)], probs_t[:, place, c:c + P],
                             v_all[:, ss, HD * hh:HD * (hh + 1)], start=(ss == 0), stop=(ss == 1))
            ins.then_inc(pv_done, 1)
            pe.wait_ge(w_masked, 2)
            for tt in range(TT):
                for hh in range(NH):
                    e, i = hh % 2, hh // 2
                    cols = slice(512 + HD * hh, 512 + HD * (hh + 1))
                    dst = bank[tt][:, HD * hh:HD * (hh + 1)]
                    c = 256 * i + P * tt
                    ins = mm(dst, sb_w[:, e, c:c + P], v_all[:, 0, cols], start=True, stop=(tt == 0))
                    if tt:
                        ins = mm(dst, sb_w[:, e, 1024 + P * i:1024 + P * (i + 1)], v_all[:, 1, cols], start=False,
                                 stop=True)
                ins.then_inc(spv_done, 1)

            transposes(1)
            pe.wait_ge(pv_out, 2)
            pe.wait_ge(xt_lo_ready, 8)
            rows_group(OUT0, 4)
            rows_group(OUT0 + 1, 6)

            transposes(2)
            pe.wait_ge(xt_lo_ready, 12)
            for n in range(4):
                if n == 0:
                    pe.wait_ge(h1_ready, 4)
                if n >= 2:
                    pe.wait_ge(query_ready, 2 * (n - 1))
                columns_group(QUERY0 + n, 4 + 2 * (n % 2))
            pe.wait_ge(sk_loaded, 16)
            pe.wait_ge(query_ready, 8)
            for u in range(8):
                tt, g0 = u // 4, 4 * (u % 4)
                b = [0, 1, 2, 3, 6, 7, 0, 1][u]
                if u >= 6:
                    pe.wait_ge(s_out, u - 5)
                t = slice(P * tt, P * (tt + 1))
                for q in range(4):
                    g = g0 + q
                    ins = mm(bank[b][:, P * q:P * (q + 1)], query[:, g, t], sk[:, g % 2, :], start=True, stop=True)
                ins.then_inc(s_done, 1)

            def hidden(q):
                three(bank[4 + q][:, 0:SEQ], [((t_hi[:, q, P * c:P * (c + 1)], t_lo[:, q, P * c:P * (c + 1)]),
                                               (xt_hi[:, c, :], xt_lo[:, c, :])) for c in range(DC)]
                      ).then_inc(hid_done, 1)

            for q in range(RING):
                pe.wait_ge(*u_lo(q, 0))
                if q >= 2:
                    pe.wait_ge(s_out, 3 + q)
                hidden(q)

            def u_steps(first, last):
                with pe.Fori(first // RING, last // RING) as i:
                    for q in range(RING):
                        pe.wait_ge(*u_lo(q, i))
                        pe.wait_ge(gelu_done, RING * i + q - RING + 1)
                        hidden(q)

            u_steps(RING, PICKS_AT)
            pe.wait_ge(hit_used, 2 * TT)
            for q in range(2):
                for tt in range(TT):
                    ins = nc.tensor.transpose(bank[q][:, P * tt:P * (tt + 1)], pick[:, tt, q, :], ident)
                ins.then_inc(pick_t_done, 1)
            pe.wait_ge(picks_ready, 1)
            for tt in range(TT):
                ins = nc.tensor.transpose(bank[2][:, P * tt:P * (tt + 1)],
                                          gate[:, tt, :, :].rearrange("p a b -> p (a b)"), ident)
            ins.then_inc(pick_t_done, 1)
            u_steps(PICKS_AT, FIRST)

            def gates(k, b, count):
                pe.wait_ge(hot_i_ready, count)
                pe.wait_ge(hot_j_ready, count)
                for q in range(4):
                    ins = mm(bank[b][:, P * q:P * (q + 1)], hot_i[:, k, q, :], hot_j[:, k, q, :], start=True,
                             stop=True)
                ins.then_inc(gates_done, 1)

            def late_step(q, i, first=False):
                n = RING * i + q
                s = n - FIRST
                pe.wait_ge(*u_lo(q, i))
                pe.wait_ge(gelu_done, n - RING + 1)
                hidden(q)
                if not first:
                    pe.wait_ge(gated, s - RING + 1)
                gates(q % 2, q, s + 1)

            for q in range(RING):
                late_step(q, FIRST // RING, True)
            with pe.Fori(FIRST // RING + 1, N_KEYS // RING) as i:
                for q in range(RING):
                    late_step(q, i)

            def expert_sum(q, i, first=False):
                if first and q < LEAD:
                    pe.wait_ge(*u_lo(q, N_KEYS // RING))
                else:
                    pe.wait_ge(t_lo_ready, v_lo + RING * i + q + 1)
                pe.wait_ge(g_lo_ready, RING * i + q + 1)
                for tt in range(TT):
                    t = slice(P * tt, P * (tt + 1))
                    for w in range(2):
                        d = slice(512 * w, 512 * (w + 1))
                        dst = bank[2 * tt + w][:, :]
                        mm(dst, g_hi[:, q % 2, t], t_hi[:, q, d], start=first and q == 0, stop=False,
                           skip_group_check=True)
                        mm(dst, g_hi[:, q % 2, t], t_lo[:, q, d], start=False, stop=False, skip_group_check=True)
                        ins = mm(dst, g_lo[:, q % 2, t], t_hi[:, q, d], start=False, stop=True,
                                 skip_group_check=True)
                ins.then_inc(v_used, 1)

            for q in range(RING):
                expert_sum(q, 0, True)
            with pe.Fori(1, N_KEYS // RING) as i:
                for q in range(RING):
                    expert_sum(q, i)

            pe.wait_ge(ple_lo, 2)
            for u in range(4):
                tt, q = u // 2, u % 2
                t, d = slice(P * tt, P * (tt + 1)), slice(512 * q, 512 * (q + 1))
                three(bank[4 + u][:, :], [((pt_hi[:, c, t], pt_lo[:, c, t]), (wp_hi[:, c, d], wp_lo[:, c, d]))
                                          for c in range(PLE // P)]).then_inc(ple_done, 1)
            pe.wait_ge(h2_ready, 4)
            transposes(3, xs_end)
            pe.wait_ge(xt_lo_ready, 16)
            pe.wait_ge(wg_lo_ready, DC)
            for u in range(4):
                tt, q = u // 2, u % 2
                t, d = slice(P * tt, P * (tt + 1)), slice(512 * q, 512 * (q + 1))
                three(bank[u][:, :], [((xt_hi[:, c, t], xt_lo[:, c, t]), (wg_hi[:, c, d], wg_lo[:, c, d]))
                                      for c in range(DC)]).then_inc(gate_done, 1)


def bucket_table():
    dist = 255 - np.arange(TAB)
    n = np.maximum(dist, 0)
    exact = REL // 2
    large = exact + (np.log(np.maximum(n, 1) / exact) / np.log(128 / exact) * (REL - exact)).astype(np.int64)
    bucket = np.where(n < exact, n, np.minimum(large, REL - 1))
    bucket = np.where(dist < 0, REL, bucket)
    return (np.arange(REL + 1)[:, None] == bucket[None, :]).astype(np.float32)


def constants():
    i = np.arange(P)
    tri = np.where(i[:, None] >= i[None, :], -1.0 / SCALE, 0.0)
    return np.ascontiguousarray(np.stack(
        [np.eye(P), tri, np.full((P, P), -1.0 / SCALE), np.broadcast_to(i, (P, P)),
         np.eye(P)[::-1]], axis=1).astype(np.float32))


def by_group(w, width=GW):
    k, n = w.shape
    return np.ascontiguousarray(w.reshape(k // P, P, n // width, width).transpose(2, 1, 0, 3))


def kernel(**inputs):
    import concourse.bacc as bacc
    from concourse.bass_utils import run_bass_kernel_spmd

    a = {k: np.asarray(v) for k, v in inputs.items()}
    w_in = by_group(a["w_in"][0])[[0, 1, 3, 4, 2, 5]]
    column = lambda g: g.reshape(DC, P).T
    arrays = {
        "x": a["x"].reshape(SEQ, D),
        "p_t": a["p"].reshape(SEQ, PLE // P, P).transpose(2, 1, 0),
        "rel_bias": a["rel_bias"],
        "bucket_onehot": bucket_table(),
        "consts": constants(),
        "gains": np.stack([column(a["attn_norm"][0]),
                           column(np.concatenate([a["out_norm_moba"][0], a["out_norm_sb"][0]])),
                           column(a["ffn_norm"][0]), column(a["ple_norm"][0])], axis=1),
        "qk_gain": np.stack([np.tile(a["q_norm"][0], 2), np.tile(a["k_norm"][0], 2)], axis=1),
        "w_in": w_in,
        "w_out": by_group(a["w_out"][0]),
        "w_query": by_group(a["peer_query"][0].reshape(D, PG * P)),
        "subkeys_t": a["peer_sub_keys"][0].transpose(2, 0, 1),
        "u_chunks": a["peer_u"][0].reshape(N_KEYS, N_KEYS, DC, P).transpose(1, 3, 2, 0).reshape(N_KEYS, P, D),
        "v_chunks": a["peer_v"][0].reshape(N_KEYS, N_KEYS, D).transpose(1, 0, 2),
        "w_gate": a["w_ple_gate"][0].reshape(DC, P, D).transpose(1, 0, 2),
        "w_ple": a["w_ple"][0].reshape(PLE // P, P, D).transpose(1, 0, 2),
    }
    arrays = {k: np.ascontiguousarray(v) for k, v in arrays.items()}
    nc = bacc.Bacc("TRN2", target_bir_lowering=False, num_devices=1)
    args = [nc.dram_tensor(k, v.shape, mybir.dt.from_np(v.dtype), kind="ExternalInput").ap() for k, v in arrays.items()]
    out = nc.dram_tensor("out", (SEQ, D), mybir.dt.float32, kind="ExternalOutput").ap()
    layer_program(nc, *args, out)
    r = run_bass_kernel_spmd(nc, [arrays], core_ids=[0])
    return r.results[0]["out"].reshape(1, SEQ, D)
```

```python
from contextlib import ExitStack

import numpy as np
import concourse.bass as bass
from concourse import mybir

P = 128
SEQ = 256
D = 1024
DC = D // P
TT = SEQ // P
HD = 64
NH = 8
REL = 32
N_KEYS = 128
TOPK = 16
PH = 8
PG = 2 * PH
PLE = 256
EPS = 1e-6
SCALE = HD ** -0.5
GW = 512
RING = 4
LEAD = 2
FIRST = 64
ONES_AT = 44
ONES = 4
TOPK_END = 52
EXP_AT = 52
PICKS_AT = 56
BLOCKS = ((0, 1, 16), (1, 3, 8), (4, 4, 4), (8, 8, 1))
PAIRS = sum(n * m for _, n, m in BLOCKS)
assert all(b < m for a0, n, m in BLOCKS for a in range(a0, a0 + n) for b in range(16 // (a + 1)))
SETS = SEQ // 4
assert SETS == N_KEYS - FIRST
END_PARTS = ((0, 0, 512, 0), (0, 512, 512, 1), (1, 0, 512, 2), (1, 512, 256, 3), (1, 768, 256, 0))
SCORE_BANKS = (4, 5, 6, 7, 0, 1, 2, 3)
TAB = 384

Q_M, K_M, Q_S, K_S, V_M, V_S = range(6)
OUT0, QUERY0, N_GROUPS = 6, 8, 12


def layer_program(nc, x, p_t, rel_bias, bucket_onehot, consts, gains, qk_gain, w_in, w_out, w_query,
                  subkeys_t, u_chunks, v_chunks, w_gate, w_ple, out):
    f32, f32r, u32 = mybir.dt.float32, mybir.dt.float32r, mybir.dt.uint32
    ALU, ACT, AX = mybir.AluOpType, mybir.ActivationFunctionType, mybir.AxisListType

    ctx = ExitStack()
    with ctx:
        base = (nc.sbuf_base + 63) // 64 * 64
        sizes = dict(h=2 * D, xt_hi=DC * SEQ, xt_lo=DC * SEQ, cst=5 * P, gains=4 * DC, qkg=32, stats=192)
        at, where = base, {}
        for name, n in sizes.items():
            where[name] = at
            at += 4 * n
        ZONE = at
        BIG = ZONE + 4 * 13312
        assert BIG + 4 * P * SEQ <= nc.sbuf_usable_end

        def tile(name, shape, offset, dt=f32):
            return nc.alloc_sbuf_tensor_at(name, shape, dt, offset=offset)

        h = tile("h", [P, TT, D], where["h"])
        xt_hi = tile("xt_hi", [P, DC, SEQ], where["xt_hi"], f32r)
        xt_lo = tile("xt_lo", [P, DC, SEQ], where["xt_lo"], f32r)
        cst = tile("cst", [P, 5, P], where["cst"])
        gain = tile("gain", [P, 4, DC], where["gains"])
        qkg = tile("qkg", [P, 2], where["qkg"])
        stats = tile("stats", [P, 192], where["stats"])
        ident, neg_tri, neg_ones, iota = cst[:, 0, :], cst[:, 1, :], cst[:, 2, :], cst[:, 3, :]
        flip = cst[:, 4, :]

        w_raw = tile("w_raw", [P, 2, DC, GW], BIG)
        w_hi = tile("w_hi", [P, 2, DC, GW], BIG + 4 * 8192, f32r)
        w_lo = tile("w_lo", [P, 2, DC, GW], BIG + 4 * 16384, f32r)
        UP = BIG + 4 * 24576
        bias = tile("bias", [P, NH, SEQ], UP)
        skew = tile("skew", [P, NH, SEQ], UP + 4 * 6144)
        v_all = tile("v_all", [P, TT, 2 * NH * HD], UP + 4 * 2048)
        qk_nat = tile("qk_nat", [P, TT, 2 * NH, HD], UP + 4 * 4096)
        o_nat = tile("o_nat", [P, TT, D], UP + 4 * 4096)
        qkt_s = tile("qkt_s", [P, 8, SEQ], UP + 4 * 6144)
        query = tile("query", [P, PG, SEQ], UP)
        slots = tile("slots", [P, N_KEYS, SEQ], BIG)
        scores = tile("scores", [P, TT, PG, N_KEYS], BIG + 4 * 20480)
        o = UP
        top_v = tile("top_v", [P, TT, PG, TOPK], o); o += 4 * 512
        top_i = tile("top_i", [P, TT, PG, TOPK], o, u32); o += 4 * 512
        top_f = tile("top_f", [P, TT, PG, TOPK], o); o += 4 * 512
        rest = tile("rest", [P, 2, 256], o); o += 4 * 512
        cand = tile("cand", [P, PH, PAIRS], o); o += 4 * PH * PAIRS
        best_v = tile("best_v", [P, TT, PH, TOPK], o); o += 4 * 256
        pos_u = tile("pos_u", [P, 3, PH * TOPK], o, u32); o += 4 * 384
        pos_f = tile("pos_f", [P, 3, PH * TOPK], o); o += 4 * 384
        pos_m = tile("pos_m", [P, 4, PH * TOPK], o); o += 4 * 512
        pos_ab = tile("pos_ab", [P, 2, PH * TOPK], o); o += 4 * 256
        assert o <= BIG + 4 * P * SEQ
        wg_raw = tile("wg_raw", [P, DC, D], BIG)
        wg_lo = tile("wg_lo", [P, DC, D], BIG, f32r)
        wg_hi = tile("wg_hi", [P, DC, D], BIG + 4 * 8192, f32r)
        wp_raw = tile("wp_raw", [P, 2, D], BIG + 4 * 16384)
        wp_lo = tile("wp_lo", [P, 2, D], BIG + 4 * 16384, f32r)
        wp_hi = tile("wp_hi", [P, 2, D], BIG + 4 * 18432, f32r)
        pt_raw = tile("pt_raw", [P, 2, SEQ], BIG + 4 * 20480)
        pt_lo = tile("pt_lo", [P, 2, SEQ], BIG + 4 * 20480, f32r)
        pt_hi = tile("pt_hi", [P, 2, SEQ], BIG + 4 * 20992, f32r)
        xs_end = tile("xs_end", [P, TT, D], BIG + 4 * 21504)
        sig = tile("sig", [P, TT, D], BIG + 4 * 24576)

        s0 = tile("s0", [P, NH, P], ZONE)
        s1 = tile("s1", [P, NH, SEQ], ZONE + 4 * 1024)
        square = tile("square", [P, 2 * NH, HD], ZONE)
        probs_t = tile("probs_t", [P, 4, 512], ZONE + 4 * 3072)
        sb_sp = tile("sb_sp", [P, 2, 1536], ZONE + 4 * 5120)
        sb_w = tile("sb_w", [P, 2, 1536], ZONE + 4 * 8192)
        qkt_m = tile("qkt_m", [P, 8, SEQ], ZONE + 4 * 11264)
        xs = tile("xs", [P, TT, D], ZONE + 4 * 5120)
        tab_in = tile("tab_in", [REL + 1, TAB + NH], ZONE + 4 * 8192)
        tab_out = tile("tab_out", [NH, TAB], ZONE + 4 * 9216)
        t_raw = tile("t_raw", [P, RING, D], ZONE)
        t_lo = tile("t_lo", [P, RING, D], ZONE, f32r)
        hit = tile("hit", [P, PH, TOPK, TOPK], ZONE + 4 * 4096)
        hot_i = tile("hot_i", [P, 2, 4, P], ZONE + 4 * 4096)
        hot_j = tile("hot_j", [P, 2, 4, P], ZONE + 4 * 5120)
        g_hi = tile("g_hi", [P, 2, SEQ], ZONE + 4 * 6144, f32r)
        g_lo = tile("g_lo", [P, 2, SEQ], ZONE + 4 * 6656, f32r)
        t_hi = tile("t_hi", [P, RING, D], ZONE + 4 * 7168, f32r)
        o = ZONE + 4 * 11264
        pick_t = tile("pick_t", [P, 3, SEQ], o); o += 4 * 768
        sk = tile("sk", [P, 2, N_KEYS], o); o += 4 * 256
        pick = tile("pick", [P, TT, 2, P], o); o += 4 * 512
        gate = tile("gate", [P, TT, PH, TOPK], o); o += 4 * 256
        assert o <= BIG

        bank = [ctx.enter_context(nc.psum_tensor(f"bank{b}", [P, 512], f32)) for b in range(8)]
        table = nc.dram_tensor("bias_table", (NH, TAB), f32, kind="Internal")

        def xt_half(k, c):
            return half(c // 2 + (4 if k == 2 else 0), c % 2)

        def end_t(tt, c):
            return bank[2 * tt + c // 4][:, P * (c % 4):P * (c % 4 + 1)]

        def out_bank(g, part, tt):
            return [4, 6, 0, 2][2 * g + part] + tt

        def half(b, j):
            return bank[b][:, 256 * j:256 * (j + 1)]

        def sem(name):
            return ctx.enter_context(nc.semaphore(name))

        small_loaded, tab_loaded = sem("small_loaded"), sem("tab_loaded")
        x_loaded = [sem(f"x_loaded{tt}") for tt in range(TT)]
        tab_made, tab_copied = sem("tab_made"), sem("tab_copied")
        tab_stored, bias_loaded = sem("tab_stored"), sem("bias_loaded")
        flip_done, bias_ready = sem("flip_done"), sem("bias_ready")
        w_loaded = [sem("w_loaded0"), sem("w_loaded1")]
        w_hi_ready, w_lo_ready, w_used = sem("w_hi_ready"), sem("w_lo_ready"), sem("w_used")
        quarter_loaded = [sem(f"quarter_loaded{b}") for b in range(8)]
        quarter_hi, quarter_lo = sem("quarter_hi"), sem("quarter_lo")
        w8_hi_ready, w8_lo_ready = sem("w8_hi_ready"), sem("w8_lo_ready")
        v_tile_done, v_out = sem("v_tile_done"), sem("v_out")
        out_done = sem("out_done")
        squares_done, mean_ready, root_ready = sem("squares_done"), sem("mean_ready"), sem("root_ready")
        xs_ready, xt_done, xt_hi_ready, xt_lo_ready = (sem("xs_ready"), sem("xt_done"), sem("xt_hi_ready"),
                                                       sem("xt_lo_ready"))
        group_out = sem("group_out")
        qk_mean, qk_root, qk_normed = sem("qk_mean"), sem("qk_root"), sem("qk_normed")
        qkt_done, qkt_out = sem("qkt_done"), sem("qkt_out")
        z_done, z_softplus, sp_added, sp_masked = sem("z_done"), sem("z_softplus"), sem("sp_added"), sem("sp_masked")
        cum_done, w_exp, w_masked = sem("cum_done"), sem("w_exp"), sem("w_masked")
        qk_done, qk_biased, s_shifted, s_exp = sem("qk_done"), sem("qk_biased"), sem("s_shifted"), sem("s_exp")
        pt_done, pt_out, pv_done, pv_out = sem("pt_done"), sem("pt_out"), sem("pv_done"), sem("pv_out")
        spv_done, spv_out = sem("spv_done"), sem("spv_out")
        h1_ready, query_ready, sk_loaded = sem("h1_ready"), sem("query_ready"), sem("sk_loaded")
        s_done, s_out = sem("s_done"), sem("s_out")
        t_loaded = [sem(f"t_loaded{q}") for q in range(RING)]
        t_hi_ready, t_lo_ready, t_lo_pool = sem("t_hi_ready"), sem("t_lo_ready"), sem("t_lo_pool")
        halves_done, ones_ready, late_used = sem("halves_done"), sem("ones_ready"), sem("late_used")
        table_row = sem("table_row")
        hid_done, gelu_done = sem("hid_done"), sem("gelu_done")
        hit_used = sem("hit_used")
        gate_shifted, gate_exp, picks_ready = sem("gate_shifted"), sem("gate_exp"), sem("picks_ready")
        pick_t_done, pick_t_out = sem("pick_t_done"), sem("pick_t_out")
        hot_i_diff, hot_i_square = sem("hot_i_diff"), sem("hot_i_square")
        hot_i_ready, hot_j_ready, gates_done, gated = (sem("hot_i_ready"), sem("hot_j_ready"), sem("gates_done"),
                                                       sem("gated"))
        g_hi_first, g_lo_first = sem("g_hi_first"), sem("g_lo_first")
        v_tile0_done = sem("v_tile0_done")
        g_hi_ready, g_lo_ready, v_used = sem("g_hi_ready"), sem("g_lo_ready"), sem("v_used")
        wg_loaded, wp_loaded = sem("wg_loaded"), sem("wp_loaded")
        wg_hi_ready, wg_lo_ready = sem("wg_hi_ready"), sem("wg_lo_ready")
        ple_hi, ple_lo = sem("ple_hi"), sem("ple_lo")
        h2_ready, gate_done, sig_ready, y_ready, stored = (
            sem("h2_ready"), sem("gate_done"), sem("sig_ready"), sem("y_ready"), sem("stored"))
        end_t_done, end_hi_ready, end_lo_ready, end_rstd_ready = (sem("end_t_done"), sem("end_hi_ready"),
                                                                  sem("end_lo_ready"), sem("end_rstd_ready"))
        act_step, dve_step = sem("act_step"), sem("dve_step")

        block = ctx.enter_context(nc.Block())

        def u_lo(q, i):
            return (t_lo_pool, (RING - 1) * i + q) if q else (t_lo_ready, i + 1)

        v_lo = N_KEYS // RING + 1 - LEAD

        def used(n):
            if n < OUT0:
                return w_used, n + 1
            return (out_done, 4 * (n - OUT0 + 1)) if n < QUERY0 else (w_used, n + 1 - (QUERY0 - OUT0))

        def split_count(n):
            return n - 1 - (n > QUERY0)

        def split(n):
            pieces = {0: (quarter_lo, 4), 1: (quarter_lo, 8), QUERY0: (w8_lo_ready, 2)}
            return pieces.get(n, (w_lo_ready, split_count(n)))

        def w_source(n):
            if n < OUT0:
                return w_in[n]
            return w_out[n - OUT0] if n < QUERY0 else w_query[n - QUERY0]

        QSS, QRSTD = stats[:, 8:40], stats[:, 40:72]
        MX0, MX1, SUM = stats[:, 72:80], stats[:, 80:88], stats[:, 88:104]
        GSUM = stats[:, 104:120]

        def norm_stats(k):
            return [stats[:, 120 + 12 * k + 4 * q:124 + 12 * k + 4 * q] for q in range(3)]

        @block.sync
        def _(sp):
            for tt in range(TT):
                sp.dma_start(h[:, tt, :], x[tt * P:(tt + 1) * P, :]).then_inc(x_loaded[tt], 16)
            sp.dma_start(cst[:, :, :], consts).then_inc(small_loaded, 16)
            sp.dma_start(gain[:, :, :], gains).then_inc(small_loaded, 16)
            sp.dma_start(qkg[:, :], qk_gain).then_inc(small_loaded, 16)
            for n in range(2):
                for b in range(4):
                    sp.dma_start(w_raw[:, n, 2 * b:2 * b + 2, :], w_in[n, :, 2 * b:2 * b + 2, :]
                                 ).then_inc(quarter_loaded[4 * n + b], 16)
            sp.dma_start(tab_in[:, 0:TAB], bucket_onehot).then_inc(tab_loaded, 16)
            sp.dma_start(tab_in[0:REL, TAB:TAB + NH], rel_bias).then_inc(tab_loaded, 16)

            def load_group(n):
                if n >= 2:
                    sp.wait_ge(*split(n - 2))
                sp.dma_start(w_raw[:, n % 2, :, :], w_source(n)).then_inc(w_loaded[n % 2], 16)

            load_group(2)
            sp.wait_ge(tab_copied, 1)
            sp.dma_start(table.ap(), tab_out[:, :]).then_inc(tab_stored, 16)
            sp.wait_ge(tab_stored, 16)
            sp.dma_start(skew[:, :, :], bass.AP(table, 0, [[1, P], [TAB, NH], [1, SEQ]])).then_inc(bias_loaded, 16)
            for n in range(3, N_GROUPS):
                load_group(n)
                if n == 9:
                    sp.wait_ge(spv_out, 2)
                    sp.wait_ge(pv_out, 2)
                    sp.dma_start(sk[:, :, :], subkeys_t).then_inc(sk_loaded, 16)
                    for q in range(RING):
                        sp.dma_start(t_raw[:, q, :], u_chunks[q]).then_inc(t_loaded[q], 16)

            def load_chunk(table, q, n):
                sp.dma_start(t_raw[:, q, :], table[bass.ds(n, 1)].rearrange("o p f -> (o p) f")
                             ).then_inc(t_loaded[q], 16)

            with sp.Fori(1, N_KEYS // RING) as i:
                for q in range(RING):
                    sp.wait_ge(hid_done, RING * i + q - RING + 1)
                    load_chunk(u_chunks, q, RING * i + q)
            for q in range(RING):
                sp.wait_ge(hid_done, N_KEYS - RING + q + 1)
                load_chunk(v_chunks, q, q)

            def v_loads(first, last, gate_weights):
                with sp.Fori(first, last) as i:
                    if gate_weights:
                        sp.dma_start(wg_raw[:, bass.ds(i - first, 1), :].rearrange("p o n -> p (o n)"),
                                     w_gate[:, bass.ds(i - first, 1), :].rearrange("p o n -> p (o n)")
                                     ).then_inc(wg_loaded, 16)
                    for q in range(RING):
                        sp.wait_ge(v_used, RING * i + q - RING + 1)
                        load_chunk(v_chunks, q, RING * i + q)

            v_loads(1, 12, False)
            sp.wait_ge(g_lo_ready, 32)
            v_loads(12, 20, True)
            sp.wait_ge(g_lo_ready, 72)
            for k in range(2):
                sp.dma_start(wp_raw[:, k, :], w_ple[:, k, :]).then_inc(wp_loaded, 16)
                v_loads(20 + k, 21 + k, False)
            sp.wait_ge(g_lo_ready, 82)
            sp.dma_start(pt_raw[:, :, :], p_t).then_inc(wp_loaded, 16)
            v_loads(22, N_KEYS // RING, False)
            for u, (tt, d0, width, b) in enumerate(END_PARTS):
                sp.wait_ge(y_ready, u + 1)
                sp.dma_start(out[tt * P:(tt + 1) * P, d0:d0 + width], h[:, tt, d0:d0 + width]).then_inc(stored, 16)
            sp.wait_ge(stored, 16 * len(END_PARTS))

        @block.scalar
        def _(act):
            steps = [0]

            def link(ins):
                steps[0] += 1
                ins.then_inc(act_step, 1)
                act.wait_ge(act_step, steps[0])

            def split_group(n):
                act.wait_ge(w_loaded[n % 2], 16 * (n // 2))
                if n >= 2:
                    act.wait_ge(*used(n - 2))
                nc.scalar.activation(w_hi[:, n % 2, :, :], w_raw[:, n % 2, :, :], ACT.Copy).then_inc(w_hi_ready, 1)

            def squares(k, c, tt, src, dump):
                ss = norm_stats(k)[0]
                nc.scalar.activation(dump, src, ACT.Square, accum_out=ss[:, c:c + 1]).then_inc(squares_done, 1)

            def root(k, first, last):
                _, ms, rstd = norm_stats(k)
                nc.scalar.activation(rstd[:, first:last], ms[:, first:last], ACT.Sqrt).then_inc(root_ready, 1)

            def transposed_hi(k, b, nth):
                act.wait_ge(xt_done, 4 * k + nth + 1)
                for c in (2 * b, 2 * b + 1):
                    ins = nc.scalar.activation(xt_hi[:, c, :], xt_half(k, c), ACT.Copy, scale=gain[:, k, c:c + 1])
                ins.then_inc(xt_hi_ready, 1)

            def out_of_psum(n):
                act.wait_ge(*used(n))
                b = 4 if n in (Q_M, Q_S) else 6
                for q in range(2):
                    if n in (Q_M, K_M):
                        dst = qk_nat[:, q, NH * n:NH * (n + 1), :].rearrange("p a b -> p (a b)")
                    else:
                        g = 4 * (n - Q_S) + 2 * q
                        dst = qkt_s[:, g:g + 2, :].rearrange("p a b -> p (a b)")
                    nc.scalar.copy(dst, bank[b + q][:, :]).then_inc(group_out, 1)

            nc.scalar.preload_act_table(ACT.Sqrt)
            for tt in range(TT):
                act.wait_ge(x_loaded[tt], 16)
                squares(0, tt, tt, h[:, tt, :], xs[:, tt, :])
                act.wait_ge(mean_ready, tt + 1)
                root(0, tt, tt + 1)
            act.wait_ge(small_loaded, 48)
            for n in range(2):
                for b in range(4):
                    act.wait_ge(quarter_loaded[4 * n + b], 16)
                    nc.scalar.activation(w_hi[:, n, 2 * b:2 * b + 2, :], w_raw[:, n, 2 * b:2 * b + 2, :],
                                         ACT.Copy).then_inc(quarter_hi, 1)
                    if n == 0:
                        transposed_hi(0, b, b)
            act.wait_ge(tab_made, 1)
            nc.scalar.copy(tab_out[:, :], bank[7][0:NH, 0:TAB]).then_inc(tab_copied, 1)
            out_of_psum(Q_M)
            split_group(2)
            out_of_psum(K_M)
            for b in range(4):
                act.wait_ge(flip_done, b + 1)
                nc.scalar.copy(bias[:, 2 * b:2 * b + 2, :].rearrange("p a b -> p (a b)"), bank[b][:, :]).then_inc(
                    bias_ready, 1)
            split_group(3)
            act.wait_ge(qk_mean, 1)
            nc.scalar.activation(QRSTD, QSS, ACT.Sqrt).then_inc(qk_root, 1)
            out_of_psum(Q_S)
            for b in range(4):
                act.wait_ge(qkt_done, b + 1)
                nc.scalar.activation(qkt_m[:, 2 * b:2 * b + 2, :].rearrange("p a b -> p (a b)"), bank[b][:, :],
                                     ACT.Copy, scale=qkg[:, b // 2:b // 2 + 1]).then_inc(qkt_out, 1)
            split_group(4)
            out_of_psum(K_S)
            split_group(5)
            for e in range(2):
                act.wait_ge(z_done, e + 1)
                for b in range(3):
                    src = bank[3 * e + b][:, :]
                    nc.scalar.activation(sb_w[:, e, 512 * b:512 * (b + 1)], src, ACT.Relu, scale=SCALE)
                    ins = nc.scalar.activation(sb_sp[:, e, 512 * b:512 * (b + 1)], src, ACT.Abs, scale=SCALE)
                link(ins)
            nc.scalar.activation(sb_sp[:, 0, :], sb_sp[:, 0, :], ACT.Exp, scale=-1.0)
            link(nc.scalar.activation(sb_sp[:, 1, :], sb_sp[:, 1, :], ACT.Exp, scale=-1.0))
            for e in range(2):
                nc.scalar.activation(sb_sp[:, e, :], sb_sp[:, e, :], ACT.Ln, bias=1.0).then_inc(z_softplus, 1)
            nc.scalar.preload_act_table(ACT.Exp)
            split_group(6)
            split_group(7)
            for e in range(2):
                act.wait_ge(cum_done, e + 1)
                for b in range(3):
                    nc.scalar.activation(sb_w[:, e, 512 * b:512 * (b + 1)], bank[3 * e + b][:, :], ACT.Exp,
                                         scale=SCALE).then_inc(w_exp, 1)
            act.wait_ge(s_shifted, 1)
            nc.scalar.activation(s0[:, :, :], s0[:, :, :], ACT.Exp).then_inc(s_exp, 1)

            def weights_out(b):
                act.wait_ge(pt_done, b + 1)
                if b >= 4:
                    act.wait_ge(pv_done, 1)
                nc.scalar.copy(probs_t[:, b % 4, :], bank[b][:, :]).then_inc(pt_out, 1)

            for k in range(2):
                act.wait_ge(s_shifted, 2 + k)
                nc.scalar.activation(s1[:, 4 * k:4 * k + 4, :], s1[:, 4 * k:4 * k + 4, :], ACT.Exp).then_inc(s_exp, 1)
                if k == 0:
                    weights_out(0)
                    weights_out(1)
            for tt in range(TT):
                act.wait_ge(spv_done, tt + 1)
                nc.scalar.copy(o_nat[:, tt, 512:1024], bank[6 + tt][:, :]).then_inc(spv_out, 1)
            for b in range(2, 6):
                weights_out(b)
            nc.scalar.preload_act_table(ACT.Sqrt)
            for nth, b in enumerate((2, 3, 0, 1)):
                if nth == 2:
                    act.wait_ge(spv_out, 2)
                    for tt in range(TT):
                        squares(1, 2 + tt, tt, o_nat[:, tt, 512:1024], xs[:, tt, 512:1024])
                transposed_hi(1, b, nth)
            for tt in range(TT):
                act.wait_ge(pv_out, tt + 1)
                squares(1, tt, tt, o_nat[:, tt, 0:512], xs[:, tt, 0:512])
            act.wait_ge(mean_ready, 3)
            root(1, 0, 4)
            act.wait_ge(w_loaded[0], 16 * 4)
            act.wait_ge(*used(OUT0))
            for k in range(2):
                nc.scalar.activation(w_hi[:, 0, 4 * k:4 * k + 4, :], w_raw[:, 0, 4 * k:4 * k + 4, :],
                                     ACT.Copy).then_inc(w8_hi_ready, 1)
            for tt in range(TT):
                if tt == 0:
                    act.wait_ge(h1_ready, 2)
                    for k in range(TT):
                        squares(2, k, k, h[:, k, 0:512], xs[:, k, 0:512])
                act.wait_ge(h1_ready, 3 + tt)
                squares(2, 2 + tt, tt, h[:, tt, 512:1024], xs[:, tt, 512:1024])
                act.wait_ge(mean_ready, 4 + tt)
                root(2, tt, tt + 1)
            for b in range(4):
                transposed_hi(2, b, b)
            split_group(9)

            def query_part(n):
                act.wait_ge(*used(QUERY0 + n))
                for q in range(2):
                    g = 4 * n + 2 * q
                    nc.scalar.copy(query[:, g:g + 2, :].rearrange("p a b -> p (a b)"),
                                   bank[2 * (n % 2) + q][:, :]).then_inc(query_ready, 1)

            query_part(0)
            split_group(10)
            query_part(1)
            split_group(11)
            query_part(2)

            def table_hi(q, count):
                act.wait_ge(t_loaded[q % RING], 16 * count)
                nc.scalar.activation(t_hi[:, q % RING, :], t_raw[:, q % RING, :], ACT.Copy).then_inc(t_hi_ready, 1)

            query_part(3)
            for n in range(LEAD):
                table_hi(n, 1)
            for u in range(8):
                n, tt = u // 2, u % 2
                act.wait_ge(s_done, u + 1)
                nc.scalar.copy(scores[:, tt, 4 * n:4 * n + 4, :].rearrange("p a b -> p (a b)"),
                               bank[SCORE_BANKS[u]][:, :]).then_inc(s_out, 1)

            def u_steps(first, last):
                with act.Fori(first // RING, last // RING) as i:
                    for q in range(RING):
                        table_hi(q + LEAD, i + 1 + (q + LEAD) // RING)
                        act.wait_ge(hid_done, RING * i + q + 1)
                        nc.scalar.activation(slots[:, bass.ds(RING * i + q, 1), :].rearrange("p o t -> p (o t)"),
                                             bank[4 + q][:, 0:SEQ], ACT.Gelu).then_inc(gelu_done, 1)

            nc.scalar.preload_act_table(ACT.Gelu)
            def u_gelu(q, i):
                act.wait_ge(hid_done, RING * i + q + 1)
                nc.scalar.activation(slots[:, bass.ds(RING * i + q, 1), :].rearrange("p o t -> p (o t)"),
                                     bank[4 + q][:, 0:SEQ], ACT.Gelu).then_inc(gelu_done, 1)

            u_steps(0, EXP_AT)
            for q in range(RING):
                table_hi(q + LEAD, EXP_AT // RING + 1 + (q + LEAD) // RING)
                if q == 0:
                    act.wait_ge(gate_shifted, TT)
                    nc.scalar.activation(gate[:, :, :, :], gate[:, :, :, :], ACT.Exp).then_inc(gate_exp, 1)
                    nc.scalar.preload_act_table(ACT.Gelu)
                u_gelu(q, EXP_AT // RING)
            u_steps(EXP_AT + RING, FIRST - RING)

            def one_hots(k, count):
                act.wait_ge(hot_i_diff, count)
                nc.scalar.activation(hot_i[:, k, :, :], hot_i[:, k, :, :], ACT.Square).then_inc(hot_i_square, 1)
                act.wait_ge(hot_i_square, count)
                nc.scalar.activation(hot_i[:, k, :, :], hot_i[:, k, :, :], ACT.Relu, scale=-1.0,
                                     bias=1.0).then_inc(hot_i_ready, 1)

            for q in range(RING):
                table_hi(q + LEAD, FIRST // RING + (q + LEAD) // RING)
                u_gelu(q, FIRST // RING - 1)
                if q >= 2:
                    one_hots(q - 2, q - 1)

            def late_step(q, i, first=False):
                table_hi(q + LEAD, i + 1 + (q + LEAD) // RING)
                if not (first and q < 2):
                    one_hots(q % 2, RING * i + q - FIRST + 1)
                act.wait_ge(hid_done, RING * i + q + 1)
                nc.scalar.activation(half(4 + q, 1), half(4 + q, 0), ACT.Gelu).then_inc(gelu_done, 1)

            for q in range(RING):
                late_step(q, FIRST // RING, True)
            with act.Fori(FIRST // RING + 1, N_KEYS // RING) as i:
                for q in range(RING):
                    late_step(q, i)

            def gated_hi_of(tt, semaphore):
                t = slice(P * tt, P * (tt + 1))
                nc.scalar.activation(g_hi[:, 0, t], slots[:, 0, t], ACT.Copy).then_inc(semaphore, 1)

            def gated_hi(k, n):
                src = slots[:, bass.ds(n, 1), :].rearrange("p o t -> p (o t)")
                nc.scalar.activation(g_hi[:, k, :], src, ACT.Copy).then_inc(g_hi_ready, 1)

            act.wait_ge(gated, SETS // 2)
            gated_hi_of(0, g_hi_first)
            act.wait_ge(gated, SETS)
            gated_hi_of(1, g_hi_ready)
            act.wait_ge(late_used, N_KEYS - FIRST)

            def v_step(q, i, skip=(), first=False):
                if q + 1 not in skip:
                    if not first:
                        act.wait_ge(v_used, RING * i + q)
                    gated_hi((q + 1) % 2, RING * i + q + 1)
                if q + LEAD not in skip:
                    table_hi(q + LEAD, i + 1 + (q + LEAD) // RING + N_KEYS // RING)

            def gate_weights_hi(c):
                act.wait_ge(wg_loaded, 16 * DC)
                at = bass.ds(c, 1)
                nc.scalar.activation(wg_hi[:, at, :], wg_raw[:, at, :], ACT.Copy).then_inc(wg_hi_ready, 1)

            for q in range(RING):
                v_step(q, 0, first=(q == 0))
            def v_steps(first, last):
                with act.Fori(first, last) as i:
                    for q in range(RING):
                        v_step(q, i)

            v_steps(1, 23)
            act.wait_ge(wp_loaded, 48)
            act.wait_ge(g_lo_ready, 84)
            for k in range(2):
                nc.scalar.activation(wp_hi[:, k, :], wp_raw[:, k, :], ACT.Copy).then_inc(ple_hi, 1)
                v_steps(23 + k, 24 + k)
            nc.scalar.activation(pt_hi[:, :, :], pt_raw[:, :, :], ACT.Copy).then_inc(ple_hi, 1)
            with act.Fori(25, N_KEYS // RING - 1) as i:
                for q in range(RING):
                    v_step(q, i)
                gate_weights_hi(i - 25)
            for q in range(RING):
                v_step(q, N_KEYS // RING - 1, skip=(RING, RING + 1))
                if q >= 2:
                    gate_weights_hi(DC - 4 + q)
            for tt in range(TT):
                for c in range(DC):
                    if c % 4 == 0:
                        act.wait_ge(end_t_done, 2 * tt + c // 4 + 1)
                    ins = nc.scalar.activation(xt_hi[:, c, P * tt:P * (tt + 1)], end_t(tt, c), ACT.Copy,
                                               scale=gain[:, 3, c:c + 1])
                    if c % 4 == 3:
                        ins.then_inc(end_hi_ready, 1)
            for tt in range(TT):
                squares(3, tt, tt, h[:, tt, :], xs_end[:, tt, :])
            act.wait_ge(mean_ready, 6)
            root(3, 0, 2)
            nc.scalar.preload_act_table(ACT.Sigmoid)
            act.wait_ge(end_rstd_ready, 1)
            for u, (tt, d0, width, b) in enumerate(END_PARTS):
                act.wait_ge(gate_done, u + 1)
                nc.scalar.activation(sig[:, tt, d0:d0 + width], bank[b][:, 0:width],
                                     ACT.Sigmoid, scale=norm_stats(3)[2][:, tt:tt + 1]).then_inc(sig_ready, 1)

        @block.vector
        def _(dve):
            steps = [0]

            def link(ins):
                steps[0] += 1
                ins.then_inc(dve_step, 1)
                dve.wait_ge(dve_step, steps[0])

            def split_group(n):
                dve.wait_ge(w_hi_ready, split_count(n))
                nc.vector.tensor_tensor(w_lo[:, n % 2, :, :], w_raw[:, n % 2, :, :],
                                        w_hi[:, n % 2, :, :].bitcast(f32), ALU.subtract).then_inc(w_lo_ready, 1)

            def mean(k, count, first, last, n):
                ss, ms, _ = norm_stats(k)
                dve.wait_ge(squares_done, count)
                nc.vector.tensor_scalar(ms[:, first:last], ss[:, first:last], 1.0 / n, EPS, ALU.mult,
                                        ALU.add).then_inc(mean_ready, 1)

            def inverse(k, count, first, last):
                rstd = norm_stats(k)[2]
                dve.wait_ge(root_ready, count)
                return nc.vector.reciprocal(rstd[:, first:last], rstd[:, first:last])

            def scaled(k, tt):
                nc.vector.tensor_scalar(xs[:, tt, :], h[:, tt, :], norm_stats(k)[2][:, tt:tt + 1], None,
                                        ALU.mult).then_inc(xs_ready, 1)

            def transposed_lo(k, b, nth):
                dve.wait_ge(xt_hi_ready, 4 * k + nth + 1)
                for c in (2 * b, 2 * b + 1):
                    nc.vector.scalar_tensor_tensor(out=xt_lo[:, c, :], in0=xt_half(k, c), scalar=gain[:, k, c:c + 1],
                                                   in1=xt_hi[:, c, :].bitcast(f32), op0=ALU.mult,
                                                   op1=ALU.subtract).then_inc(xt_lo_ready, 1)

            nc.vector.memset(tab_in[REL:REL + 1, TAB:TAB + NH], -1e30).then_inc(table_row, 1)
            for tt in range(TT):
                mean(0, tt + 1, tt, tt + 1, D)
                link(inverse(0, tt + 1, tt, tt + 1))
                scaled(0, tt)
            for n in range(2):
                for b in range(4):
                    dve.wait_ge(quarter_hi, 4 * n + b + 1)
                    nc.vector.tensor_tensor(w_lo[:, n, 2 * b:2 * b + 2, :], w_raw[:, n, 2 * b:2 * b + 2, :],
                                            w_hi[:, n, 2 * b:2 * b + 2, :].bitcast(f32),
                                            ALU.subtract).then_inc(quarter_lo, 1)
                    if n == 0:
                        transposed_lo(0, b, b)
            split_group(2)
            dve.wait_ge(group_out, 4)
            for tt in range(TT):
                link(nc.vector.tensor_tensor(square[:, :, :], qk_nat[:, tt, :, :], qk_nat[:, tt, :, :], ALU.mult))
                link(nc.vector.tensor_reduce(QSS[:, 16 * tt:16 * tt + 16], square[:, :, :], AX.X, ALU.add))
            nc.vector.tensor_scalar(QSS, QSS, 1.0 / HD, EPS, ALU.mult, ALU.add).then_inc(qk_mean, 1)
            dve.wait_ge(qk_root, 1)
            link(nc.vector.reciprocal(QRSTD, QRSTD))
            for tt in range(TT):
                r = QRSTD[:, 16 * tt:16 * tt + 16].unsqueeze(2).to_broadcast([P, 2 * NH, HD])
                nc.vector.tensor_tensor(qk_nat[:, tt, :, :], qk_nat[:, tt, :, :], r, ALU.mult).then_inc(qk_normed, 1)
            split_group(3)
            split_group(4)
            split_group(5)

            def value_out(g, tt):
                if tt:
                    dve.wait_ge(*used(V_M + g))
                else:
                    dve.wait_ge(v_tile_done, g + 1)
                nc.vector.tensor_copy(v_all[:, tt, 512 * g:512 * (g + 1)], bank[6 + tt][:, :]).then_inc(v_out, 1)

            value_out(0, 0)
            value_out(0, 1)
            for e in range(2):
                dve.wait_ge(z_softplus, e + 1)
                nc.vector.tensor_tensor(sb_sp[:, e, :], sb_sp[:, e, :], sb_w[:, e, :], ALU.add).then_inc(sp_added, 1)
            value_out(1, 0)
            split_group(6)
            value_out(1, 1)
            dve.wait_ge(bias_ready, 4)

            def biased(r, dst, first, n, s_from):
                dve.wait_ge(qk_done, r + 1)
                for e in range(2):
                    a, b = first + e, first + e + 2 * n - 1
                    ins = nc.vector.scalar_tensor_tensor(
                        out=dst[:, a:b:2, :], scalar=SCALE,
                        in0=bank[[6, 0, 6][r] + e][:, :].rearrange("p (a b) -> p a b", a=n),
                        in1=bias[:, a:b:2, s_from:SEQ], op0=ALU.mult, op1=ALU.add)
                ins.then_inc(qk_biased, 1)

            def shifted(r, s, mx, n):
                dve.wait_ge(qk_biased, r + 1)
                link(nc.vector.tensor_reduce(mx, s, AX.X, ALU.max))
                nc.vector.tensor_tensor(s, s, mx.unsqueeze(2).to_broadcast([P, mx.shape[1], n]),
                                        ALU.subtract).then_inc(s_shifted, 1)

            biased(0, s0, 0, 4, P)
            shifted(0, s0[:, :, :], MX0, P)
            biased(1, s1, 0, 2, 0)
            biased(2, s1, 4, 2, 0)
            shifted(1, s1[:, 0:4, :], MX1[:, 0:4], SEQ)
            shifted(2, s1[:, 4:8, :], MX1[:, 4:8], SEQ)
            for tt, s in ((0, s0), (1, s1)):
                dve.wait_ge(s_exp, [1, 3][tt])
                link(nc.vector.tensor_reduce(SUM[:, 8 * tt:8 * tt + 8], s[:, :, :], AX.X, ALU.add))
                link(nc.vector.reciprocal(SUM[:, 8 * tt:8 * tt + 8], SUM[:, 8 * tt:8 * tt + 8]))
            split_group(7)
            for tt in range(TT):
                dve.wait_ge(pv_done, tt + 1)
                r = SUM[:, 8 * tt:8 * tt + 8].unsqueeze(2).to_broadcast([P, NH, HD])
                nc.vector.tensor_tensor(o_nat[:, tt, 0:512].rearrange("p (a b) -> p a b", a=NH),
                                        bank[tt][:, :].rearrange("p (a b) -> p a b", a=NH), r,
                                        ALU.mult).then_inc(pv_out, 1)
            for nth, b in enumerate((2, 3, 0, 1)):
                transposed_lo(1, b, nth)
            mean(1, 2 + 4, 0, 4, 512)
            link(inverse(1, 3, 0, 4))
            r_out = norm_stats(1)[2]

            def projected(g, tt, part):
                if g:
                    dve.wait_ge(out_done, 5 + 2 * tt + part)
                cols = slice(512 * g, 512 * g + 512)
                ins = nc.vector.scalar_tensor_tensor(out=h[:, tt, cols], in0=bank[out_bank(g, part, tt)][:, :],
                                                     scalar=r_out[:, 2 * part + tt:2 * part + tt + 1],
                                                     in1=h[:, tt, cols], op0=ALU.mult, op1=ALU.add)
                if part == 0:
                    link(ins)
                else:
                    ins.then_inc(h1_ready, 1)

            def norm2_scaled(tt):
                dve.wait_ge(squares_done, 9 + tt)
                ss = norm_stats(2)[0]
                link(nc.vector.tensor_tensor(ss[:, tt:tt + 1], ss[:, tt:tt + 1], ss[:, 2 + tt:3 + tt], ALU.add))
                mean(2, 9 + tt, tt, tt + 1, D)
                link(inverse(2, 4 + tt, tt, tt + 1))
                scaled(2, tt)

            dve.wait_ge(*used(OUT0))
            for tt in range(TT):
                for part in range(2):
                    projected(0, tt, part)
            dve.wait_ge(w8_hi_ready, 1)
            nc.vector.tensor_tensor(w_lo[:, 0, 0:4, :], w_raw[:, 0, 0:4, :], w_hi[:, 0, 0:4, :].bitcast(f32),
                                    ALU.subtract).then_inc(w8_lo_ready, 1)
            for part in range(2):
                projected(1, 0, part)
            norm2_scaled(0)
            projected(1, 1, 0)
            projected(1, 1, 1)
            norm2_scaled(1)
            for b in range(4):
                transposed_lo(2, b, b)
            split_group(9)
            split_group(10)
            split_group(11)

            def table_lo(q, count):
                dve.wait_ge(t_hi_ready, count)
                nc.vector.tensor_tensor(t_lo[:, q % RING, :], t_raw[:, q % RING, :],
                                        t_hi[:, q % RING, :].bitcast(f32), ALU.subtract).then_inc(t_lo_ready, 1)

            table_lo(0, 1)
            dve.wait_ge(s_out, 8)

            def top16(jobs):
                def each(op):
                    done = []
                    for job in jobs:
                        steps[0] += 1
                        op(*job).then_inc(dve_step, 1)
                        done.append(steps[0])
                    return done

                def after(done, op):
                    waits = iter(done)

                    def waited(*job):
                        dve.wait_ge(dve_step, next(waits))
                        return op(*job)
                    return each(waited)

                first = each(lambda src, v, i, rest: nc.vector.max(v[:, 0:8], src))
                replaced = after(first, lambda src, v, i, rest: nc.vector.match_replace(rest, v[:, 0:8], src, -3e38))
                each(lambda src, v, i, rest: nc.vector.max_index(i[:, 0:8], v[:, 0:8], src))
                second = after(replaced, lambda src, v, i, rest: nc.vector.max(v[:, 8:16], rest))
                last = after(second, lambda src, v, i, rest: nc.vector.max_index(i[:, 8:16], v[:, 8:16], rest))
                dve.wait_ge(dve_step, last[-1])

            def halves(tt, g):
                top16([(scores[:, tt, g + k, :], top_v[:, tt, g + k, :], top_i[:, tt, g + k, :], rest[:, k, 0:P])
                       for k in range(2)])

            def pairs_of(tt):
                v = top_v[:, tt, :, :].rearrange("p (h two) k -> p h two k", two=2)
                link(nc.vector.tensor_copy(top_f[:, tt, :, :], top_i[:, tt, :, :]))
                place = 0
                for a, n, m in BLOCKS:
                    ins = nc.vector.tensor_tensor(
                        cand[:, :, place:place + n * m].rearrange("p h (a b) -> p h a b", a=n),
                        v[:, :, 0, a:a + n].unsqueeze(3).to_broadcast([P, PH, n, m]),
                        v[:, :, 1, 0:m].unsqueeze(2).to_broadcast([P, PH, n, m]), ALU.add)
                    place += n * m
                link(ins)

            def best_of(tt, h):
                top16([(cand[:, hh, :], best_v[:, tt, hh, :], pos_u[:, 0, TOPK * hh:TOPK * (hh + 1)],
                        rest[:, hh % 2, 0:PAIRS]) for hh in (h, h + 1)])

            def positions(tt):
                nc.vector.tensor_scalar(pos_u[:, 1, :], pos_u[:, 0, :], 3, None, ALU.logical_shift_right)
                link(nc.vector.tensor_scalar(pos_u[:, 2, :], pos_u[:, 0, :], 2, None, ALU.logical_shift_right))
                link(nc.vector.tensor_copy(pos_f[:, :, :], pos_u[:, :, :]))
                c, c8, c4 = (pos_f[:, k, :] for k in range(3))
                m0, m1, m2, m3 = (pos_m[:, k, :] for k in range(4))
                a, b = pos_ab[:, 0, :], pos_ab[:, 1, :]
                link(nc.vector.tensor_scalar(m0, c8, -1.0, 0.0, ALU.add, ALU.max))
                link(nc.vector.scalar_tensor_tensor(out=m1, in0=c4, scalar=-6.0, in1=m0, op0=ALU.add, op1=ALU.max))
                link(nc.vector.scalar_tensor_tensor(out=a, in0=c, scalar=-48.0, in1=m1, op0=ALU.add, op1=ALU.max))
                nc.vector.tensor_scalar(m2, a, 8.0, 8.0, ALU.mult, ALU.add)
                link(nc.vector.tensor_scalar(m3, a, 4.0, 24.0, ALU.mult, ALU.add))
                nc.vector.scalar_tensor_tensor(out=m0, in0=a, scalar=16.0, in1=m2, op0=ALU.mult, op1=ALU.min)
                link(nc.vector.scalar_tensor_tensor(out=m1, in0=a, scalar=48.0, in1=m3, op0=ALU.add, op1=ALU.min))
                link(nc.vector.tensor_tensor(m2, m0, m1, ALU.min))
                link(nc.vector.tensor_tensor(b, c, m2, ALU.subtract))
                top = best_v[:, tt, :, 0:1].to_broadcast([P, PH, TOPK])
                nc.vector.tensor_tensor(gate[:, tt, :, :], best_v[:, tt, :, :], top,
                                        ALU.subtract).then_inc(gate_shifted, 1)

            def picked(tt, q):
                lanes = iota[:, 0:TOPK].unsqueeze(1).unsqueeze(1).to_broadcast([P, PH, TOPK, TOPK])
                place = pos_ab[:, q, :].rearrange("p (a b) -> p a b", a=PH).unsqueeze(3).to_broadcast(
                    [P, PH, TOPK, TOPK])
                number = top_f[:, tt, :, :].rearrange("p (h two) k -> p h two k", two=2)[:, :, q, :].unsqueeze(
                    2).to_broadcast([P, PH, TOPK, TOPK])

                def summed():
                    ins = nc.vector.tensor_reduce(pick[:, tt, q, :].rearrange("p (a b) -> p a b", a=PH),
                                                  hit[:, :, :, :], AX.X, ALU.add)
                    ins.then_inc(hit_used, 1)
                    dve.wait_ge(hit_used, 2 * tt + q + 1)

                return [lambda: link(nc.vector.tensor_tensor(hit[:, :, :, :], lanes, place, ALU.is_equal)),
                        lambda: link(nc.vector.tensor_tensor(hit[:, :, :, :], hit[:, :, :, :], number, ALU.mult)),
                        summed]

            def gates_of_picks():
                dve.wait_ge(gate_exp, 1)
                link(nc.vector.tensor_reduce(GSUM.rearrange("p (a b) -> p a b", a=TT), gate[:, :, :, :], AX.X,
                                             ALU.add))
                link(nc.vector.reciprocal(GSUM, GSUM))
                nc.vector.tensor_tensor(gate[:, :, :, :], gate[:, :, :, :],
                                        GSUM.rearrange("p (a b) -> p a b", a=TT).unsqueeze(3).to_broadcast(
                                            [P, TT, PH, TOPK]), ALU.mult).then_inc(picks_ready, 1)

            pieces = []
            for tt in range(TT):
                pieces += [(1, lambda tt=tt, g=g: halves(tt, g)) for g in range(0, PG, 2)]
                if tt:
                    pieces += [(0, lambda: dve.sem_inc(halves_done, 1))]
                pieces += [(1, lambda tt=tt: pairs_of(tt))]
                pieces += [(1, lambda tt=tt, hh=hh: best_of(tt, hh)) for hh in range(0, PH, 2)]
                pieces += [(2, lambda tt=tt: positions(tt))]
                pieces += [(2, lambda step=step: step()) for q in range(2) for step in picked(tt, q)]
            splits = TOPK_END // RING
            total, spent, pieces = sum(w for w, _ in pieces), 0, iter(pieces)
            for k in range(splits):
                while 2 * spent * splits < total * (2 * k + 1):
                    weight, piece = next(pieces)
                    piece()
                    spent += weight
                table_lo(0, RING * (k + 1) + 1)
            for _, piece in pieces:
                piece()
            gates_of_picks()

            for n in range(TOPK_END + RING, FIRST, RING):
                table_lo(0, n + 1)
            for q in range(3):
                dve.wait_ge(pick_t_done, q + 1)
                nc.vector.tensor_copy(pick_t[:, q, :], half(q, 0)).then_inc(pick_t_out, 1)
            table_lo(0, FIRST + 1)

            def one_hots(k, s):
                for q in range(4):
                    t = 4 * s + q
                    ins = nc.vector.tensor_scalar(hot_j[:, k, q, :], iota, pick_t[:, 1, bass.ds(t, 1)],
                                                  pick_t[:, 2, bass.ds(t, 1)], ALU.is_equal, ALU.mult)
                ins.then_inc(hot_j_ready, 1)

            def gated_set(b, s):
                dve.wait_ge(gates_done, s + 1)
                dst = slots[:, :, bass.ds(4 * s, 4)]
                nc.vector.tensor_tensor(dst, dst, bank[b][:, :].rearrange("p (t j) -> p j t", t=4),
                                        ALU.mult).then_inc(gated, 1)

            def late_gelu(q, n, count):
                dve.wait_ge(gelu_done, n + 1)
                dve.wait_ge(gated, count)
                dst = slots[:, bass.ds(n, 1), :].rearrange("p o t -> p (o t)")
                nc.vector.tensor_tensor(dst, dst, half(4 + q, 1), ALU.mult).then_inc(late_used, 1)

            def late_step(q, i, nth=2):
                n = RING * i + q
                s = n - FIRST
                one_hots(q % 2, s)
                if nth == 1:
                    dve.wait_ge(ones_ready, (N_KEYS - FIRST) // ONES)
                    dve.wait_ge(gelu_done, FIRST)
                if nth:
                    if nth > 1:
                        dve.wait_ge(late_used, s - 1)
                    gated_set((q - 1) % RING, s - 1)
                    late_gelu((q - 1) % RING, n - 1, s)
                if (q + LEAD) % RING == 0:
                    table_lo(0, n + LEAD + 1)

            def gated_lo_of(tt, semaphore):
                t = slice(P * tt, P * (tt + 1))
                nc.vector.tensor_tensor(g_lo[:, 0, t], slots[:, 0, t], g_hi[:, 0, t].bitcast(f32),
                                        ALU.subtract).then_inc(semaphore, 1)

            dve.wait_ge(pick_t_out, 3)
            for q in range(RING):
                late_step(q, FIRST // RING, q)
            with dve.Fori(FIRST // RING + 1, N_KEYS // RING) as i:
                for q in range(RING):
                    late_step(q, i)
            dve.wait_ge(late_used, N_KEYS - FIRST - 1)
            gated_set(RING - 1, SETS - 1)
            dve.wait_ge(g_hi_first, 1)
            gated_lo_of(0, g_lo_first)
            late_gelu(RING - 1, N_KEYS - 1, SETS)
            dve.wait_ge(g_hi_ready, 1)
            gated_lo_of(1, g_lo_ready)

            def gated_lo(k, n):
                dve.wait_ge(g_hi_ready, n + 1)
                src = slots[:, bass.ds(n, 1), :].rearrange("p o t -> p (o t)")
                nc.vector.tensor_tensor(g_lo[:, k, :], src, g_hi[:, k, :].bitcast(f32),
                                        ALU.subtract).then_inc(g_lo_ready, 1)

            def v_step(q, i, skip=()):
                if q + 1 not in skip:
                    gated_lo((q + 1) % 2, RING * i + q + 1)
                if q + LEAD not in skip:
                    table_lo(q + LEAD, N_KEYS + RING * i + q + LEAD + 1)

            def gate_weights_lo(c):
                dve.wait_ge(wg_hi_ready, c + 1)
                at = bass.ds(c, 1)
                nc.vector.tensor_tensor(wg_lo[:, at, :], wg_raw[:, at, :], wg_hi[:, at, :].bitcast(f32),
                                        ALU.subtract).then_inc(wg_lo_ready, 1)

            with dve.Fori(0, 25) as i:
                for q in range(RING):
                    v_step(q, i)
            with dve.Fori(25, N_KEYS // RING - 1) as i:
                for q in range(RING):
                    v_step(q, i)
                gate_weights_lo(i - 25)
            for q in range(RING):
                v_step(q, N_KEYS // RING - 1, skip=(RING, RING + 1))
                if q >= 2:
                    gate_weights_lo(DC - 4 + q)
            for tt in range(TT):
                if tt:
                    dve.wait_ge(v_used, N_KEYS)
                else:
                    dve.wait_ge(v_tile0_done, 1)
                for q in range(2):
                    nc.vector.tensor_tensor(h[:, tt, 512 * q:512 * q + 512], h[:, tt, 512 * q:512 * q + 512],
                                            bank[2 * tt + q][:, :], ALU.add).then_inc(h2_ready, 1)
            for tt in range(TT):
                for c in range(DC):
                    if c % 4 == 0:
                        dve.wait_ge(end_hi_ready, 2 * tt + c // 4 + 1)
                    t = slice(P * tt, P * (tt + 1))
                    ins = nc.vector.scalar_tensor_tensor(out=xt_lo[:, c, t], in0=end_t(tt, c),
                                                         scalar=gain[:, 3, c:c + 1],
                                                         in1=xt_hi[:, c, t].bitcast(f32), op0=ALU.mult,
                                                         op1=ALU.subtract)
                    if c % 4 == 3:
                        ins.then_inc(end_lo_ready, 1)
            mean(3, 12, 0, 2, D)
            inverse(3, 6, 0, 2).then_inc(end_rstd_ready, 1)
            for u, (tt, d0, width, b) in enumerate(END_PARTS):
                d = slice(d0, d0 + width)
                dve.wait_ge(sig_ready, u + 1)
                link(nc.vector.tensor_tensor(sig[:, tt, d], sig[:, tt, d],
                                             bank[4 + 2 * tt + d0 // 512][:, d0 % 512:d0 % 512 + width], ALU.mult))
                nc.vector.tensor_tensor(h[:, tt, d], h[:, tt, d], sig[:, tt, d], ALU.add).then_inc(y_ready, 1)

        @block.gpsimd
        def _(pool):
            def strict(t, e, half_s):
                if half_s == 0:
                    v = t[:, e, 0:1024].rearrange("p (i t) -> p i t", i=4)[:, :, 0:P]
                else:
                    v = t[:, e, 1024:1536].rearrange("p (i t) -> p i t", i=4)
                return nc.gpsimd.affine_select(out=v, in_=v, compare_op=ALU.is_gt, fill=0.0, base=0,
                                               pattern=[[0, 4], [1, P]], channel_multiplier=-1)

            for e in range(2):
                pool.wait_ge(sp_added, e + 1)
                strict(sb_sp, e, 0)
                strict(sb_sp, e, 1).then_inc(sp_masked, 1)
            for e in range(2):
                pool.wait_ge(w_exp, 3 * (e + 1))
                strict(sb_w, e, 0)
                strict(sb_w, e, 1).then_inc(w_masked, 1)
            pool.wait_ge(w8_hi_ready, 2)
            nc.gpsimd.tensor_tensor(w_lo[:, 0, 4:8, :], w_raw[:, 0, 4:8, :], w_hi[:, 0, 4:8, :].bitcast(f32),
                                    ALU.subtract).then_inc(w8_lo_ready, 1)

            def table_lo(q, n):
                pool.wait_ge(t_hi_ready, n + 1)
                nc.gpsimd.tensor_tensor(t_lo[:, q, :], t_raw[:, q, :], t_hi[:, q, :].bitcast(f32),
                                        ALU.subtract).then_inc(t_lo_pool, 1)

            def u_steps(first, last):
                with pool.Fori(first // RING, last // RING) as i:
                    for q in range(RING):
                        if (q + LEAD) % RING:
                            table_lo((q + LEAD) % RING, RING * i + q + LEAD)

            def ones_steps(first, last):
                for n in range(first, last):
                    if (n + LEAD) % RING:
                        table_lo((n + LEAD) % RING, n + LEAD)
                    at = FIRST + ONES * (n - ONES_AT)
                    nc.gpsimd.memset(slots[:, at:at + ONES, :], 1.0).then_inc(ones_ready, 1)

            for n in range(1, LEAD):
                table_lo(n, n)
            u_steps(0, ONES_AT)
            pool.wait_ge(halves_done, 1)
            ones_steps(ONES_AT, TOPK_END)
            pool.wait_ge(hit_used, 4)
            pool.wait_ge(gate_shifted, TT)
            ones_end = ONES_AT + (N_KEYS - FIRST) // ONES
            ones_steps(TOPK_END, ones_end)

            def one_hots(k, s):
                chosen = pick_t[:, 0, bass.ds(4 * s, 4)].unsqueeze(2).to_broadcast([P, 4, P])
                nc.gpsimd.tensor_tensor(hot_i[:, k, :, :], iota.unsqueeze(1).to_broadcast([P, 4, P]), chosen,
                                        ALU.subtract).then_inc(hot_i_diff, 1)

            pool.wait_ge(pick_t_out, 3)
            for n in range(ones_end, FIRST):
                if (n + LEAD) % RING:
                    table_lo((n + LEAD) % RING, n + LEAD)
                else:
                    for k in range(2):
                        one_hots(k, k)

            def late_step(q, i, first=False):
                n = RING * i + q
                s = n - FIRST
                if not (first and q < 2):
                    pool.wait_ge(gates_done, s - 1)
                    one_hots(q % 2, s)
                if (q + LEAD) % RING:
                    table_lo((q + LEAD) % RING, n + LEAD)

            for q in range(RING):
                late_step(q, FIRST // RING, True)
            with pool.Fori(FIRST // RING + 1, N_KEYS // RING) as i:
                for q in range(RING):
                    late_step(q, i)
            pool.wait_ge(ple_hi, 3)
            nc.gpsimd.tensor_tensor(wp_lo[:, :, :], wp_raw[:, :, :], wp_hi[:, :, :].bitcast(f32),
                                    ALU.subtract).then_inc(ple_lo, 1)
            nc.gpsimd.tensor_tensor(pt_lo[:, :, :], pt_raw[:, :, :], pt_hi[:, :, :].bitcast(f32),
                                    ALU.subtract).then_inc(ple_lo, 1)

        @block.tensor
        def _(pe):
            mm = nc.tensor.matmul

            def transpose(src, tt, c, dst):
                return nc.tensor.transpose(dst, src[:, tt, P * c:P * (c + 1)], ident)

            def transposes(k, count):
                for tt in range(TT):
                    pe.wait_ge(xs_ready, count + tt + 1)
                    for c in range(DC):
                        ins = transpose(xs, tt, c, xt_half(k, c)[:, P * tt:P * (tt + 1)])
                        if tt and c % 2:
                            ins.then_inc(xt_done, 1)

            def three(dst, pairs, last=None):
                n = len(pairs)
                for c, ((ah, al), (bh, bl)) in enumerate(pairs):
                    mm(dst, ah, bh, start=(c == 0), stop=False)
                    mm(dst, ah, bl, start=False, stop=False)
                    ins = mm(dst, al, bh, start=False, stop=(c == n - 1))
                return ins

            def rows_group(n, b, tile_done=None, read=None):
                pe.wait_ge(*split(n))
                for tt in range(TT):
                    if read:
                        pe.wait_ge(read, tt + 1)
                    t = slice(P * tt, P * (tt + 1))
                    ins = three(bank[b + tt][:, :], [((xt_hi[:, c, t], xt_lo[:, c, t]),
                                                      (w_hi[:, n % 2, c, :], w_lo[:, n % 2, c, :])) for c in range(DC)])
                    if tile_done and tt == 0:
                        ins.then_inc(tile_done, 1)
                ins.then_inc(w_used, 1)

            def columns_group(n, b):
                pe.wait_ge(*split(n))
                for q in range(4):
                    m = slice(P * q, P * (q + 1))
                    dst = half(b + q // 2, q % 2)
                    for c in range(DC):
                        if n == QUERY0 and q == 0:
                            pe.wait_ge(xt_lo_ready, 2 * DC + c + 1)
                        mm(dst, w_hi[:, n % 2, c, m], xt_hi[:, c, :], start=(c == 0), stop=False)
                        mm(dst, w_lo[:, n % 2, c, m], xt_hi[:, c, :], start=False, stop=False)
                        ins = mm(dst, w_hi[:, n % 2, c, m], xt_lo[:, c, :], start=False, stop=(c == DC - 1))
                ins.then_inc(w_used, 1)

            pe.wait_ge(small_loaded, 48)
            transposes(0, 0)
            for c in range(DC):
                pe.wait_ge(xt_lo_ready, c + 1)
                pe.wait_ge(quarter_lo, c // 2 + 1)
                for tt in range(TT):
                    t, dst = slice(P * tt, P * (tt + 1)), bank[4 + tt][:, :]
                    mm(dst, xt_hi[:, c, t], w_hi[:, 0, c, :], start=(c == 0), stop=False)
                    mm(dst, xt_hi[:, c, t], w_lo[:, 0, c, :], start=False, stop=False)
                    ins = mm(dst, xt_lo[:, c, t], w_hi[:, 0, c, :], start=False, stop=(c == DC - 1))
            ins.then_inc(w_used, 1)
            pe.wait_ge(tab_loaded, 32)
            pe.wait_ge(table_row, 1)
            mm(bank[7][0:NH, 0:TAB], tab_in[:, TAB:TAB + NH], tab_in[:, 0:TAB], start=True, stop=True).then_inc(
                tab_made, 1)
            pe.wait_ge(tab_copied, 1)
            rows_group(K_M, 6)
            pe.wait_ge(bias_loaded, 16)
            for b in range(4):
                mm(bank[b][:, :], flip, skew[:, 2 * b:2 * b + 2, :].rearrange("p a b -> p (a b)"), start=True,
                   stop=True).then_inc(flip_done, 1)
            pe.wait_ge(group_out, 2)
            columns_group(Q_S, 4)
            pe.wait_ge(qk_normed, TT)
            pe.wait_ge(bias_ready, 4)
            for g in range(8):
                for tt in range(TT):
                    ins = nc.tensor.transpose(bank[g // 2][:, 256 * (g % 2) + P * tt:256 * (g % 2) + P * (tt + 1)],
                                              qk_nat[:, tt, 2 * g:2 * g + 2, :].rearrange("p a b -> p (a b)"), ident)
                if g % 2:
                    ins.then_inc(qkt_done, 1)
            pe.wait_ge(group_out, 4)
            columns_group(K_S, 6)

            pe.wait_ge(qkt_out, 4)
            pe.wait_ge(group_out, 7)
            for e in range(2):
                r = slice(HD * e, HD * (e + 1))
                for i in range(4):
                    if e == 0 and i == 2:
                        pe.wait_ge(group_out, 8)
                    mm(bank[3 * e + i // 2][:, 256 * (i % 2):256 * (i % 2) + 256], qkt_s[r, 4 + i, 0:P], qkt_s[r, i, :],
                       start=(i % 2 == 0), stop=True, skip_group_check=True)
                for i in range(4):
                    ins = mm(bank[3 * e + 2][:, P * i:P * (i + 1)], qkt_s[r, 4 + i, P:SEQ], qkt_s[r, i, P:SEQ],
                             start=(i == 0), stop=True, skip_group_check=True)
                ins.then_inc(z_done, 1)
            rows_group(V_M, 6, v_tile_done)
            rows_group(V_S, 6, v_tile_done, v_out)

            def softmax_scores(r, tt, first, n, b):
                width = P * (tt + 1)
                for i in range(n):
                    for e in range(2):
                        hh = first + 2 * i + e
                        rows = slice(HD * e, HD * (e + 1))
                        ins = mm(bank[b + e][:, width * i:width * (i + 1)], qkt_m[rows, hh // 2, P * tt:P * (tt + 1)],
                                 qkt_m[rows, 4 + hh // 2, 0:width], start=True, stop=True)
                ins.then_inc(qk_done, 1)

            def running_sum(e):
                pe.wait_ge(sp_masked, e + 1)
                lower, upper = sb_sp[:, e, 0:1024], sb_sp[:, e, 1024:1536]
                for b in range(2):
                    mm(bank[3 * e + b][:, :], neg_tri, lower[:, 512 * b:512 * (b + 1)], start=False, stop=False,
                       skip_group_check=True)
                    mm(bank[3 * e + b][:, :].rearrange("p (i t) -> p i t", i=2)[:, :, P:SEQ], neg_ones,
                       upper[:, 256 * b:256 * (b + 1)].rearrange("p (i t) -> p i t", i=2), start=False, stop=True,
                       skip_group_check=True)
                mm(bank[3 * e + 2][:, :], neg_tri, upper, start=False, stop=True,
                   skip_group_check=True).then_inc(cum_done, 1)

            running_sum(0)
            pe.wait_ge(v_out, 4)
            softmax_scores(0, 0, 0, 4, 6)
            running_sum(1)
            pe.wait_ge(w_exp, 3)
            softmax_scores(1, 1, 0, 2, 0)
            pe.wait_ge(qk_biased, 1)
            softmax_scores(2, 1, 4, 2, 6)

            pe.wait_ge(qk_biased, 2)
            pe.wait_ge(s_exp, 1)
            for hh in range(NH):
                ins = nc.tensor.transpose(bank[hh // 4][:, P * (hh % 4):P * (hh % 4 + 1)], s0[:, hh, :], ident)
                if hh % 4 == 3:
                    ins.then_inc(pt_done, 1)
            pe.wait_ge(qk_biased, 3)
            pe.wait_ge(w_masked, 2)
            for tt in range(TT):
                for hh in range(NH):
                    e, i = hh % 2, hh // 2
                    cols = slice(512 + HD * hh, 512 + HD * (hh + 1))
                    dst = bank[6 + tt][:, HD * hh:HD * (hh + 1)]
                    c = 256 * i + P * tt
                    ins = mm(dst, sb_w[:, e, c:c + P], v_all[:, 0, cols], start=True, stop=(tt == 0))
                    if tt:
                        ins = mm(dst, sb_w[:, e, 1024 + P * i:1024 + P * (i + 1)], v_all[:, 1, cols], start=False,
                                 stop=True)
                ins.then_inc(spv_done, 1)
            pe.wait_ge(pt_out, 2)
            for hh in range(NH):
                ins = mm(bank[0][:, HD * hh:HD * (hh + 1)], probs_t[:, hh // 4, P * (hh % 4):P * (hh % 4 + 1)],
                         v_all[:, 0, HD * hh:HD * (hh + 1)], start=True, stop=True)
            ins.then_inc(pv_done, 1)
            pe.wait_ge(w_exp, 6)
            for hh in range(NH):
                if hh % 4 == 0:
                    pe.wait_ge(s_exp, 2 + hh // 4)
                for ss in range(2):
                    c = 256 * (hh % 2) + P * ss
                    ins = nc.tensor.transpose(bank[2 + hh // 2][:, c:c + P], s1[:, hh, P * ss:P * (ss + 1)], ident)
                if hh % 2:
                    ins.then_inc(pt_done, 1)
            for hh in range(NH):
                if hh % 2 == 0:
                    pe.wait_ge(pt_out, 3 + hh // 2)
                place = (2 + hh // 2) % 4
                for ss in range(2):
                    c = 256 * (hh % 2) + P * ss
                    ins = mm(bank[1][:, HD * hh:HD * (hh + 1)], probs_t[:, place, c:c + P],
                             v_all[:, ss, HD * hh:HD * (hh + 1)], start=(ss == 0), stop=(ss == 1))
            ins.then_inc(pv_done, 1)

            for part, out_ready in ((1, spv_out), (0, pv_out)):
                pe.wait_ge(out_ready, 2)
                for c in range(4 * part, 4 * part + 4):
                    for tt in range(TT):
                        ins = transpose(o_nat, tt, c, xt_half(1, c)[:, P * tt:P * (tt + 1)])
                    if c % 2:
                        ins.then_inc(xt_done, 1)

            def projection(g, part, tt):
                pe.wait_ge(xt_lo_ready, DC + (4 if part else 8))
                t, k = slice(P * tt, P * (tt + 1)), (OUT0 + g) % 2
                three(bank[out_bank(g, part, tt)][:, :],
                      [((xt_hi[:, c, t], xt_lo[:, c, t]), (w_hi[:, k, c, :], w_lo[:, k, c, :]))
                       for c in range(4 * part, 4 * part + 4)]).then_inc(out_done, 1)

            pe.wait_ge(*split(OUT0))
            for part in (1, 0):
                for tt in range(TT):
                    projection(0, part, tt)
            pe.wait_ge(*split(OUT0 + 1))
            for tt in range(TT):
                for part in range(2):
                    projection(1, part, tt)
            pe.wait_ge(h1_ready, 2)
            transposes(2, TT)
            for n in range(4):
                if n == 0:
                    pe.wait_ge(h1_ready, 4)
                if n >= 2:
                    pe.wait_ge(query_ready, 2 * (n - 1))
                columns_group(QUERY0 + n, 2 * (n % 2))
            pe.wait_ge(sk_loaded, 16)
            for u in range(8):
                n, tt = u // 2, u % 2
                if tt == 0:
                    pe.wait_ge(query_ready, 2 * (n + 1))
                t = slice(P * tt, P * (tt + 1))
                for q in range(4):
                    g = 4 * n + q
                    ins = mm(bank[SCORE_BANKS[u]][:, P * q:P * (q + 1)], query[:, g, t], sk[:, g % 2, :], start=True,
                             stop=True)
                ins.then_inc(s_done, 1)

            def hidden(q):
                three(bank[4 + q][:, 0:SEQ], [((t_hi[:, q, P * c:P * (c + 1)], t_lo[:, q, P * c:P * (c + 1)]),
                                               (xt_hi[:, c, :], xt_lo[:, c, :])) for c in range(DC)]
                      ).then_inc(hid_done, 1)

            for q in range(RING):
                pe.wait_ge(*u_lo(q, 0))
                pe.wait_ge(s_out, q + 1)
                hidden(q)

            def u_steps(first, last):
                with pe.Fori(first // RING, last // RING) as i:
                    for q in range(RING):
                        pe.wait_ge(*u_lo(q, i))
                        pe.wait_ge(gelu_done, RING * i + q - RING + 1)
                        hidden(q)

            u_steps(RING, PICKS_AT)
            pe.wait_ge(hit_used, 2 * TT)
            for q in range(2):
                for tt in range(TT):
                    ins = nc.tensor.transpose(bank[q][:, P * tt:P * (tt + 1)], pick[:, tt, q, :], ident)
                ins.then_inc(pick_t_done, 1)
            pe.wait_ge(picks_ready, 1)
            for tt in range(TT):
                ins = nc.tensor.transpose(bank[2][:, P * tt:P * (tt + 1)],
                                          gate[:, tt, :, :].rearrange("p a b -> p (a b)"), ident)
            ins.then_inc(pick_t_done, 1)
            u_steps(PICKS_AT, FIRST)

            def gates(k, b, count):
                pe.wait_ge(hot_i_ready, count)
                pe.wait_ge(hot_j_ready, count)
                for q in range(4):
                    ins = mm(bank[b][:, P * q:P * (q + 1)], hot_i[:, k, q, :], hot_j[:, k, q, :], start=True,
                             stop=True)
                ins.then_inc(gates_done, 1)

            def late_step(q, i, first=False):
                n = RING * i + q
                s = n - FIRST
                pe.wait_ge(*u_lo(q, i))
                if first:
                    pe.wait_ge(gelu_done, n - RING + 1)
                else:
                    pe.wait_ge(late_used, s - RING + 1)
                hidden(q)
                if not first:
                    pe.wait_ge(gated, s - RING + 1)
                gates(q % 2, q, s + 1)

            for q in range(RING):
                late_step(q, FIRST // RING, True)
            with pe.Fori(FIRST // RING + 1, N_KEYS // RING) as i:
                for q in range(RING):
                    late_step(q, i)

            def expert_sum(q, i, first=False, last=False):
                if first and q < LEAD:
                    pe.wait_ge(*u_lo(q, N_KEYS // RING))
                else:
                    pe.wait_ge(t_lo_ready, v_lo + RING * i + q + 1)
                if first and q == 0:
                    pe.wait_ge(g_lo_first, 1)
                else:
                    pe.wait_ge(g_lo_ready, RING * i + q + 1)
                for tt in range(TT):
                    if first and q == 0 and tt:
                        pe.wait_ge(g_lo_ready, 1)
                    t = slice(P * tt, P * (tt + 1))
                    for w in range(2):
                        d = slice(512 * w, 512 * (w + 1))
                        dst = bank[2 * tt + w][:, :]
                        mm(dst, g_hi[:, q % 2, t], t_hi[:, q, d], start=first and q == 0, stop=False,
                           skip_group_check=True)
                        mm(dst, g_hi[:, q % 2, t], t_lo[:, q, d], start=False, stop=False, skip_group_check=True)
                        ins = mm(dst, g_lo[:, q % 2, t], t_hi[:, q, d], start=False, stop=True,
                                 skip_group_check=True)
                    if last and tt == 0:
                        ins.then_inc(v_tile0_done, 1)
                ins.then_inc(v_used, 1)

            pe.wait_ge(gated, SETS)
            for q in range(RING):
                expert_sum(q, 0, first=True)
            with pe.Fori(1, N_KEYS // RING - 1) as i:
                for q in range(RING):
                    expert_sum(q, i)
            for q in range(RING):
                expert_sum(q, N_KEYS // RING - 1, last=(q == RING - 1))

            pe.wait_ge(ple_lo, 2)
            for u in range(4):
                tt, q = u // 2, u % 2
                t, d = slice(P * tt, P * (tt + 1)), slice(512 * q, 512 * (q + 1))
                three(bank[4 + u][:, :], [((pt_hi[:, c, t], pt_lo[:, c, t]), (wp_hi[:, c, d], wp_lo[:, c, d]))
                                          for c in range(PLE // P)])
            for tt in range(TT):
                pe.wait_ge(h2_ready, 2 * (tt + 1))
                for c in range(DC):
                    ins = transpose(h, tt, c, end_t(tt, c))
                    if c % 4 == 3:
                        ins.then_inc(end_t_done, 1)
            pe.wait_ge(wg_lo_ready, DC)
            for u, (tt, d0, width, b) in enumerate(END_PARTS):
                t, d = slice(P * tt, P * (tt + 1)), slice(d0, d0 + width)
                dst = bank[b][:, 0:width]
                if u == 4:
                    pe.wait_ge(sig_ready, 1)
                for c in range(DC):
                    if c % 4 == 0:
                        pe.wait_ge(end_lo_ready, 2 * tt + c // 4 + 1)
                        if c == 0 and b % 2:
                            pe.wait_ge(end_lo_ready, 2 * tt + 2)
                    mm(dst, xt_hi[:, c, t], wg_hi[:, c, d], start=(c == 0), stop=False, skip_group_check=True)
                    mm(dst, xt_hi[:, c, t], wg_lo[:, c, d], start=False, stop=False, skip_group_check=True)
                    ins = mm(dst, xt_lo[:, c, t], wg_hi[:, c, d], start=False, stop=(c == DC - 1),
                             skip_group_check=True)
                ins.then_inc(gate_done, 1)


def bucket_table():
    dist = 255 - np.arange(TAB)
    n = np.maximum(dist, 0)
    exact = REL // 2
    large = exact + (np.log(np.maximum(n, 1) / exact) / np.log(128 / exact) * (REL - exact)).astype(np.int64)
    bucket = np.where(n < exact, n, np.minimum(large, REL - 1))
    bucket = np.where(dist < 0, REL, bucket)
    return (np.arange(REL + 1)[:, None] == bucket[None, :]).astype(np.float32)


def constants():
    i = np.arange(P)
    tri = np.where(i[:, None] >= i[None, :], -1.0 / SCALE, 0.0)
    return np.ascontiguousarray(np.stack(
        [np.eye(P), tri, np.full((P, P), -1.0 / SCALE), np.broadcast_to(i, (P, P)),
         np.eye(P)[::-1]], axis=1).astype(np.float32))


def by_group(w, width=GW):
    k, n = w.shape
    return np.ascontiguousarray(w.reshape(k // P, P, n // width, width).transpose(2, 1, 0, 3))


def kernel(**inputs):
    import concourse.bacc as bacc
    from concourse.bass_utils import run_bass_kernel_spmd

    a = {k: np.asarray(v) for k, v in inputs.items()}
    w_in = by_group(a["w_in"][0])[[0, 1, 3, 4, 2, 5]]
    column = lambda g: g.reshape(DC, P).T
    arrays = {
        "x": a["x"].reshape(SEQ, D),
        "p_t": a["p"].reshape(SEQ, PLE // P, P).transpose(2, 1, 0),
        "rel_bias": a["rel_bias"],
        "bucket_onehot": bucket_table(),
        "consts": constants(),
        "gains": np.stack([column(a["attn_norm"][0]),
                           column(np.concatenate([a["out_norm_moba"][0], a["out_norm_sb"][0]])),
                           column(a["ffn_norm"][0]), column(a["ple_norm"][0])], axis=1),
        "qk_gain": np.stack([np.tile(a["q_norm"][0], 2), np.tile(a["k_norm"][0], 2)], axis=1),
        "w_in": w_in,
        "w_out": by_group(a["w_out"][0]),
        "w_query": by_group(a["peer_query"][0].reshape(D, PG * P)),
        "subkeys_t": a["peer_sub_keys"][0].transpose(2, 0, 1),
        "u_chunks": a["peer_u"][0].reshape(N_KEYS, N_KEYS, DC, P).transpose(1, 3, 2, 0).reshape(N_KEYS, P, D),
        "v_chunks": a["peer_v"][0].reshape(N_KEYS, N_KEYS, D).transpose(1, 0, 2),
        "w_gate": a["w_ple_gate"][0].reshape(DC, P, D).transpose(1, 0, 2),
        "w_ple": a["w_ple"][0].reshape(PLE // P, P, D).transpose(1, 0, 2),
    }
    arrays = {k: np.ascontiguousarray(v) for k, v in arrays.items()}
    nc = bacc.Bacc("TRN2", target_bir_lowering=False, num_devices=1)
    args = [nc.dram_tensor(k, v.shape, mybir.dt.from_np(v.dtype), kind="ExternalInput").ap() for k, v in arrays.items()]
    out = nc.dram_tensor("out", (SEQ, D), mybir.dt.float32, kind="ExternalOutput").ap()
    layer_program(nc, *args, out)
    r = run_bass_kernel_spmd(nc, [arrays], core_ids=[0])
    return r.results[0]["out"].reshape(1, SEQ, D)
```
